# Optimizing a Trainium2 kernel written in Bass

```python
import math
import jax, jax.numpy as jnp
from jax import lax
import numpy as np
import jax
import jax.numpy as jnp

D_MODEL = 1024
BATCH = 1
SEQ = 512
DEPTH = 2

GRID_W = 64
CTX_LEN = 256
N_MOD = 9
D_FF = 2816
MACARON = 0.5
A_HEADS = 8
QK_NOPE = 64
QK_ROPE = 32
V_DIM = 64
Q_RANK = 384
KV_RANK = 256
A_WIDTH = A_HEADS * V_DIM
ATTN_SCALE = 1.0 / math.sqrt(QK_NOPE + QK_ROPE)
ROPE_BASE = 10000.0
Q_BLOCK = 128
CHUNK = 128
B_GROUPS = 4
B_GROUP_CH = 128
B_WIDTH = B_GROUPS * B_GROUP_CH
OFF_KV = Q_RANK
OFF_KR = Q_RANK + KV_RANK
OFF_B = OFF_KR + QK_ROPE
IN_E = OFF_B + 2 * B_WIDTH
CONV_W = 31
LN_EPS = 1e-5
RMS_EPS = 1e-6
ALPHA = (2 * DEPTH) ** 0.25
BETA = (8 * DEPTH) ** -0.25
N_EVEN = (DEPTH + 1) // 2
N_ODD = DEPTH // 2


def layer_norm(x, g, b):
    xf = x.astype(jnp.float32)
    mu = jnp.mean(xf, axis=-1, keepdims=True)
    var = jnp.mean(jnp.square(xf - mu), axis=-1, keepdims=True)
    return ((xf - mu) * lax.rsqrt(var + LN_EPS)).astype(x.dtype) * g + b

def rms_norm(x, g):
    xf = x.astype(jnp.float32)
    return (xf * lax.rsqrt(jnp.mean(xf * xf, axis=-1, keepdims=True) + RMS_EPS)).astype(x.dtype) * g

def adaln(cond, w_mod, b_mod):
    m = jax.nn.silu(cond) @ w_mod + b_mod
    return m.reshape(cond.shape[:-1] + (N_MOD, D_MODEL))

def modulate(h, mod, idx):
    return h * (1 + mod[:, 3 * idx + 1][:, None]) + mod[:, 3 * idx][:, None]

def residual(h, y, mod, idx, g, b, weight):
    return layer_norm(ALPHA * h + weight * mod[:, 3 * idx + 2][:, None] * y, g, b)

def swiglu(h, w13, w2):
    gt, up = jnp.split(h @ w13, 2, axis=-1)
    return (jax.nn.silu(gt) * up) @ w2

def ffn_sublayer(h, mod, idx, w13, w2, g, b):
    return residual(h, swiglu(modulate(h, mod, idx), w13, w2), mod, idx, g, b, MACARON)

def axial_rope(rows, cols):
    half = QK_ROPE // 2
    inv = 1.0 / (ROPE_BASE ** (jnp.arange(0, half, 2, dtype=jnp.float32) / half))
    ang = jnp.concatenate([rows[:, None] * inv, cols[:, None] * inv], axis=-1)
    return jnp.cos(ang), jnp.sin(ang)

def apply_rope(x, cos, sin):
    xp = x.reshape(x.shape[:-1] + (QK_ROPE // 2, 2))
    x0, x1 = xp[..., 0], xp[..., 1]
    extra = (1,) * (x.ndim - 3)
    c = cos.reshape(cos.shape[:1] + extra + cos.shape[1:]).astype(x.dtype)
    s = sin.reshape(sin.shape[:1] + extra + sin.shape[1:]).astype(x.dtype)
    return jnp.stack([x0 * c - x1 * s, x0 * s + x1 * c], axis=-1).reshape(x.shape)

def mla_queries(cq, q_norm_g, w_q_up):
    q = (rms_norm(cq, q_norm_g) @ w_q_up).reshape(cq.shape[:2] + (A_HEADS, QK_NOPE + QK_ROPE))
    return q[..., :QK_NOPE], q[..., QK_NOPE:]

def mla_keys_values(ckv, kv_norm_g, w_kv_up):
    kv = (rms_norm(ckv, kv_norm_g) @ w_kv_up).reshape(ckv.shape[:2] + (A_HEADS, QK_NOPE + V_DIM))
    return kv[..., :QK_NOPE], kv[..., QK_NOPE:]

def mla_attend(q_nope, q_rope, k_nope, k_rope, v):
    s = (jnp.einsum('bqhd,bkhd->bhqk', q_nope, k_nope)
         + jnp.einsum('bqhr,bkr->bhqk', q_rope, k_rope)) * ATTN_SCALE
    p = jax.nn.softmax(s.astype(jnp.float32), axis=-1).astype(v.dtype)
    return jnp.einsum('bhqk,bkhd->bqhd', p, v)

def mla_latent_attention(q_nope, q_rope, k_nope, k_rope, v):
    bn, length = q_nope.shape[:2]
    nb = length // Q_BLOCK

    def to_blocks(t):
        return jnp.moveaxis(t.reshape((bn, nb, Q_BLOCK) + t.shape[2:]), 1, 0)

    out = lax.map(lambda qb: mla_attend(qb[0], qb[1], k_nope, k_rope, v),
                  (to_blocks(q_nope), to_blocks(q_rope)))
    return jnp.moveaxis(out, 0, 1).reshape(bn, length, A_WIDTH)

def spatial_gating(zb, sgu_g, sgu_b, w_s, b_s):
    u, v = jnp.split(jax.nn.gelu(zb, approximate=False), 2, axis=-1)
    v = layer_norm(v, sgu_g, sgu_b)
    bn, length = v.shape[:2]
    vc = v.reshape(bn, length // CHUNK, CHUNK, B_GROUPS, B_GROUP_CH)
    mixed = jnp.einsum('gij,bnjgc->bnigc', w_s, vc) + b_s.T[:, :, None]
    return u * mixed.reshape(bn, length, B_WIDTH)

def even_mixer(h_lat, h_ctx, ctx_out, cos, sin, w_in, q_norm_g, kv_norm_g, w_q_up, w_kv_up,
               sgu_g, sgu_b, w_s, b_s, w_out):
    cq, ckv, kr, zb = jnp.split(h_lat @ w_in, [OFF_KV, OFF_KR, OFF_B], axis=-1)
    if ctx_out:
        cq_c, ckv_c, kr_c, zb_c = jnp.split(h_ctx @ w_in, [OFF_KV, OFF_KR, OFF_B], axis=-1)
    else:
        ckv_c, kr_c = jnp.split(h_ctx @ w_in[:, OFF_KV:OFF_B], [KV_RANK], axis=-1)
    kn_c, v_c = mla_keys_values(ckv_c, kv_norm_g, w_kv_up)
    kn_l, v_l = mla_keys_values(ckv, kv_norm_g, w_kv_up)
    kr_l = apply_rope(kr, cos, sin)
    qn_l, qr_l = mla_queries(cq, q_norm_g, w_q_up)
    qr_l = apply_rope(qr_l, cos, sin)
    k_nope = jnp.concatenate([kn_c, kn_l], axis=1)
    k_rope = jnp.concatenate([kr_c, kr_l], axis=1)
    v_all = jnp.concatenate([v_c, v_l], axis=1)
    a_lat = mla_latent_attention(qn_l, qr_l, k_nope, k_rope, v_all)
    b_lat = spatial_gating(zb, sgu_g, sgu_b, w_s, b_s)
    y_lat = jnp.concatenate([a_lat, b_lat], axis=-1) @ w_out
    if not ctx_out:
        return y_lat, None
    qn_c, qr_c = mla_queries(cq_c, q_norm_g, w_q_up)
    a_ctx = mla_attend(qn_c, qr_c, kn_c, kr_c, v_c).reshape(h_ctx.shape[0], h_ctx.shape[1], A_WIDTH)
    b_ctx = spatial_gating(zb_c, sgu_g, sgu_b, w_s, b_s)
    y_ctx = jnp.concatenate([a_ctx, b_ctx], axis=-1) @ w_out
    return y_lat, y_ctx

def conv_mixer(h, w_pw1, b_pw1, w_dw, b_dw, cg, cb, w_out, b_out):
    a, gt = jnp.split(h @ w_pw1 + b_pw1, 2, axis=-1)
    y = a * jax.nn.sigmoid(gt)
    y = lax.conv_general_dilated(y, w_dw[:, None, :], window_strides=(1,), padding='SAME',
                                 dimension_numbers=('NWC', 'WIO', 'NWC'),
                                 feature_group_count=D_MODEL) + b_dw
    y = jax.nn.silu(layer_norm(y, cg, cb))
    return y @ w_out + b_out

def _ctx_needed(l):
    return any(j % 2 == 0 for j in range(l, DEPTH))

def first_inputs(seed: int = 0) -> dict:
    key = jax.random.key(seed)
    ks = iter(jax.random.split(key, 40))

    def nrm(shape, s):
        return jax.random.normal(next(ks), shape, jnp.float32) * s

    D = D_MODEL
    kv_scale = jnp.concatenate([jnp.ones((QK_NOPE,), jnp.float32), jnp.full((V_DIM,), BETA, jnp.float32)])
    w_kv_up = (nrm((N_EVEN, KV_RANK, A_HEADS, QK_NOPE + V_DIM), KV_RANK ** -0.5) * kv_scale
               ).reshape(N_EVEN, KV_RANK, A_HEADS * (QK_NOPE + V_DIM))
    return {
        "x": nrm((BATCH, SEQ, D), 1.0),
        "c": nrm((BATCH, D), 1.0),
        "ctx": nrm((BATCH, CTX_LEN, D), 1.0),
        "c_ctx": nrm((D,), 1.0),
        "w_mod": nrm((DEPTH, D, N_MOD * D), 0.5 * D ** -0.5),
        "b_mod": nrm((DEPTH, N_MOD * D), 0.02),
        "ln_g": 1.0 + nrm((DEPTH, 3, D), 0.02),
        "ln_b": nrm((DEPTH, 3, D), 0.02),
        "ffn_w13": nrm((DEPTH, 2, D, 2 * D_FF), D ** -0.5),
        "ffn_w2": nrm((DEPTH, 2, D_FF, D), BETA * D_FF ** -0.5),
        "e_w_in": nrm((N_EVEN, D, IN_E), D ** -0.5),
        "e_q_norm": 1.0 + nrm((N_EVEN, Q_RANK), 0.02),
        "e_kv_norm": 1.0 + nrm((N_EVEN, KV_RANK), 0.02),
        "e_w_q_up": nrm((N_EVEN, Q_RANK, A_HEADS * (QK_NOPE + QK_ROPE)), Q_RANK ** -0.5),
        "e_w_kv_up": w_kv_up,
        "e_sgu_g": 1.0 + nrm((N_EVEN, B_WIDTH), 0.02),
        "e_sgu_b": nrm((N_EVEN, B_WIDTH), 0.02),
        "e_w_s": nrm((N_EVEN, B_GROUPS, CHUNK, CHUNK), CHUNK ** -0.5),
        "e_b_s": 1.0 + nrm((N_EVEN, B_GROUPS, CHUNK), 0.02),
        "e_w_out": nrm((N_EVEN, D, D), BETA * D ** -0.5),
        "o_w_pw1": nrm((N_ODD, D, 2 * D), D ** -0.5),
        "o_b_pw1": nrm((N_ODD, 2 * D), 0.02),
        "o_w_dw": nrm((N_ODD, CONV_W, D), CONV_W ** -0.5),
        "o_b_dw": nrm((N_ODD, D), 0.02),
        "o_ln_g": 1.0 + nrm((N_ODD, D), 0.02),
        "o_ln_b": nrm((N_ODD, D), 0.02),
        "o_w_out": nrm((N_ODD, D, D), BETA * D ** -0.5),
        "o_b_out": nrm((N_ODD, D), 0.02),
    }

def first_block(x, c, ctx, c_ctx, w_mod, b_mod, ln_g, ln_b, ffn_w13, ffn_w2,
              e_w_in, e_q_norm, e_kv_norm, e_w_q_up, e_w_kv_up, e_sgu_g, e_sgu_b, e_w_s, e_b_s, e_w_out,
              o_w_pw1, o_b_pw1, o_w_dw, o_b_dw, o_ln_g, o_ln_b, o_w_out, o_b_out):
    length = x.shape[1]
    ROWS = length // GRID_W
    rows = jnp.repeat(jnp.arange(ROWS, dtype=jnp.float32), GRID_W)
    cols = jnp.tile(jnp.arange(GRID_W, dtype=jnp.float32), ROWS)
    cos, sin = axial_rope(rows, cols)

    lat, cx = x, ctx
    for l in range(DEPTH):
        ctx_in = _ctx_needed(l)
        ctx_out = _ctx_needed(l + 1)
        m_lat = adaln(c, w_mod[l], b_mod[l])
        lat = ffn_sublayer(lat, m_lat, 0, ffn_w13[l, 0], ffn_w2[l, 0], ln_g[l, 0], ln_b[l, 0])
        h_lat = modulate(lat, m_lat, 1)
        h_ctx = None
        if ctx_in:
            m_ctx = adaln(c_ctx[None], w_mod[l], b_mod[l])
            cx = ffn_sublayer(cx, m_ctx, 0, ffn_w13[l, 0], ffn_w2[l, 0], ln_g[l, 0], ln_b[l, 0])
            h_ctx = modulate(cx, m_ctx, 1)
        if l % 2 == 0:
            e = l // 2
            y_lat, y_ctx = even_mixer(h_lat, h_ctx, ctx_out, cos, sin, e_w_in[e], e_q_norm[e], e_kv_norm[e],
                                      e_w_q_up[e], e_w_kv_up[e], e_sgu_g[e], e_sgu_b[e], e_w_s[e], e_b_s[e],
                                      e_w_out[e])
        else:
            o = l // 2
            conv_args = (o_w_pw1[o], o_b_pw1[o], o_w_dw[o], o_b_dw[o], o_ln_g[o], o_ln_b[o], o_w_out[o], o_b_out[o])
            y_lat = conv_mixer(h_lat, *conv_args)
            y_ctx = conv_mixer(h_ctx, *conv_args) if ctx_out else None
        lat = residual(lat, y_lat, m_lat, 1, ln_g[l, 1], ln_b[l, 1], 1.0)
        lat = ffn_sublayer(lat, m_lat, 2, ffn_w13[l, 1], ffn_w2[l, 1], ln_g[l, 2], ln_b[l, 2])
        if ctx_out:
            cx = residual(cx, y_ctx, m_ctx, 1, ln_g[l, 1], ln_b[l, 1], 1.0)
            cx = ffn_sublayer(cx, m_ctx, 2, ffn_w13[l, 1], ffn_w2[l, 1], ln_g[l, 2], ln_b[l, 2])
    return lat


_first_inputs = first_inputs


def first_inputs(seed=0):
    import zlib

    import numpy as np

    out = dict(_first_inputs(seed))
    spreads = {}
    factors = {'ctx': 8.0,
     'c_ctx': 8.0,
     'b_mod': 5.76,
     'e_q_norm': 8.0,
     'e_kv_norm': 8.0,
     'e_w_q_up': 8.0,
     'e_w_kv_up': 5.114,
     'e_sgu_g': 8.0,
     'e_sgu_b': 8.0,
     'e_b_s': 8.0,
     'o_b_pw1': 8.0,
     'o_b_dw': 8.0,
     'o_ln_g': 8.0,
     'o_ln_b': 8.0,
     'o_b_out': 8.0}
    for name, (base, spread) in spreads.items():
        noise = np.random.default_rng([zlib.crc32(name.encode()), seed]).standard_normal(out[name].shape)
        drawn = base * np.exp(spread * noise) if base else spread * noise
        out[name] = __import__('jax').numpy.asarray(drawn.astype(out[name].dtype))
    for name, factor in factors.items():
        out[name] = (out[name] * factor).astype(out[name].dtype)
    return out


_narrow_inputs = first_inputs


def first_inputs(seed=0):

    out = dict(_narrow_inputs(seed))
    wider = {'e_sgu_g': 12.0, 'e_sgu_b': 12.0, 'e_b_s': 12.0, 'o_ln_g': 5.88, 'o_ln_b': 5.64}
    for name, times in wider.items():
        mean = out[name].mean()
        out[name] = (mean + times * (out[name] - mean)).astype(out[name].dtype)
    return out


DEPTH_2 = 1

GLA_HEADS = 4
GLA_DK = 128
GLA_DV = 128
GLA_RANK = 16
GLA_TAU = 16.0
GLA_CHUNK = 16
DIL_PATTERNS = ((128, 1), (512, 4), (2048, 16))
DIL_GROUPS = 3
DIL_HEADS = 4
DIL_DH = 128
DIL_BLOCK = 128
N_GROUPS = 4
EXPERTS_PER_GROUP = 8
N_EXPERTS = N_GROUPS * EXPERTS_PER_GROUP
TOP_K = 2
D_EXPERT = 512
MOE_BLOCK = 128
EPS = 1e-6

GLA_QK_W = GLA_HEADS * GLA_DK
GLA_V_W = GLA_HEADS * GLA_DV
DIL_W = DIL_HEADS * DIL_DH
SPLIT_SIZES = (GLA_QK_W, GLA_QK_W, GLA_V_W, GLA_V_W, GLA_RANK) + (DIL_W,) * (3 * DIL_GROUPS)
IN_COLS = sum(SPLIT_SIZES)
SPLIT_POINTS = tuple(int(v) for v in np.cumsum(SPLIT_SIZES)[:-1])
ALIBI_SLOPES = tuple(2.0 ** (-8.0 * (i + 1) / (DIL_GROUPS * DIL_HEADS)) for i in range(DIL_GROUPS * DIL_HEADS))


def rms_norm_2(x, g):
    xf = x.astype(jnp.float32)
    y = xf * lax.rsqrt(jnp.mean(xf * xf, axis=-1, keepdims=True) + EPS)
    return (y * g.astype(jnp.float32)).astype(x.dtype)

def gla_chunked(q, k, v, log_a):
    B, S, H, DK = q.shape
    DV = v.shape[-1]
    C = GLA_CHUNK
    N = S // C
    def chunks(t):
        return t.astype(jnp.float32).reshape(B, N, C, H, t.shape[-1]).transpose(1, 0, 3, 2, 4)
    qc = chunks(q) * (DK ** -0.5)
    kc = chunks(k)
    vc = chunks(v)
    b = jnp.cumsum(chunks(log_a), axis=3)
    b_last = b[:, :, :, -1:, :]
    q_in = qc * jnp.exp(b)
    k_in = kc * jnp.exp(-b)
    k_end = kc * jnp.exp(b_last - b)
    causal = jnp.tril(jnp.ones((C, C), dtype=bool))
    att = jnp.where(causal, jnp.einsum('nbhik,nbhjk->nbhij', q_in, k_in), 0.0)
    o_intra = jnp.einsum('nbhij,nbhjv->nbhiv', att, vc)

    def step(state, xs):
        q_n, k_n, v_n, dec_n = xs
        o_n = jnp.einsum('bhik,bhkv->bhiv', q_n, state)
        state = dec_n[:, :, 0, :, None] * state + jnp.einsum('bhjk,bhjv->bhkv', k_n, v_n)
        return state, o_n

    state0 = jnp.zeros((B, H, DK, DV), jnp.float32)
    _, o_inter = lax.scan(step, state0, (q_in, k_end, vc, jnp.exp(b_last)))
    o = o_intra + o_inter
    return o.transpose(1, 0, 3, 2, 4).reshape(B, S, H, DV)

def dilated_group(q, k, v, slopes, window, dilation):
    B, S, H, E = q.shape
    L = S // dilation
    Q = DIL_BLOCK
    span = window // dilation
    nb = -(-L // Q)
    Lp = nb * Q

    def to_sub(t):
        t = jnp.swapaxes(t.reshape(B, L, dilation, H, E), 1, 2)
        return jnp.pad(t, ((0, 0), (0, 0), (0, Lp - L), (0, 0), (0, 0)))

    def kv_blocks(t):
        t = jnp.pad(to_sub(t), ((0, 0), (0, 0), (Q, 0), (0, 0), (0, 0))).reshape(B, dilation, nb + 1, Q, H, E)
        return jnp.concatenate([t[:, :, :-1], t[:, :, 1:]], axis=3)

    def from_sub(t):
        t = t.reshape((B, dilation, Lp) + t.shape[4:])[:, :, :L]
        t = jnp.swapaxes(t, 1, 2)
        return t.reshape((B, S) + t.shape[3:])

    qb = to_sub(q).reshape(B, dilation, nb, Q, H, E)
    kb = kv_blocks(k)
    vb = kv_blocks(v)
    s = jnp.einsum('bdnqhe,bdnkhe->bdnhqk', qb, kb, preferred_element_type=jnp.float32) * (E ** -0.5)
    dist = jnp.arange(Q)[:, None] + Q - jnp.arange(2 * Q)[None, :]
    key_pos = jnp.arange(nb)[:, None, None] * Q + jnp.arange(2 * Q)[None, None, :] - Q
    valid = (dist >= 0) & (dist <= span) & (key_pos >= 0)
    bias = -slopes[:, None, None] * (dilation * dist).astype(jnp.float32)
    s = jnp.where(valid[:, None], s + bias, -jnp.inf)
    m = jnp.max(s, axis=-1)
    p = jnp.exp(s - m[..., None])
    den = jnp.sum(p, axis=-1)
    den_t = jnp.swapaxes(den, -1, -2)
    o = jnp.einsum('bdnhqk,bdnkhe->bdnqhe', p, vb.astype(jnp.float32)) / den_t[..., None]
    return from_sub(o), from_sub(jnp.swapaxes(m, -1, -2)), from_sub(den_t)

def hier_moe(h, w_rg, b_rg, w_re, b_re, w_gate, w_up, w_down):
    B, S, D = h.shape
    T = B * S
    hf = h.reshape(T, D)
    g_logit = (hf @ w_rg).astype(jnp.float32) + b_rg
    g_prob = jax.nn.softmax(g_logit, axis=-1)
    g_sel = jnp.argmax(g_logit, axis=-1)
    g_p = jnp.take_along_axis(g_prob, g_sel[:, None], axis=-1)[:, 0]
    e_logit = ((hf @ w_re).astype(jnp.float32) + b_re).reshape(T, N_GROUPS, EXPERTS_PER_GROUP)
    e_logit = jnp.take_along_axis(e_logit, g_sel[:, None, None], axis=1)[:, 0]
    top_v, top_i = lax.top_k(e_logit, TOP_K)
    gate = jax.nn.softmax(top_v, axis=-1) * g_p[:, None]
    eid = g_sel[:, None] * EXPERTS_PER_GROUP + top_i

    A = T * TOP_K
    flat_e = eid.reshape(A).astype(jnp.int32)
    flat_w = gate.reshape(A)
    flat_t = jnp.repeat(jnp.arange(T, dtype=jnp.int32), TOP_K)
    order = jnp.argsort(flat_e)
    se, st, sw = flat_e[order], flat_t[order], flat_w[order]
    counts = jnp.bincount(flat_e, length=N_EXPERTS)
    starts = jnp.cumsum(counts) - counts
    pcounts = (counts + MOE_BLOCK - 1) // MOE_BLOCK * MOE_BLOCK
    pends = jnp.cumsum(pcounts)
    pstarts = pends - pcounts
    dest = pstarts[se] + jnp.arange(A, dtype=jnp.int32) - starts[se]
    P = A + N_EXPERTS * MOE_BLOCK
    NB = P // MOE_BLOCK
    row_t = jnp.full((P,), T, jnp.int32).at[dest].set(st)
    row_w = jnp.zeros((P,), jnp.float32).at[dest].set(sw)
    blk_e = jnp.minimum(jnp.searchsorted(pends, jnp.arange(NB, dtype=jnp.int32) * MOE_BLOCK, side='right'), N_EXPERTS - 1)
    h_pad = jnp.concatenate([hf, jnp.zeros((1, D), hf.dtype)], axis=0)
    xin = h_pad[row_t].reshape(NB, MOE_BLOCK, D)

    def expert_block(args):
        xb, e = args
        return (jax.nn.silu(xb @ w_gate[e]) * (xb @ w_up[e])) @ w_down[e]

    yb = lax.map(expert_block, (xin, blk_e)).reshape(P, D)
    out = jnp.zeros((T + 1, D), jnp.float32).at[row_t].add(yb.astype(jnp.float32) * row_w[:, None])[:T]
    return out.reshape(B, S, D).astype(h.dtype)

def second_inputs(seed: int = 0) -> dict:
    key = jax.random.key(seed)
    ks = jax.random.split(key, 22)
    def nrm(k, shape, scale):
        return scale * jax.random.normal(k, shape, jnp.float32)
    L = DEPTH_2
    return {
        'x': nrm(ks[0], (BATCH, SEQ, D_MODEL), 1.0),
        'norm1_g': 1.0 + nrm(ks[1], (L, D_MODEL), 0.02),
        'w_in': nrm(ks[2], (L, D_MODEL, IN_COLS), D_MODEL ** -0.5),
        'w_gla_a2': nrm(ks[3], (L, GLA_RANK, GLA_QK_W), GLA_RANK ** -0.5),
        'b_gla_a': nrm(ks[4], (L, GLA_QK_W), 0.1),
        'gla_out_norm_g': 1.0 + nrm(ks[5], (L, GLA_DV), 0.02),
        'dil_q_norm_g': 1.0 + nrm(ks[6], (L, DIL_GROUPS, DIL_DH), 0.02),
        'dil_k_norm_g': 1.0 + nrm(ks[7], (L, DIL_GROUPS, DIL_DH), 0.02),
        'w_proj_gla': nrm(ks[8], (L, GLA_V_W, D_MODEL), GLA_V_W ** -0.5),
        'w_proj_attn': nrm(ks[9], (L, DIL_W, D_MODEL), DIL_W ** -0.5),
        'w_branch_gate': nrm(ks[10], (L, D_MODEL, 2 * D_MODEL), D_MODEL ** -0.5),
        'b_branch_gate': nrm(ks[11], (L, 2 * D_MODEL), 0.01),
        'w_out': nrm(ks[12], (L, D_MODEL, D_MODEL), D_MODEL ** -0.5),
        'norm2_g': 1.0 + nrm(ks[13], (L, D_MODEL), 0.02),
        'w_router_group': nrm(ks[14], (L, D_MODEL, N_GROUPS), D_MODEL ** -0.5),
        'b_router_group': nrm(ks[15], (L, N_GROUPS), 0.01),
        'w_router_expert': nrm(ks[16], (L, D_MODEL, N_EXPERTS), D_MODEL ** -0.5),
        'b_router_expert': nrm(ks[17], (L, N_EXPERTS), 0.01),
        'w_gate': nrm(ks[18], (L, N_EXPERTS, D_MODEL, D_EXPERT), D_MODEL ** -0.5),
        'w_up': nrm(ks[19], (L, N_EXPERTS, D_MODEL, D_EXPERT), D_MODEL ** -0.5),
        'w_down': nrm(ks[20], (L, N_EXPERTS, D_EXPERT, D_MODEL), D_EXPERT ** -0.5),
    }

def second_block(x, norm1_g, w_in, w_gla_a2, b_gla_a, gla_out_norm_g, dil_q_norm_g, dil_k_norm_g,
              w_proj_gla, w_proj_attn, w_branch_gate, b_branch_gate, w_out, norm2_g,
              w_router_group, b_router_group, w_router_expert, b_router_expert, w_gate, w_up, w_down):
    B, S, D = x.shape
    slopes = jnp.asarray(ALIBI_SLOPES, jnp.float32).reshape(DIL_GROUPS, DIL_HEADS)
    def heads(t, e):
        return t.reshape(B, S, -1, e)
    for l in range(DEPTH_2):
        h = rms_norm_2(x, norm1_g[l])
        parts = jnp.split(h @ w_in[l], list(SPLIT_POINTS), axis=-1)
        gq, gk, gv, gr, ga_lr = parts[:5]
        log_a = jax.nn.log_sigmoid((ga_lr @ w_gla_a2[l] + b_gla_a[l]).astype(jnp.float32)) / GLA_TAU
        o_gla = gla_chunked(heads(gq, GLA_DK), heads(gk, GLA_DK), heads(gv, GLA_DV), heads(log_a, GLA_DK))
        o_gla = rms_norm_2(o_gla, gla_out_norm_g[l]).reshape(B, S, GLA_V_W) * jax.nn.silu(gr.astype(jnp.float32))
        y_gla = o_gla.astype(x.dtype) @ w_proj_gla[l]
        outs, maxes, dens = [], [], []
        for gi, (window, dilation) in enumerate(DIL_PATTERNS):
            q, k, v = parts[5 + 3 * gi: 8 + 3 * gi]
            q = rms_norm_2(heads(q, DIL_DH), dil_q_norm_g[l, gi])
            k = rms_norm_2(heads(k, DIL_DH), dil_k_norm_g[l, gi])
            o_g, m_g, d_g = dilated_group(q, k, heads(v, DIL_DH), slopes[gi], window, dilation)
            outs.append(o_g)
            maxes.append(m_g)
            dens.append(d_g)
        m_all = jnp.stack(maxes)
        wts = jnp.stack(dens) * jnp.exp(m_all - jnp.max(m_all, axis=0))
        o_att = jnp.sum(wts[..., None] * jnp.stack(outs), axis=0) / jnp.sum(wts, axis=0)[..., None]
        y_att = o_att.reshape(B, S, DIL_W).astype(x.dtype) @ w_proj_attn[l]
        g_gla, g_att = jnp.split(jax.nn.sigmoid(h @ w_branch_gate[l] + b_branch_gate[l]), 2, axis=-1)
        x = x + ((g_gla * y_gla + g_att * y_att) @ w_out[l]).astype(x.dtype)
        x = x + hier_moe(rms_norm_2(x, norm2_g[l]), w_router_group[l], b_router_group[l], w_router_expert[l],
                         b_router_expert[l], w_gate[l], w_up[l], w_down[l])
    return x


def setup_inputs(seed=0):
    out = dict(first_inputs(seed))
    for name, value in second_inputs(seed + 1).items():
        if name != "x":
            out[name + "_2"] = value
    return out


def reference(
    x, c, ctx, c_ctx, w_mod, b_mod, ln_g, ln_b, ffn_w13, ffn_w2, e_w_in, e_q_norm, e_kv_norm,
    e_w_q_up, e_w_kv_up, e_sgu_g, e_sgu_b, e_w_s, e_b_s, e_w_out, o_w_pw1, o_b_pw1, o_w_dw,
    o_b_dw, o_ln_g, o_ln_b, o_w_out, o_b_out, norm1_g_2, w_in_2, w_gla_a2_2, b_gla_a_2,
    gla_out_norm_g_2, dil_q_norm_g_2, dil_k_norm_g_2, w_proj_gla_2, w_proj_attn_2,
    w_branch_gate_2, b_branch_gate_2, w_out_2, norm2_g_2, w_router_group_2, b_router_group_2,
    w_router_expert_2, b_router_expert_2, w_gate_2, w_up_2, w_down_2,
):
    x = first_block(
        x, c, ctx, c_ctx, w_mod, b_mod, ln_g, ln_b, ffn_w13, ffn_w2, e_w_in, e_q_norm,
        e_kv_norm, e_w_q_up, e_w_kv_up, e_sgu_g, e_sgu_b, e_w_s, e_b_s, e_w_out, o_w_pw1,
        o_b_pw1, o_w_dw, o_b_dw, o_ln_g, o_ln_b, o_w_out, o_b_out,
    )
    return second_block(
        x, norm1_g_2, w_in_2, w_gla_a2_2, b_gla_a_2, gla_out_norm_g_2, dil_q_norm_g_2,
        dil_k_norm_g_2, w_proj_gla_2, w_proj_attn_2, w_branch_gate_2, b_branch_gate_2, w_out_2,
        norm2_g_2, w_router_group_2, b_router_group_2, w_router_expert_2, b_router_expert_2,
        w_gate_2, w_up_2, w_down_2,
    )


_drawn_inputs = setup_inputs


def setup_inputs(seed=0):
    import zlib

    import numpy as np

    out = dict(_drawn_inputs(seed))
    spreads = {}
    factors = {'gla_out_norm_g_2': 3.579,
     'dil_q_norm_g_2': 8.0,
     'dil_k_norm_g_2': 8.0,
     'b_branch_gate_2': 8.0,
     'b_router_group_2': 6.793,
     'b_router_expert_2': 6.36,
     'norm2_g_2': 2.827}
    for name, (base, spread) in spreads.items():
        noise = np.random.default_rng([zlib.crc32(name.encode()), seed]).standard_normal(out[name].shape)
        drawn = base * np.exp(spread * noise) if base else spread * noise
        out[name] = jnp.asarray(drawn.astype(out[name].dtype))
    for name, factor in factors.items():
        out[name] = (out[name] * factor).astype(out[name].dtype)
    return out
```

```python
import math
from contextlib import ExitStack

import concourse.bass as bass
from concourse import mybir

P = 128
ACT = mybir.ActivationFunctionType
ALU = mybir.AluOpType
AXX = mybir.AxisListType.X
F32 = mybir.dt.float32
F32R = mybir.dt.float32r
U32 = mybir.dt.uint32
I32 = mybir.dt.int32

D = 1024
KD = D // P
S = 512
C = 256
T0 = S + C
ST = S // P
FF = 2816
KF = FF // P
FG = 8
FGS, FREST = KF // FG, KF % FG
ALPHA = 4.0 ** 0.25
LN_EPS = 1e-5
RMS_EPS = 1e-6
HEADS = 8
NOPE, ROPE, VD = 64, 32, 64
QK = NOPE + ROPE
Q_RANK, KV_RANK = 384, 256
ATTN_SCALE = 1.0 / math.sqrt(QK)
BW = 512
TAPS = 31
PAD = TAPS // 2
GH = 4
GC = 16
NCH = S // GC
GLA_TAU = 16.0
GROUPS = 3
EXPERTS = 32
EG = 8
NG = 4
DE = 512
TABLE = S * EXPERTS

SLOTS = 4
SLOT = 2048

VECTORS = [("c", 8), ("c_ctx", 8), ("b_mod", 144), ("ln_g", 48), ("ln_b", 48), ("e_q_norm", 3), ("e_kv_norm", 2),
           ("o_b_pw1", 16), ("o_w_dw", 8 * TAPS), ("o_b_dw", 8), ("o_ln_g", 8), ("o_ln_b", 8), ("o_b_out", 8),
           ("norm1_g_2", 8), ("b_gla_a_2", 4), ("gla_out_norm_g_2", 1), ("dil_q_norm_g_2", 3),
           ("dil_k_norm_g_2", 3), ("b_branch_gate_2", 16), ("norm2_g_2", 8)]
COLUMN = {}
_at = 0
for _name, _rows in VECTORS:
    COLUMN[_name] = _at
    _at += _rows
NCOL = _at
COL_TILES = -(-NCOL // P)


class Core:

    def sem(self, name):
        s = self.nc.alloc_semaphore(name)
        self.stage_sems.append(s)
        return s

    def renew_semaphores(self):
        self.nc.clear_and_free_semaphores(self.stage_sems)
        self.nc.all_engine_barrier()
        self.stage_sems = []


class WeightRing:

    def __init__(self, ring, landed):
        self.ring, self.landed = ring, landed
        self.sections, self.total, self.issued, self.taken, self.entered = [], 0, 0, 0, 0
        self.used = {}

    def plan(self, bodies, tail, source, per=SLOTS):
        self.sections.append((self.total, per, bodies, tail, source))
        self.total += per * bodies + tail

    def _load(self, sp, n, i, r):
        base, per, _, _, source = self.sections[n]
        slot = (base + r) % SLOTS
        if not isinstance(i, int):
            sem, value = self.used[n](i, r - SLOTS) if r >= SLOTS else self.used[n](i - 1, r - SLOTS + per)
            sp.wait_ge(sem, value)
        elif base + per * i + r >= SLOTS:
            before = base + per * i + r - SLOTS
            m = max(j for j, sec in enumerate(self.sections) if sec[0] <= before)
            at = before - self.sections[m][0]
            sem, value = self.used[m](at // self.sections[m][1], at % self.sections[m][1])
            sp.wait_ge(sem, value)
        view, src = source(self.ring[:, slot, :], i, r)
        sp.dma_start(view, src).then_inc(self.landed[slot], 16)

    def issue(self, sp, upto):
        upto = min(upto, self.total)
        for n, (base, per, bodies, tail, _) in enumerate(self.sections):
            size = per * bodies + tail
            at = self.issued - base
            end = min(upto - base, size)
            if at < 0 or end <= at:
                continue
            while at < end and (at % per or at >= per * bodies or at < per):
                self._load(sp, n, at // per, at % per)
                at += 1
            b0, b1 = at // per, min(end // per, bodies)
            if b1 - b0 >= 2:
                with sp.Fori(b0, b1) as i:
                    for r in range(per):
                        self._load(sp, n, i, r)
                at = per * b1
            while at < end:
                self._load(sp, n, at // per, at % per)
                at += 1
            self.issued = base + at

    def ahead(self, sp, *used):
        for fn in used:
            self.used[self.entered] = fn
            self.entered += 1
        base, per, bodies, tail, _ = self.sections[self.entered - 1]
        self.issue(sp, base + per * bodies + tail + SLOTS)

    def take(self, eng):
        g = self.taken
        self.taken += 1
        eng.wait_ge(self.landed[g % SLOTS], 16 * (g // SLOTS + 1))
        return self.ring[:, g % SLOTS, :]

    def take_in_loop(self, eng, i, r, per=SLOTS):
        g = self.taken + r
        eng.wait_ge(self.landed[g % SLOTS], (16 * per // SLOTS) * i + 16 * (g // SLOTS + 1))
        return self.ring[:, g % SLOTS, :]

    def slot(self, r):
        return self.ring[:, (self.taken + r) % SLOTS, :]

    def skip(self, n):
        self.taken += n


def wide(view, n=256, k=KD):
    return view[:, 0:k * n].rearrange("p (k n) -> p k n", k=k)


def rows_of(w, k=KD):
    return w.rearrange("(k p) n -> p k n", p=P)


def span(at, n):
    return slice(at, at + n) if isinstance(at, int) else bass.ds(at, n)


def sweep(w, cols=256):
    def source(view, i, r):
        n = w.shape[1]
        if isinstance(i, int):
            at = (SLOTS * i + r) * cols
            width = min(cols, n - at)
            return wide(view, width, w.shape[0] // P), rows_of(w)[:, :, at:at + width]
        return wide(view, cols, w.shape[0] // P), rows_of(w)[:, :, bass.ds(i * (SLOTS * cols) + r * cols, cols)]
    return source


def half_rows(w, at):
    def source(view, i, r):
        return wide(view, 512, 4), w.rearrange("(k p) n -> p k n", p=P)[:, 4 * r:4 * r + 4, at:at + 512]
    return source


def plan_weights(k):
    a, w = k.a, k.weights
    def adaln_plan(l):
        w.plan(9, 0, sweep(a["w_mod"][l]))

    def ffn_plan(l, s):
        w13, w2 = a["ffn_w13"][l, s], a["ffn_w2"][l, s]

        def group(first, last):
            def source(view, i, r):
                f = first + i * FG
                if r < last:
                    return wide(view), rows_of(w13)[:, :, span(f * P + ((r // 2) * 256 + (r % 2) * FF), 256)]
                q = r - last
                return wide(view, 256, last), rows_of(w2)[:, span(f, last), q * 256:q * 256 + 256]
            return source

        w.plan(FGS, 0, group(0, FG), per=FG + 4)
        w.plan(0, FREST + 4, group(FGS * FG, FREST), per=FG + 4)

    adaln_plan(0)
    ffn_plan(0, 0)
    w_in = a["e_w_in"][0]
    w.plan(0, 3, sweep(w_in[:, 0:672]))
    w.plan(0, 2, sweep(w_in[:, 672:1184]))
    w.plan(0, 2, half_rows(w_in, 1184))

    def q_up(view, i, r):
        return wide(view, 384, 3), a["e_w_q_up"][0].rearrange("(k p) n -> p k n", p=P)[:, :, 384 * r:384 * r + 384]

    def kv_up(view, i, r):
        return wide(view, 1024, 2), a["e_w_kv_up"][0].rearrange("(k p) n -> p k n", p=P)
    w.plan(0, 2, q_up)
    w.plan(0, 1, kv_up)
    w.plan(0, 4, sweep(a["e_w_out"][0]))
    ffn_plan(0, 1)
    adaln_plan(1)
    ffn_plan(1, 0)
    pw1 = a["o_w_pw1"][0]

    def pw(view, i, r):
        at = (1 - r % 2) * D + (r // 2) * 256 + i * 512
        return wide(view), rows_of(pw1)[:, :, at:at + 256]
    w.plan(2, 0, pw)
    w.plan(0, 4, sweep(a["o_w_out"][0]))
    ffn_plan(1, 1)
    w2_in = a["w_in_2"][0]
    w.plan(0, 4, sweep(w2_in[:, 0:1024]))
    w.plan(0, 2, half_rows(w2_in, 1024))
    w.plan(0, 3, sweep(w2_in[:, 1536:2064]))
    for g in range(GROUPS):
        w.plan(0, 4, sweep(w2_in[:, 2064 + 1536 * g:2064 + 1536 * g + 1024]))
        w.plan(0, 2, half_rows(w2_in, 2064 + 1536 * g + 1024))

    def merge(view, i, r):
        if r < 2:
            return wide(view), rows_of(a["w_branch_gate_2"][0])[:, :, span(i * 256 + D * r, 256)]
        src = a["w_proj_gla_2"][0] if r == 2 else a["w_proj_attn_2"][0]
        return wide(view, 256, 4), rows_of(src)[:, :, span(i * 256, 256)]
    w.plan(4, 0, merge)
    w.plan(0, 4, sweep(a["w_out_2"][0]))


def load_stage(k):
    nc, a = k.nc, k.a
    with ExitStack() as st:
        rows = st.enter_context(nc.sbuf_tensor("token_rows", [P, T0 // P, D], F32))
        vec = st.enter_context(nc.sbuf_tensor("vector_rows", [P, COL_TILES, P], F32))
        sem = lambda n: k.sem(n)
        s_tok, s_vec, s_con, s_tp, s_cp = sem("ld_tokens"), sem("ld_vectors"), sem("ld_consts"), sem("ld_transposed"), sem("ld_copied")
        s_ms, s_z = sem("ld_memset"), sem("ld_zeroed")
        tiles = [(t, 0) for t in range(T0 // P)]
        block = st.enter_context(nc.Block())

        @block.sync
        def _(sp):
            sp.dma_start(k.ident[:], k.a["k_ident"]).then_inc(s_con, 16)
            sp.dma_start(rows[:, 0:ST, :], a["x"][0].rearrange("(t p) d -> p t d", p=P)).then_inc(s_tok, 16)
            sp.dma_start(rows[:, ST:, :], a["ctx"][0].rearrange("(t p) d -> p t d", p=P)).then_inc(s_tok, 16)
            k.weights.issue(sp, SLOTS)

        @block.scalar
        def _(act):
            act.wait_ge(s_z, 1)
            n = 0
            for name, count in VECTORS:
                src = k.flat[name]
                done = 0
                while done < count:
                    row = COLUMN[name] + done
                    m = min(P - row % P, count - done)
                    act.dma_start(vec[row % P:row % P + m, row // P, :], src[done:done + m, :]).then_inc(s_vec, 16)
                    done += m
                    n += 1
            k.n_vec = n
            for j in range(T0 // P * 2):
                act.wait_ge(s_tp, j + 1)
                t, h = divmod(j, 2)
                ins = act.activation(k.X[:, 4 * h:4 * h + 4, t * P:(t + 1) * P],
                                     k.PS[j % 4][:, 0:512].rearrange("p (a b) -> p a b", a=4), ACT.Copy)
                ins.then_inc(s_cp, 1)

        @block.gpsimd
        def _(pool):
            pool.memset(vec[:, COL_TILES - 1, :], 0.0).then_inc(s_z, 1)
            pool.memset(k.ones[:], 1.0).then_inc(s_ms, 1)

        @block.tensor
        def _(pe):
            pe.wait_ge(s_con, 16)
            pe.wait_ge(s_tok, 32)
            for j in range(T0 // P * 2):
                if j >= 4:
                    pe.wait_ge(s_cp, j - 3)
                t, h = divmod(j, 2)
                for c in range(4):
                    ins = pe.transpose(k.PS[j % 4][:, c * P:(c + 1) * P], rows[:, t, (4 * h + c) * P:(4 * h + c + 1) * P], k.ident[:])
                ins.then_inc(s_tp, 1)
            pe.wait_ge(s_vec, 16 * k.n_vec)
            pe.wait_ge(s_cp, 2 * (T0 // P))
            for c in range(COL_TILES):
                ins = pe.transpose(k.PS[c // 4][:, (c % 4) * P:(c % 4 + 1) * P], vec[:, c, :], k.ident[:])
            ins.then_inc(s_tp, 1)

        @block.vector
        def _(dve):
            dve.wait_ge(s_tp, 2 * (T0 // P) + 1)
            dve.tensor_copy(k.col[:, 0:512], k.PS[0][:, 0:512]).then_inc(s_ms, 1)
            dve.tensor_copy(k.col[:, 512:COL_TILES * P], k.PS[1][:, 0:COL_TILES * P - 512]).then_inc(s_ms, 1)
            dve.wait_ge(s_ms, 3)


def chained(eng, s, n, ins):
    ins.then_inc(s, 1)
    n[0] += 1
    eng.wait_ge(s, n[0])


def adaln_stage(k, l):
    nc = k.nc
    mod = k.mod[l]
    with ExitStack() as st:
        sem = lambda n: k.sem(f"ada{l}_{n}")
        s_c, s_done, s_row, s_cols, s_ch = sem("silu"), sem("products"), sem("rows"), sem("columns"), sem("chain")
        rows = st.enter_context(nc.sbuf_tensor(f"ada{l}_rows", [2, SLOTS, 256], F32))
        block = st.enter_context(nc.Block())
        cols = k.PS[2][:, 0:144].rearrange("p (m w) -> p m w", w=2)
        bank = lambda r: k.PS[r // 2][0:2, 512 * (r % 2):512 * (r % 2) + 256]

        @block.sync
        def _(sp):
            k.weights.ahead(sp, lambda i, r: (s_done, i * SLOTS + (r + 1)))

        @block.scalar
        def _(act):
            act.activation(k.cond[:], k.col[:, 0:16].rearrange("p (w k) -> p w k", w=2), ACT.Silu).then_inc(s_c, 1)
            act.sem_inc(s_cols, SLOTS)
            with act.Fori(0, 9) as i:
                for r in range(SLOTS):
                    act.wait_ge(s_done, i * SLOTS + (r + 1))
                    act.wait_ge(s_cols, i * SLOTS + (r + 1))
                    act.activation(rows[:, r, :], bank(r), ACT.Copy).then_inc(s_row, 1)

        @block.tensor
        def _(pe):
            def turn(i, r):
                pe.wait_ge(s_row, i * SLOTS + (r + 1))
                for m in range(2):
                    ins = pe.matmul(cols[:, bass.ds(i * 8 + (2 * r + m), 1), :], rows[:, r, m * P:(m + 1) * P],
                                    k.ident[0:2, 0:2], start=True, stop=True)
                ins.then_inc(s_cols, 1)
            pe.wait_ge(s_c, 1)
            with pe.Fori(0, 9) as i:
                for r in range(SLOTS):
                    w = wide(k.weights.take_in_loop(pe, i, r))
                    for kk in range(KD):
                        ins = pe.matmul(bank(r), k.cond[:, :, kk], w[:, kk, :], start=kk == 0, stop=kk == KD - 1)
                    ins.then_inc(s_done, 1)
                    if r:
                        turn(i, r - 1)
                turn(i, SLOTS - 1)
            k.weights.skip(36)

        @block.vector
        def _(dve):
            n = [0]
            dve.wait_ge(s_cols, 36 + SLOTS)
            b = k.col[:, COLUMN["b_mod"] + 72 * l:COLUMN["b_mod"] + 72 * l + 72]
            for w in range(2):
                chained(dve, s_ch, n, dve.tensor_tensor(mod[:, w, :], cols[:, :, w], b, ALU.add))
            for idx in (1, 4, 7):
                chained(dve, s_ch, n, dve.tensor_scalar(mod[:, :, 8 * idx:8 * idx + 8], mod[:, :, 8 * idx:8 * idx + 8], 1.0, None, ALU.add))
            for idx in (2, 8):
                chained(dve, s_ch, n, dve.tensor_scalar(mod[:, :, 8 * idx:8 * idx + 8], mod[:, :, 8 * idx:8 * idx + 8], 0.5, None, ALU.mult))


def modulate_steps(eng, out, x, mod, idx, segments, wait, done):
    for kk in range(KD):
        wait(kk)
        for which, at, n in segments:
            j = 24 * idx + kk
            ins = eng.tensor_scalar(out[:, kk, at:at + n], x[:, kk, at:at + n], mod[:, which, j + 8:j + 9],
                                    mod[:, which, j:j + 1], ALU.mult, ALU.add)
        if done is not None:
            ins.then_inc(done, 1)


def split_product(pe, bank, w_hi, w_lo, x_hi, x_lo, halves, start, stop):
    passes = ((w_hi, x_hi), (w_hi, x_lo), (w_lo, x_hi))
    for n, (w, x) in enumerate(passes):
        for at, width in halves:
            ins = pe.matmul(bank[:, at:at + width], w, x[:, at:at + width],
                            start=start and n == 0, stop=stop and n == len(passes) - 1)
    return ins


def ffn_stage(k, name, l, s, idx, segments):
    nc, W = k.nc, k.weights
    T = sum(n for _, _, n in segments)
    halves = [(0, 512)] + ([(512, T - 512)] if T > 512 else [])
    mod = k.mod[l]
    CH = FG + 4
    assert CH % SLOTS == 0 and FREST >= 4
    with ExitStack() as st:
        sb = lambda n, shape, dt: st.enter_context(nc.sbuf_tensor(f"{name}_{n}", shape, dt))
        h_hi, h_lo = sb("h_hi", [P, KD, T], F32R), sb("h_lo", [P, KD, T], F32R)
        f_hi, f_lo = sb("hidden_hi", [P, FG, T], F32R), sb("hidden_lo", [P, FG, T], F32R)
        w_hi, w_lo = sb("weights_hi", [P, 2, SLOT], F32R), sb("weights_lo", [P, 2, SLOT], F32R)
        tmp = sb("swiglu", [P, 2, T], F32)
        sem = lambda n: k.sem(f"{name}_{n}")
        s_hi, s_lo, s_mod, s_xhi, s_xlo, s_tile, s_silu, s_mul, s_fhi, s_flo, s_scaled, s_add = (
            sem("weights_hi"), sem("weights_lo"), sem("modulated"), sem("h_hi"), sem("h_lo"), sem("tiles"), sem("silu"), sem("product"),
            sem("hidden_hi"), sem("hidden_lo"), sem("scaled"), sem("added"))
        block = st.enter_context(nc.Block())
        G, U, Y = k.PS[0:2], k.PS[2:4], k.PS[0:2]
        CREDIT = 2

        @block.sync
        def _(sp):
            W.ahead(sp, lambda i, r: (s_lo, i * CH + (r + 1)), lambda i, r: (s_lo, FGS * CH + r + 1))

        @block.gpsimd
        def _(pool):
            pool.wait_ge(s_mod, KD)
            for kk in range(KD):
                ins = pool.tensor_scalar(k.X[:, kk, 0:T], k.X[:, kk, 0:T], ALPHA, 0.0, ALU.mult, ALU.add)
            ins.then_inc(s_scaled, 1)

        @block.tensor
        def _(pe):
            def group(i, n):
                for c in range(n + 4):
                    pe.wait_ge(s_lo, i * CH + (c + 1))
                    rows = KD if c < n else n
                    hi, lo = wide(w_hi[:, c % 2, :], 256, rows), wide(w_lo[:, c % 2, :], 256, rows)
                    for b in range(2):
                        f = 2 * (c // 2) + b
                        m = 2 * (c - n) + b
                        if c >= n:
                            bank = Y[b]
                            if m < 2:
                                pe.wait_ge(s_silu, i * FG + (n - 1 + b))
                            else:
                                pe.wait_ge(s_add, i * KD + (m - 1 + CREDIT))
                        elif c % 2 == 0:
                            bank = G[b]
                            if f < 2:
                                pe.wait_ge(s_add, i * KD + (f - 1 + CREDIT))
                            else:
                                pe.wait_ge(s_silu, i * FG + (f - 1))
                        else:
                            bank = U[b]
                            if f >= 2:
                                pe.wait_ge(s_mul, i * FG + (f - 1))
                        for kk in range(rows):
                            if c == 0 and b == 0:
                                pe.wait_ge(s_xlo, kk + 1)
                            if c == n and b == 0:
                                pe.wait_ge(s_flo, i * FG + (kk + 1))
                            x_hi, x_lo = (h_hi, h_lo) if c < n else (f_hi, f_lo)
                            ins = split_product(pe, bank, hi[:, kk, b * P:(b + 1) * P], lo[:, kk, b * P:(b + 1) * P],
                                                x_hi[:, kk, :], x_lo[:, kk, :], halves, kk == 0, kk == rows - 1)
                        ins.then_inc(s_tile, 1)
            with pe.Fori(0, FGS) as i:
                group(i, FG)
            group(FGS, FREST)

        @block.scalar
        def _(act):
            def chunk_hi(i, c, n):
                at = (i * CH if isinstance(i, int) else 0) + c
                rows = KD if c < n or c >= CH else n
                raw = W.take_in_loop(act, 0 if isinstance(i, int) else i, at, CH)
                act.activation(w_hi[:, c % 2, 0:rows * 256], raw[:, 0:rows * 256], ACT.Copy).then_inc(s_hi, 1)

            def group(i, n, last=False):
                for c in range(n + 4):
                    if c < n:
                        for b in range(2):
                            f = 2 * (c // 2) + b
                            if c % 2 == 0:
                                act.wait_ge(s_tile, i * (2 * CH) + (2 * c + b + 1))
                                if f >= 2:
                                    act.wait_ge(s_flo, i * FG + (f - 1))
                                act.activation(tmp[:, b, :], G[b][:, 0:T], ACT.Silu).then_inc(s_silu, 1)
                            else:
                                act.wait_ge(s_mul, i * FG + (f + 1))
                                act.activation(f_hi[:, f, :], tmp[:, b, :], ACT.Copy).then_inc(s_fhi, 1)
                    if not last or c + 2 < n + 4:
                        act.wait_ge(s_tile, i * (2 * CH) + (2 * c + 2))
                        chunk_hi(i, c + 2, n)
            chunk_hi(0, 0, FG)
            for kk in range(KD):
                act.wait_ge(s_mod, kk + 1)
                act.activation(h_hi[:, kk, :], tmp[:, kk % 2, :], ACT.Copy).then_inc(s_xhi, 1)
            chunk_hi(0, 1, FG)
            with act.Fori(0, FGS) as i:
                group(i, FG)
            group(FGS, FREST, last=True)

        @block.vector
        def _(dve):
            def chunk_lo(i, c, n):
                rows = KD if c < n or c >= CH else n
                dve.wait_ge(s_hi, i * CH + (c + 1))
                dve.tensor_tensor(w_lo[:, c % 2, 0:rows * 256], W.slot((i * CH if isinstance(i, int) else 0) + c)[:, 0:rows * 256],
                                  w_hi[:, c % 2, 0:rows * 256].bitcast(F32), ALU.subtract).then_inc(s_lo, 1)

            def group(i, n, last=False):
                for c in range(n + 4):
                    for b in range(2):
                        f, m = 2 * (c // 2) + b, 2 * (c - n) + b
                        if c >= n:
                            dve.wait_ge(s_tile, i * (2 * CH) + (2 * c + b + 1))
                            for which, at, width in segments:
                                j = 24 * idx + 16 + m
                                ins = dve.scalar_tensor_tensor(k.X[:, m, at:at + width], Y[b][:, at:at + width], mod[:, which, j:j + 1],
                                                               k.X[:, m, at:at + width], ALU.mult, ALU.add)
                            ins.then_inc(s_add, 1)
                        elif c % 2:
                            dve.wait_ge(s_silu, i * FG + (f + 1))
                            dve.wait_ge(s_tile, i * (2 * CH) + (2 * c + b + 1))
                            dve.tensor_tensor(tmp[:, b, :], tmp[:, b, :], U[b][:, 0:T], ALU.mult).then_inc(s_mul, 1)
                            dve.wait_ge(s_fhi, i * FG + (f + 1))
                            dve.tensor_tensor(f_lo[:, f, :], tmp[:, b, :], f_hi[:, f, :].bitcast(F32), ALU.subtract).then_inc(s_flo, 1)
                    if not last or c + 2 < n + 4:
                        chunk_lo(i, c + 2, n)
            dve.sem_inc(s_add, CREDIT)

            def modulated(kk):
                if kk >= 2:
                    dve.wait_ge(s_xlo, kk - 1)
                for which, at, width in segments:
                    j = 24 * idx + kk
                    ins = dve.tensor_scalar(tmp[:, kk % 2, at:at + width], k.X[:, kk, at:at + width], mod[:, which, j + 8:j + 9],
                                            mod[:, which, j:j + 1], ALU.mult, ALU.add)
                ins.then_inc(s_mod, 1)
            modulated(0)
            chunk_lo(0, 0, FG)
            for kk in range(KD):
                if kk + 1 < KD:
                    modulated(kk + 1)
                dve.wait_ge(s_xhi, kk + 1)
                dve.tensor_tensor(h_lo[:, kk, :], tmp[:, kk % 2, :], h_hi[:, kk, :].bitcast(F32), ALU.subtract).then_inc(s_xlo, 1)
            chunk_lo(0, 1, FG)
            dve.wait_ge(s_scaled, 1)
            with dve.Fori(0, FGS) as i:
                group(i, FG)
            group(FGS, FREST, last=True)
        W.skip(FGS * CH + FREST + 4)


def norm_stage(k, name, X, T, tiles, width, eps, gain, shift=None, center=True, out=None, func=None, then=None):
    nc = k.nc
    out = X if out is None else out
    halves = [(0, min(T, 512))] + ([(512, T - 512)] if T > 512 else [])
    with ExitStack() as st:
        sq = st.enter_context(nc.sbuf_tensor(f"{name}_sq", [P, 2, T], F32))
        rstd = st.enter_context(nc.sbuf_tensor(f"{name}_rstd", [P, T], F32))
        sem = lambda n: k.sem(f"{name}_{n}")
        s_mean, s_cen, s_sq, s_var, s_rs, s_root, s_nrm, s_out, s_h = (
            sem("mean"), sem("centred"), sem("squared"), sem("var"), sem("rs"), sem("root"), sem("scaled"), sem("out"), sem("h"))
        block = st.enter_context(nc.Block())
        MU, VAR = k.PS[0], k.PS[1]

        @block.tensor
        def _(pe):
            if center:
                for kk in range(tiles):
                    for at, n in halves:
                        ins = pe.matmul(MU[:, at:at + n], k.ones[:], X[:, kk, at:at + n], start=kk == 0, stop=kk == tiles - 1)
                ins.then_inc(s_mean, 1)
            for kk in range(tiles):
                pe.wait_ge(s_sq, kk + 1)
                for at, n in halves:
                    ins = pe.matmul(VAR[:, at:at + n], k.ones[:], sq[:, kk % 2, at:at + n], start=kk == 0, stop=kk == tiles - 1)
                ins.then_inc(s_var, 1)

        @block.scalar
        def _(act):
            for kk in range(tiles):
                if center:
                    act.wait_ge(s_cen, kk + 1)
                if kk >= 2:
                    act.wait_ge(s_var, kk - 1)
                act.activation(sq[:, kk % 2, :], X[:, kk, 0:T], ACT.Square).then_inc(s_sq, 1)
            act.wait_ge(s_rs, 1)
            act.activation(rstd[:], rstd[:], ACT.Ln).then_inc(s_root, 1)
            act.wait_ge(s_root, 1)
            act.activation(rstd[:], rstd[:], ACT.Exp, scale=-0.5).then_inc(s_root, 1)
            for kk in range(tiles):
                act.wait_ge(s_nrm, kk + 1)
                act.activation(out[:, kk, 0:T], out[:, kk, 0:T], func or ACT.Identity, scale=gain(kk),
                               bias=shift(kk) if shift else 0.0).then_inc(s_out, 1)

        @block.vector
        def _(dve):
            if center:
                dve.wait_ge(s_mean, 1)
                for kk in range(tiles):
                    dve.scalar_tensor_tensor(X[:, kk, 0:T], MU[:, 0:T], -1.0 / width, X[:, kk, 0:T],
                                             ALU.mult, ALU.add).then_inc(s_cen, 1)
            dve.wait_ge(s_var, tiles)
            dve.tensor_scalar(rstd[:], VAR[:, 0:T], 1.0 / width, eps, ALU.mult, ALU.add).then_inc(s_rs, 1)
            dve.wait_ge(s_root, 2)
            if center:
                dve.wait_ge(s_cen, tiles)
            for kk in range(tiles):
                dve.tensor_tensor(out[:, kk, 0:T], X[:, kk, 0:T], rstd[:], ALU.mult).then_inc(s_nrm, 1)

        if then is not None:
            @block.gpsimd
            def _(pool):
                l, idx, segments = then
                modulate_steps(pool, k.H, out, k.mod[l], idx, segments, lambda kk: pool.wait_ge(s_out, kk + 1), s_h)
                pool.wait_ge(s_h, KD)


class Job:

    def __init__(self, pe, act=None, dve=None, tmp=False):
        self.pe, self.act, self.dve, self.tmp = pe, act, dve, tmp


def product_stage(k, name, jobs, used=(), pool=None, act_first=None, dve_first=None, dve_last=None, loads=(), pe_needs_loads=True):
    nc = k.nc
    banks = 4
    by_act = [j for j, job in enumerate(jobs) if job.act]
    by_dve = [j for j, job in enumerate(jobs) if job.dve]
    count = lambda js, j: sum(x <= j for x in js)
    with ExitStack() as st:
        sem = lambda n: k.sem(f"{name}_{n}")
        s = Core()
        s.out, s.act, s.dve, s.chain, s.first, s.load, s.pool = (
            sem("products"), sem("act"), sem("dve"), sem("chain"), sem("first"), sem("load"), sem("pool"))
        s.n_chain, s.n_loads = [0], len(loads)
        s.link = lambda eng, ins: chained(eng, s.chain, s.n_chain, ins)
        s.acts_before = lambda j: count(by_act, j)
        s.dves_before = lambda j: count(by_dve, j)
        block = st.enter_context(nc.Block())

        @block.sync
        def _(sp):
            for dst, src in loads:
                sp.dma_start(dst, src).then_inc(s.load, 16)
            if used:
                k.weights.ahead(sp, *[(lambda i, r, u=u: (s.out, u(i, r) if callable(u) else u[SLOTS * i + r])) for u in used])

        @block.tensor
        def _(pe):
            if loads and pe_needs_loads:
                pe.wait_ge(s.load, 16 * len(loads))
            for j, job in enumerate(jobs):
                if j >= banks:
                    if jobs[j - banks].dve:
                        pe.wait_ge(s.dve, count(by_dve, j - banks))
                    else:
                        pe.wait_ge(s.act, count(by_act, j - banks))
                job.pe(pe, k.PS[j % banks], s).then_inc(s.out, 1)

        @block.scalar
        def _(act):
            if act_first:
                act_first(act, s)
            for j in by_act:
                act.wait_ge(s.out, j + 1)
                if jobs[j].tmp and j >= 2:
                    act.wait_ge(s.dve, count(by_dve, j - 2))
                jobs[j].act(act, k.PS[j % banks], s).then_inc(s.act, 1)

        @block.vector
        def _(dve):
            if dve_first:
                dve_first(dve, s)
            for nth, j in enumerate(by_dve):
                if nth >= 2:
                    dve.wait_ge(s.dve, nth - 1)
                if jobs[j].act:
                    dve.wait_ge(s.act, count(by_act, j))
                else:
                    dve.wait_ge(s.out, j + 1)
                jobs[j].dve(dve, k.PS[j % banks], s).then_inc(s.dve, 1)
            if dve_last:
                dve.wait_ge(s.dve, len(by_dve))
                dve_last(dve, s)

        if pool:
            @block.gpsimd
            def _(gp):
                pool(gp, s)


def feature_product(k, rhs, segments, weights, rows=P, cols=0, kt=KD, at_row=0):
    def pe_part(pe, bank, s):
        w = weights(pe)
        for kk in range(kt):
            for at, n in segments:
                ins = pe.matmul(bank[at_row:at_row + rows, at:at + n], w[:, kk, cols:cols + rows], rhs[:, kk, at:at + n],
                                start=kk == 0, stop=kk == kt - 1)
        return ins
    return pe_part


def shared(k, shape=lambda w: wide(w)):
    got = []

    def weights(pe):
        if not got:
            got.append(shape(k.weights.take(pe)))
        return got[0]
    return weights


def token_product(k, lhs, t, halves, n=512):
    def pe_part(pe, bank, s):
        ws = [h(pe) for h in halves]
        for kk in range(KD):
            ins = pe.matmul(bank[:, 0:n], lhs[:, kk, t * P:(t + 1) * P], ws[kk // 4][:, kk % 4, 0:n],
                            start=kk == 0, stop=kk == KD - 1)
        return ins
    return pe_part


def residual_stage(k, name, rhs, gate, scale=ALPHA, bias=None, last_scale=True):
    jobs = []
    for m in range(KD):
        if m % 2 == 0:
            w = shared(k)

        def add(dve, bank, s, m=m):
            if gate is None:
                return dve.tensor_tensor(k.X[:, m, 0:S], bank[:, 0:S], k.X[:, m, 0:S], ALU.add)
            return dve.scalar_tensor_tensor(k.X[:, m, 0:S], bank[:, 0:S], gate(m), k.X[:, m, 0:S], ALU.mult, ALU.add)
        jobs.append(Job(feature_product(k, rhs, [(0, S)], w, cols=(m % 2) * P), dve=add))

    def scale_x(pool, s):
        for kk in range(KD):
            if bias is None:
                ins = pool.tensor_scalar(k.X[:, kk, 0:S], k.X[:, kk, 0:S], scale, None, ALU.mult)
            else:
                ins = pool.tensor_scalar(k.X[:, kk, 0:S], k.X[:, kk, 0:S], scale, bias(kk), ALU.mult, ALU.add)
        ins.then_inc(s.pool, 1)
    needs_scaling = gate is not None
    product_stage(k, name, jobs, used=[[2 * c + 2 for c in range(4)]], pool=scale_x if needs_scaling else None,
                  dve_first=(lambda dve, s: dve.wait_ge(s.pool, 1)) if needs_scaling else None)


def even_mixer(k):
    nc, a = k.nc, k.a
    BOTH = [(0, S), (S, C)]
    with ExitStack() as st:
        sb = lambda n, shape: st.enter_context(nc.sbuf_tensor(n, shape, F32))
        QT, KT = sb("QT", [P, HEADS, S]), sb("KT", [P, HEADS, T0])
        V = sb("V", [P, T0 // P, HEADS * VD])
        AB = sb("AB", [P, KD, S])
        with ExitStack() as inner:
            sb = lambda n, shape: inner.enter_context(nc.sbuf_tensor(n, shape, F32))
            CQ, CKV, KR = sb("CQ", [P, 3, S]), sb("CKV", [P, 2, T0]), sb("KR", [P, 1, T0])
            UT, VT = sb("UT", [P, 4, S]), sb("VT", [P, ST, BW])
            copy_to = lambda dst, n, lo=0, hi=P: lambda act, bank, s: act.activation(dst[lo:hi], bank[lo:hi, 0:n], ACT.Copy)
            w0, w1, w2 = (shared(k), shared(k), shared(k, lambda w: wide(w, 160)))
            jobs = [Job(feature_product(k, k.H, BOTH[:1], w0), act=copy_to(CQ[:, 0, :], S)),
                    Job(feature_product(k, k.H, BOTH[:1], w0, cols=P), act=copy_to(CQ[:, 1, :], S)),
                    Job(feature_product(k, k.H, BOTH[:1], w1), act=copy_to(CQ[:, 2, :], S)),
                    Job(feature_product(k, k.H, BOTH, w1, cols=P), act=copy_to(CKV[:, 0, :], T0)),
                    Job(feature_product(k, k.H, BOTH, w2), act=copy_to(CKV[:, 1, :], T0)),
                    Job(feature_product(k, k.H, BOTH, w2, rows=QK, cols=64), act=copy_to(KR[:, 0, :], T0, NOPE, QK))]
            for m in range(4):
                if m % 2 == 0:
                    w = shared(k)
                jobs.append(Job(feature_product(k, k.H, BOTH[:1], w, cols=(m % 2) * P),
                                act=lambda act, bank, s, m=m: act.activation(UT[:, m, :], bank[:, 0:S], ACT.Gelu)))
            halves = [shared(k, lambda w: wide(w, 512, 4)) for _ in range(2)]
            for t in range(ST):
                jobs.append(Job(token_product(k, k.H, t, halves),
                                act=lambda act, bank, s, t=t: act.activation(VT[:, t, :], bank[:, 0:BW], ACT.Gelu)))
            product_stage(k, "e_in", jobs, used=[[2, 4, 6], [8, 10], [14, 14]])
            norm_stage(k, "e_qn", CQ, S, 3, Q_RANK, RMS_EPS, norm_columns(k, "e_q_norm"), center=False)
            norm_stage(k, "e_kvn", CKV, T0, 2, KV_RANK, RMS_EPS, norm_columns(k, "e_kv_norm"), center=False)
            spatial_norm(k, VT)
            even_heads(k, QT, KT, V, AB, CQ, CKV, KR, UT, VT)
        latent_attention(k, QT, KT, V, AB)
        residual_stage(k, "e_out", AB, lambda m: k.mod[0][:, 0, 40 + m:41 + m])


def spatial_norm(k, VT):
    nc, a = k.nc, k.a
    with ExitStack() as st:
        sb = lambda n, shape: st.enter_context(nc.sbuf_tensor(n, shape, F32))
        g, b, stats, mv, rs = sb("sgu_g", [P, BW]), sb("sgu_b", [P, BW]), sb("sgu_st", [P, ST, 6]), sb("sgu_mv", [P, ST, 2]), sb("sgu_rs", [P, ST])
        sem = lambda n: k.sem(f"sgu_{n}")
        s_ld, s_ch, s_sq = sem("load"), sem("chain"), sem("sqrt")
        block = st.enter_context(nc.Block())

        @block.sync
        def _(sp):
            sp.dma_start(g[:], a["e_sgu_g"].partition_broadcast(P)).then_inc(s_ld, 16)
            sp.dma_start(b[:], a["e_sgu_b"].partition_broadcast(P)).then_inc(s_ld, 16)

        @block.vector
        def _(dve):
            n = [0]
            for t in range(ST):
                ins = dve.bn_stats(stats[:, t, :], VT[:, t, :])
            chained(dve, s_ch, n, ins)
            for t in range(ST):
                ins = dve.bn_aggr(mv[:, t, :], stats[:, t, :])
            chained(dve, s_ch, n, ins)
            chained(dve, s_ch, n, dve.tensor_scalar(rs[:], mv[:, :, 1], LN_EPS, None, ALU.add))
            dve.wait_ge(s_sq, 1)
            chained(dve, s_ch, n, dve.reciprocal(rs[:], rs[:]))
            for t in range(ST):
                ins = dve.tensor_scalar(VT[:, t, :], VT[:, t, :], mv[:, t, 0:1], rs[:, t:t + 1], ALU.subtract, ALU.mult)
            chained(dve, s_ch, n, ins)
            dve.wait_ge(s_ld, 32)
            for t in range(ST):
                ins = dve.tensor_tensor(VT[:, t, :], VT[:, t, :], g[:], ALU.mult)
            chained(dve, s_ch, n, ins)
            for t in range(ST):
                ins = dve.tensor_tensor(VT[:, t, :], VT[:, t, :], b[:], ALU.add)
            chained(dve, s_ch, n, ins)

        @block.scalar
        def _(act):
            act.wait_ge(s_ch, 3)
            act.activation(rs[:], rs[:], ACT.Sqrt).then_inc(s_sq, 1)


def even_heads(k, QT, KT, V, AB, CQ, CKV, KR, UT, VT):
    nc, a = k.nc, k.a
    with ExitStack() as st:
        sb = lambda n, shape: st.enter_context(nc.sbuf_tensor(n, shape, F32))
        WS, WST, BS = sb("WS", [P, 4, P]), sb("WST", [P, 4, P]), sb("BS", [P, 4, P])
        rope, swap, t1 = sb("rope", [P, 2, S]), sb("swap", [P, QK]), sb("rot", [P, 2, S])
        loads = [(swap[0:QK, :], a["k_swap"]), (rope[0:QK, :, :], a["k_rope"].rearrange("w p t -> p w t")),
                 (WS[:], a["e_w_s"][0].rearrange("g i j -> i g j")),
                 (BS[:].rearrange("p g i -> p (g i)"), a["e_b_s"].rearrange("o g i -> o (g i)").partition_broadcast(P))]
        jobs = []

        def rotate(x, lo, hi, slot):
            def dve_part(dve, bank, s):
                s.link(dve, dve.tensor_tensor(t1[lo:hi, slot, :], bank[lo:hi, 0:S], rope[lo:hi, 1, :], ALU.mult))
                s.link(dve, dve.tensor_tensor(x, x, rope[lo:hi, 0, :], ALU.mult))
                return dve.tensor_tensor(x, x, t1[lo:hi, slot, :], ALU.add)
            return dve_part
        jobs.append(Job(lambda pe, bank, s: pe.matmul(bank[NOPE:QK, 0:S], swap[NOPE:QK, NOPE:QK], KR[NOPE:QK, 0, 0:S], start=True, stop=True),
                        dve=rotate(KR[NOPE:QK, 0, 0:S], NOPE, QK, 0)))
        wq = [shared(k, lambda w: wide(w, 384, 3)) for _ in range(2)]

        def swap_job(h):
            def pe_part(pe, bank, s):
                pe.wait_ge(s.act, h + 1)
                return pe.matmul(bank[0:QK, 0:S], swap[0:QK, :], QT[0:QK, h, :], start=True, stop=True)
            return Job(pe_part, dve=rotate(QT[0:QK, h, :], 0, QK, (h + 1) % 2))
        for h in range(HEADS):
            jobs.append(Job(feature_product(k, CQ, [(0, S)], wq[h // 4], rows=QK, cols=(h % 4) * QK, kt=3),
                            act=lambda act, bank, s, h=h: act.activation(QT[0:QK, h, :], bank[0:QK, 0:S], ACT.Copy)))
            if h == 4:
                after_first = len(jobs) - 1
            if h:
                jobs.append(swap_job(h - 1))
        after_q = len(jobs)
        jobs.append(swap_job(HEADS - 1))
        wkv = shared(k, lambda w: wide(w, 1024, 2))
        for h in range(HEADS):
            jobs.append(Job(feature_product(k, CKV, [(0, S), (S, C)], wkv, rows=NOPE, cols=h * P, kt=2),
                            act=lambda act, bank, s, h=h: act.activation(KT[0:NOPE, h, :], bank[0:NOPE, 0:T0], ACT.Copy)))
        for t in range(T0 // P):
            def values(pe, bank, s, t=t):
                w = wkv(pe).rearrange("p k (h c) -> p k h c", c=P)
                for kk in range(2):
                    ins = pe.matmul(bank[:, 0:512].rearrange("p (h c) -> p h c", c=VD), CKV[:, kk, t * P:(t + 1) * P], w[:, kk, :, NOPE:P],
                                    start=kk == 0, stop=kk == 1)
                return ins
            jobs.append(Job(values, dve=lambda dve, bank, s, t=t: dve.tensor_copy(V[:, t, :], bank[:, 0:512])))
        after_kv = len(jobs)

        def turn(pe, bank, s):
            for g in range(4):
                ins = pe.transpose(bank[:, g * P:(g + 1) * P], WS[:, g, :], k.ident[:])
            return ins
        jobs.append(Job(turn, act=lambda act, bank, s: act.activation(WST[:].rearrange("p g i -> p (g i)"), bank[:, 0:512], ACT.Copy)))
        turned = len(jobs)
        for c in range(ST):
            def mix(pe, bank, s, c=c):
                if c == 0:
                    pe.wait_ge(s.act, s.acts_before(turned))
                for g in range(4):
                    ins = pe.matmul(bank[:, g * P:(g + 1) * P], VT[:, c, g * P:(g + 1) * P], WST[:, g, :], start=True, stop=True)
                return ins

            def gated(dve, bank, s, c=c):
                m = t1[:, c % 2, :].rearrange("p (g i) -> p g i", g=4)
                s.link(dve, dve.tensor_tensor(m, bank[:, 0:512].rearrange("p (g i) -> p g i", g=4), BS[:], ALU.add))
                return dve.tensor_tensor(AB[:, 4:8, c * P:(c + 1) * P], m, UT[:, :, c * P:(c + 1) * P], ALU.mult)
            jobs.append(Job(mix, dve=gated))

        def spread(pool, s):
            pool.wait_ge(s.dve, 1)
            for h in range(HEADS):
                pool.tensor_copy(KT[NOPE:QK, h, :], KR[NOPE:QK, 0, :])
        product_stage(k, "e_heads", jobs, used=[[after_first, after_q], [after_kv]], loads=loads, pool=spread,
                      dve_first=lambda dve, s: dve.wait_ge(s.load, 16 * s.n_loads))


def latent_attention(k, QT, KT, V, AB):
    nc = k.nc
    NK = T0 // P
    with ExitStack() as st:
        sb = lambda n, shape: st.enter_context(nc.sbuf_tensor(n, shape, F32))
        PT = sb("PT", [P, 2, NK, S])
        mx, neg, rs, ri = sb("mx", [P, 8]), sb("neg", [P, 8]), sb("rs", [P, 8]), sb("ri", [P, 8])
        sem = lambda n: k.sem(f"att_{n}")
        s_sc, s_mx, s_nm, s_exp, s_ri, s_p, s_t, s_cv, s_ca, s_pv, s_o = (
            sem("scores"), sem("max"), sem("negmax"), sem("exp"), sem("rinv"), sem("probs"), sem("turned"),
            sem("copied_dve"), sem("copied_act"), sem("pv"), sem("out"))
        Pr = lambda n: k.H[:, 4 * ((n // 4) % 2) + n % 4, :]
        block = st.enter_context(nc.Block())
        T = lambda kt: k.PS[2][:, 512 * (kt % 2):512 * (kt % 2) + 512]
        O = lambda h: k.PS[3][:, 512 * (h // 2 % 2):512 * (h // 2 % 2) + 512]

        @block.tensor
        def _(pe):
            def scores(n):
                h, q = divmod(n, 4)
                if n >= 2:
                    pe.wait_ge(s_exp, n - 1)
                for at, w in ((0, S), (S, C)):
                    ins = pe.matmul(k.PS[n % 2][:, at:at + w], QT[0:QK, h, q * P:(q + 1) * P], KT[0:QK, h, at:at + w], start=True, stop=True)
                ins.then_inc(s_sc, 1)

            def turn(h, kt):
                if kt == 0:
                    pe.wait_ge(s_p, 4 * h + 4)
                n = NK * h + kt
                if n >= 2:
                    pe.wait_ge((s_cv, s_ca)[kt % 2], (n - 2) // 2 + 1)
                for q in range(4):
                    ins = pe.transpose(T(kt)[:, q * P:(q + 1) * P], Pr(4 * h + q)[:, kt * P:(kt + 1) * P], k.ident[:])
                ins.then_inc(s_t, 1)

            def pv(h, kt):
                pe.wait_ge((s_cv, s_ca)[kt % 2], (NK * h + kt) // 2 + 1)
                if kt == 0 and h % 2 == 0 and h >= 4:
                    pe.wait_ge(s_o, h // 2 - 1)
                r = VD * (h % 2)
                ins = pe.matmul(O(h)[r:r + VD, :], V[:, kt, h * VD:(h + 1) * VD], PT[:, h % 2, kt, :], start=kt == 0, stop=kt == NK - 1)
                if kt == NK - 1:
                    ins.then_inc(s_pv, 1)
            for q in range(4):
                scores(q)
            for h in range(HEADS):
                for kt in range(NK):
                    if kt < 4 and h + 1 < HEADS:
                        scores(4 * h + 4 + kt)
                    turn(h, kt)
                    if kt:
                        pv(h, kt - 1)
                pv(h, NK - 1)

        @block.vector
        def _(dve):
            def top(n):
                dve.wait_ge(s_sc, n + 1)
                dve.reduce_max(mx[:, n % 8:n % 8 + 1], k.PS[n % 2][:, 0:T0], AXX).then_inc(s_mx, 1)
                dve.wait_ge(s_mx, n + 1)
                if n >= 8:
                    dve.wait_ge(s_exp, n - 7)
                dve.tensor_scalar(neg[:, n % 8:n % 8 + 1], mx[:, n % 8:n % 8 + 1], -ATTN_SCALE, None, ALU.mult).then_inc(s_nm, 1)

            def norm(n):
                dve.wait_ge(s_exp, n + 1)
                dve.reciprocal(ri[:, n % 8:n % 8 + 1], rs[:, n % 8:n % 8 + 1]).then_inc(s_ri, 1)
                dve.wait_ge(s_ri, n + 1)
                dve.tensor_scalar(Pr(n), Pr(n), ri[:, n % 8:n % 8 + 1], None, ALU.mult).then_inc(s_p, 1)

            def copy(h, kt):
                n = NK * h + kt
                dve.wait_ge(s_t, n + 1)
                if h >= 2:
                    dve.wait_ge(s_pv, h - 1)
                dve.tensor_copy(PT[:, h % 2, kt, :], T(kt)).then_inc(s_cv, 1)
            for q in range(4):
                top(q)
                if q:
                    norm(q - 1)
            norm(3)
            for h in range(HEADS):
                for kt in range(NK):
                    if kt < 4 and h + 1 < HEADS:
                        top(4 * h + 4 + kt)
                    if kt % 2 == 0:
                        copy(h, kt)
                    if 1 <= kt < 5 and h + 1 < HEADS:
                        norm(4 * h + 3 + kt)

        @block.scalar
        def _(act):
            def expo(n):
                act.wait_ge(s_nm, n + 1)
                if n >= 8:
                    act.wait_ge(s_t, NK * ((n - 4) // 4))
                    act.wait_ge(s_ri, n - 7)
                act.activation(Pr(n), k.PS[n % 2][:, 0:T0], ACT.Exp, bias=neg[:, n % 8:n % 8 + 1], scale=ATTN_SCALE,
                               accum_out=rs[:, n % 8:n % 8 + 1]).then_inc(s_exp, 1)

            for q in range(4):
                expo(q)
            for h in range(HEADS):
                for kt in range(NK):
                    if kt < 4 and h + 1 < HEADS:
                        expo(4 * h + 4 + kt)
                    if kt % 2:
                        act.wait_ge(s_t, NK * h + kt + 1)
                        if h >= 2:
                            act.wait_ge(s_pv, h - 1)
                        act.activation(PT[:, h % 2, kt, :], T(kt), ACT.Copy).then_inc(s_ca, 1)
                if h % 2:
                    act.wait_ge(s_pv, h + 1)
                    act.activation(AB[:, h // 2, :], O(h), ACT.Copy).then_inc(s_o, 1)


def conv_mixer(k):
    nc, a = k.nc, k.a
    c = lambda name: norm_columns(k, name)
    b1, bdw, wdw = c("o_b_pw1"), c("o_b_dw"), c("o_w_dw")
    with ExitStack() as st:
        sb = lambda n, shape: st.enter_context(nc.sbuf_tensor(n, shape, F32))
        Y = sb("conv_in", [P, KD, S + 2 * PAD])
        sig = sb("conv_sig", [P, 2, S])
        jobs = []
        for c2 in range(4):
            wg, wv = shared(k), shared(k)
            for half in range(2):
                m = 2 * c2 + half

                def both(pe, bank, s, wg=wg, wv=wv, half=half):
                    feature_product(k, k.H, [(0, S)], wg, cols=half * P)(pe, bank[:, 512:1024], s)
                    return feature_product(k, k.H, [(0, S)], wv, cols=half * P)(pe, bank, s)
                jobs.append(Job(both, tmp=True,
                                act=lambda act, bank, s, m=m: act.activation(sig[:, m % 2, :], bank[:, 512:1024], ACT.Sigmoid, bias=b1(KD + m)),
                                dve=lambda dve, bank, s, m=m: dve.scalar_tensor_tensor(Y[:, m, PAD:PAD + S], bank[:, 0:S], b1(m), sig[:, m % 2, :], ALU.add, ALU.mult)))

        def edges(pool, s):
            pool.memset(Y[:, :, 0:PAD], 0.0)
            pool.memset(Y[:, :, PAD + S:], 0.0)
            for kk in range(KD):
                ins = pool.tensor_tensor(k.cond2[:, kk:kk + 1], c("o_b_out")(kk), k.mod[1][:, 0, 40 + kk:41 + kk], ALU.mult)
        product_stage(k, "c_in", jobs, used=[[2 * (r // 2) + 2 for r in range(8)]], pool=edges)
        depthwise(k, Y, wdw, bdw)
        norm_stage(k, "c_n", k.H, S, KD, D, LN_EPS, c("o_ln_g"), c("o_ln_b"), func=ACT.Silu)
        residual_stage(k, "c_out", k.H, lambda m: k.mod[1][:, 0, 40 + m:41 + m], bias=lambda kk: k.cond2[:, kk:kk + 1])


ON_PE = 13


def depthwise(k, Y, wdw, bdw):
    nc = k.nc
    with ExitStack() as st:
        sb = lambda n, shape: st.enter_context(nc.sbuf_tensor(n, shape, F32))
        diag = sb("diag", [P, 4, P])
        sem = lambda n: k.sem(f"dw_{n}")
        s_diag, s_tap, s_pe, s_acc, s_left = sem("diagonals"), sem("taps"), sem("summed"), sem("acc"), sem("left")
        block = st.enter_context(nc.Block())

        @block.scalar
        def _(act):
            for n in range(KD * ON_PE):
                m, w = divmod(n, ON_PE)
                if n >= 4:
                    act.wait_ge(s_tap, n - 3)
                act.activation(diag[:, n % 4, :], k.ident[:], ACT.Copy, scale=wdw(w * KD + m)).then_inc(s_diag, 1)

        @block.tensor
        def _(pe):
            for n in range(KD * ON_PE):
                m, w = divmod(n, ON_PE)
                if w == 0 and m >= 4:
                    pe.wait_ge(s_left, m - 3)
                pe.wait_ge(s_diag, n + 1)
                pe.matmul(k.PS[m % 4][:, 0:S], diag[:, n % 4, :], Y[:, m, w:w + S], start=w == 0, stop=w == ON_PE - 1).then_inc(s_tap, 1)

        @block.vector
        def _(dve):
            n = 0

            def step(ins):
                nonlocal n
                ins.then_inc(s_acc, 1)
                n += 1
            for m0 in range(0, KD, 2):
                for m in (m0, m0 + 1):
                    step(dve.tensor_scalar(k.H[:, m, 0:S], Y[:, m, ON_PE:ON_PE + S], wdw(ON_PE * KD + m), bdw(m), ALU.mult, ALU.add))
                for w in range(ON_PE + 1, TAPS):
                    for m in (m0, m0 + 1):
                        dve.wait_ge(s_acc, n - 1)
                        step(dve.scalar_tensor_tensor(k.H[:, m, 0:S], Y[:, m, w:w + S], wdw(w * KD + m), k.H[:, m, 0:S], ALU.mult, ALU.add))
                for m in (m0, m0 + 1):
                    dve.wait_ge(s_acc, n - 1 + m - m0)
                    dve.wait_ge(s_tap, (m + 1) * ON_PE)
                    dve.tensor_tensor(k.H[:, m, 0:S], k.PS[m % 4][:, 0:S], k.H[:, m, 0:S], ALU.add).then_inc(s_left, 1)


def second_block(k, out, stop):
    nc, a = k.nc, k.a
    c = lambda name: norm_columns(k, name)
    norm_stage(k, "s_n1", k.X, S, KD, D, 1e-6, c("norm1_g_2"), center=False, out=k.H)
    with ExitStack() as st:
        OG = st.enter_context(nc.sbuf_tensor("gla_out", [P, GH, S], F32))
        linear_attention(k, OG)
        if stop == 5:
            return stop_here(k)
        with ExitStack() as inner:
            sb = lambda n, shape: inner.enter_context(nc.sbuf_tensor(n, shape, F32))
            dil = dict(q=sb("dil_q", [P, GROUPS, GH, S]), k=sb("dil_k", [P, GROUPS, GH, S]), v=sb("dil_v", [P, GROUPS, ST, S]),
                       bias=sb("alibi", [P, GROUPS, GH, S]))
            dilated_attention(k, dil)
            if stop == 6:
                return stop_here(k)
            k.MX = dil["k"][:, 0:2, :, :].rearrange("p g h t -> p (g h) t")
            merge_branches(k, OG, dil["q"][:, 0, :, :])
            residual_stage(k, "s_out", k.MX, None)
    if stop == 7:
        return stop_here(k)
    norm_stage(k, "s_n2", k.X, S, KD, D, 1e-6, c("norm2_g_2"), center=False, out=k.H)
    k.renew_semaphores()
    mixture(k, out, stop)


def to_rows(x):
    return x.rearrange("p h t -> p (h t)")


def linear_attention(k, OG):
    nc, a = k.nc, k.a
    w = a["w_in_2"][0]
    with ExitStack() as st:
        sb = lambda n, shape: st.enter_context(nc.sbuf_tensor(n, shape, F32))
        Q, K, R, V = sb("gq", [P, GH, S]), sb("gk", [P, GH, S]), sb("gr", [P, GH, S]), sb("gv", [P, ST, S])
        Z, KE, KET = sb("gz", [P, GH, S]), sb("gke", [P, GH, S]), sb("gket", [P, ST, S])
        E = sb("ge", [P, GH, S])
        LR, WA, reset = sb("glr", [P, S]), sb("gwa", [P, S]), sb("reset", [P, S])
        causal, chunk = sb("causal", [P, P]), sb("chunk_mask", [P, P // GC])
        jobs = []
        one = [(0, S)]
        for name, dst, first in (("q", Q, 0), ("k", K, 4)):
            for m in range(4):
                if m % 2 == 0:
                    wt = shared(k)
                jobs.append(Job(feature_product(k, k.H, one, wt, cols=(m % 2) * P),
                                act=lambda act, bank, s, m=m, dst=dst: act.activation(
                                    dst[:, m, :], bank[:, 0:S], ACT.Copy, scale=P ** -0.5 if dst is Q else 1.0)))
        halves = [shared(k, lambda w: wide(w, 512, 4)) for _ in range(2)]
        for t in range(ST):
            jobs.append(Job(token_product(k, k.H, t, halves), dve=lambda dve, bank, s, t=t: dve.tensor_copy(V[:, t, :], bank[:, 0:S])))
        for m in range(4):
            if m % 2 == 0:
                wt = shared(k)
            jobs.append(Job(feature_product(k, k.H, one, wt, cols=(m % 2) * P),
                            act=lambda act, bank, s, m=m: act.activation(R[:, m, :], bank[:, 0:S], ACT.Silu)))
        wl = shared(k, lambda w: wide(w, GC))
        jobs.append(Job(feature_product(k, k.H, one, wl, rows=GC),
                        act=lambda act, bank, s: act.activation(LR[0:GC, :], bank[0:GC, 0:S], ACT.Copy)))
        lowrank = len(jobs)
        b = norm_columns(k, "b_gla_a_2")
        for m in range(4):
            def decay(pe, bank, s, m=m):
                if m == 0:
                    pe.wait_ge(s.act, s.acts_before(lowrank))
                return pe.matmul(bank[:, 0:S], WA[0:GC, m * P:(m + 1) * P], LR[0:GC, :], start=True, stop=True)
            jobs.append(Job(decay, dve=lambda dve, bank, s, m=m: dve.tensor_scalar(Z[:, m, :], bank[:, 0:S], b(m), None, ALU.add)))
        product_stage(k, "g_in", jobs, used=[[2, 4, 6, 8], [12, 12], [14, 16, 17]],
                      loads=[(WA[0:GC, :], a["w_gla_a2_2"][0]), (reset[:], a["k_reset"]), (causal[:], a["k_causal"]), (chunk[:], a["k_chunk"])])
        s_a, s_d, s_p = k.sem("gd_act"), k.sem("gd_dve"), k.sem("gd_pool")
        fl = to_rows
        with nc.Block() as block:
            @block.scalar
            def _(act):
                act.activation(fl(E[:]), fl(Z[:]), ACT.Abs).then_inc(s_a, 1)
                act.wait_ge(s_a, 1)
                act.activation(fl(E[:]), fl(E[:]), ACT.Exp, scale=-1.0).then_inc(s_a, 1)
                act.wait_ge(s_a, 2)
                act.activation(fl(E[:]), fl(E[:]), ACT.Ln, bias=1.0).then_inc(s_a, 1)
                act.wait_ge(s_d, 6)
                act.activation(fl(KE[:]), fl(KE[:]), ACT.Exp, scale=1.0 / GLA_TAU).then_inc(s_a, 1)
                act.activation(fl(E[:]), fl(Z[:]), ACT.Exp, scale=-1.0 / GLA_TAU).then_inc(s_a, 1)
                act.wait_ge(s_a, 5)
                act.activation(fl(Z[:]), fl(Z[:]), ACT.Exp, scale=1.0 / GLA_TAU).then_inc(s_a, 1)

            @block.vector
            def _(dve):
                dve.wait_ge(s_a, 3)
                dve.scalar_tensor_tensor(fl(E[:]), fl(Z[:]), 0.0, fl(E[:]), ALU.min, ALU.subtract).then_inc(s_d, 1)
                dve.wait_ge(s_d, 1)
                for h in range(GH):
                    dve.tensor_tensor_scan(Z[:, h, :], reset[:], E[:, h, :], 0.0, ALU.mult, ALU.add).then_inc(s_d, 1)
                dve.wait_ge(s_d, 5)
                z = fl(Z[:]).rearrange("p (c i) -> p c i", i=GC)
                dve.tensor_tensor(fl(KE[:]).rearrange("p (c i) -> p c i", i=GC), z[:, :, GC - 1:GC].broadcast_to([P, GH * NCH, GC]), z,
                                  ALU.subtract).then_inc(s_d, 1)
                dve.wait_ge(s_a, 4)
                dve.tensor_tensor(fl(KE[:]), fl(KE[:]), fl(K[:]), ALU.mult).then_inc(s_d, 1)
                dve.wait_ge(s_a, 5)
                dve.wait_ge(s_d, 7)
                dve.tensor_tensor(fl(K[:]), fl(E[:]), fl(K[:]), ALU.mult).then_inc(s_d, 1)
                dve.wait_ge(s_a, 6)
                dve.tensor_tensor(fl(Q[:]), fl(Z[:]), fl(Q[:]), ALU.mult).then_inc(s_d, 1)
                dve.wait_ge(s_d, 9)
        jobs = []
        for t in range(ST):
            def turn(pe, bank, s, t=t):
                for h in range(GH):
                    ins = pe.transpose(bank[:, h * P:(h + 1) * P], KE[:, h, t * P:(t + 1) * P], k.ident[:])
                return ins
            jobs.append(Job(turn, act=lambda act, bank, s, t=t: act.activation(KET[:, t, :], bank[:, 0:S], ACT.Copy)))
        product_stage(k, "g_turn", jobs)
        gla_scan(k, Q, K, V, KET, Z, causal, chunk, OG)
        row_norm_stage(k, "g_norm", [(OG[:, h, :], norm_columns(k, "gla_out_norm_g_2")(0), None) for h in range(GH)], 1e-6)
        s_g = k.sem("gate_done")
        with nc.Block() as block:
            @block.vector
            def _(dve):
                dve.tensor_tensor(fl(OG[:]), fl(OG[:]), fl(R[:]), ALU.mult).then_inc(s_g, 1)
                dve.wait_ge(s_g, 1)


def gla_scan(k, Q, K, V, KET, DEC, causal, chunk, OG):
    nc = k.nc
    NC = P // GC
    N = ST * GH
    with ExitStack() as st:
        sb = lambda n, shape: st.enter_context(nc.sbuf_tensor(n, shape, F32))
        VX, AT, SS = sb("v_spread", [P, 2, NC, P]), sb("att", [P, 2, P]), sb("states", [P, GH, NC + 1, P])
        sem = lambda n: k.sem(f"gs_{n}")
        s_vx, s_att, s_kv, s_mask, s_st, s_scan, s_o, s_oc = (sem("v_spread"), sem("att"), sem("kv"), sem("masked"),
                                                              sem("state"), sem("scanned"), sem("out"), sem("copied"))
        block = st.enter_context(nc.Block())
        A = lambda n: k.PS[2][:, 512 * (n % 2):512 * (n % 2) + P]
        O = lambda n: k.PS[3][:, 512 * (n % 2):512 * (n % 2) + P]
        tok = lambda n: slice((n // GH) * P, (n // GH + 1) * P)

        @block.gpsimd
        def _(pool):
            for n in range(N):
                t, h = divmod(n, GH)
                if n >= 2:
                    pool.wait_ge(s_kv, n - 1)
                pool.tensor_tensor(VX[:, n % 2, :, :], V[:, t:t + 1, h * P:(h + 1) * P].broadcast_to([P, NC, P]),
                                   chunk[:].unsqueeze(2).broadcast_to([P, NC, P]), ALU.mult).then_inc(s_vx, 1)

        @block.tensor
        def _(pe):
            def first(n):
                t, h = divmod(n, GH)
                if n >= 2:
                    pe.wait_ge(s_mask, n - 1)
                pe.matmul(A(n), K[:, h, tok(n)], Q[:, h, tok(n)], start=True, stop=True).then_inc(s_att, 1)
                pe.wait_ge(s_vx, n + 1)
                if n >= 2:
                    pe.wait_ge(s_scan, n - 1)
                for c in range(2):
                    ins = pe.matmul(k.PS[n % 2][:, 512 * c:512 * c + 512], KET[:, t, h * P:(h + 1) * P],
                                    VX[:, n % 2, 4 * c:4 * c + 4, :].rearrange("p a b -> p (a b)"), start=True, stop=True)
                ins.then_inc(s_kv, 1)

            def second(n):
                t, h = divmod(n, GH)
                pe.wait_ge(s_mask, n + 1)
                pe.wait_ge(s_scan, n + 1)
                if n >= 2:
                    pe.wait_ge(s_oc, n - 1)
                pe.matmul(O(n), V[:, t, h * P:(h + 1) * P], AT[:, n % 2, :], start=True, stop=True)
                for c in range(NC):
                    at = t * P + c * GC
                    ins = pe.matmul(O(n)[:, c * GC:(c + 1) * GC], SS[:, h, c, :], Q[:, h, at:at + GC], start=False, stop=True,
                                    skip_group_check=True)
                ins.then_inc(s_o, 1)
            first(0)
            for n in range(N):
                if n + 1 < N:
                    first(n + 1)
                second(n)

        @block.vector
        def _(dve):
            c_st = [0]
            chained(dve, s_st, c_st, dve.memset(SS[:, :, 0, :], 0.0))
            for n in range(N):
                t, h = divmod(n, GH)
                dve.wait_ge(s_att, n + 1)
                if n >= 2:
                    dve.wait_ge(s_o, n - 1)
                dve.tensor_tensor(AT[:, n % 2, :], A(n), causal[:], ALU.mult).then_inc(s_mask, 1)
                if t:
                    dve.wait_ge(s_o, n - GH + 1)
                    chained(dve, s_st, c_st, dve.tensor_copy(SS[:, h, 0, :], SS[:, h, NC, :]))
                dve.wait_ge(s_kv, n + 1)
                for c in range(NC):
                    at = t * P + c * GC + GC - 1
                    ins = dve.scalar_tensor_tensor(SS[:, h, c + 1, :], SS[:, h, c, :], DEC[:, h, at:at + 1],
                                                   k.PS[n % 2][:, c * P:(c + 1) * P], ALU.mult, ALU.add)
                    if c < NC - 1:
                        chained(dve, s_st, c_st, ins)
                ins.then_inc(s_scan, 1)
                dve.wait_ge(s_scan, n + 1)

        @block.scalar
        def _(act):
            for n in range(N):
                act.wait_ge(s_o, n + 1)
                act.activation(OG[:, n % GH, tok(n)], O(n), ACT.Copy).then_inc(s_oc, 1)


def row_norm_stage(k, name, items, eps):
    nc = k.nc
    N = len(items)
    full = [n for n in range(N) if items[n][2] is None]
    with ExitStack() as st:
        sb = lambda n, shape: st.enter_context(nc.sbuf_tensor(f"{name}_{n}", shape, F32))
        sq, rs, bc = sb("sq", [P, 2, S]), sb("rs", [P, 4 * N]), sb("bc", [P, 2, ST, P])
        sem = lambda n: k.sem(f"{name}_{n}")
        s_sq, s_ss, s_rs, s_rt, s_bc, s_bk, s_out, s_gain = (sem("squared"), sem("sums"), sem("rs"), sem("root"),
                                                             sem("spread"), sem("bank"), sem("out"), sem("gain"))
        block = st.enter_context(nc.Block())

        @block.scalar
        def _(act):
            for n in range(N):
                if n >= 2:
                    act.wait_ge(s_ss, n - 1)
                act.activation(sq[:, n % 2, :], items[n][0], ACT.Square).then_inc(s_sq, 1)
            act.wait_ge(s_rs, 1)
            act.activation(rs[:], rs[:], ACT.Sqrt).then_inc(s_rt, 1)
            act.wait_ge(s_sq, N)
            for n in range(N):
                if items[n][2] is not None:
                    act.activation(items[n][0], items[n][0], ACT.Copy, scale=items[n][1])

        @block.tensor
        def _(pe):
            for n in range(N):
                pe.wait_ge(s_sq, n + 1)
                for t in range(ST):
                    ins = pe.matmul(k.PS[0][:, 4 * n + t:4 * n + t + 1], sq[:, n % 2, t * P:(t + 1) * P], k.ones[:, 0:1], start=True, stop=True)
                ins.then_inc(s_ss, 1)
            for j, n in enumerate(full):
                pe.wait_ge(s_bc, j + 1)
                if j >= 3:
                    pe.wait_ge(s_out, j - 2)
                for t in range(ST):
                    ins = pe.matmul(k.PS[1 + j % 3][:, t * P:(t + 1) * P], bc[:, j % 2, t, :], k.ident[:], start=True, stop=True)
                ins.then_inc(s_bk, 1)

        @block.vector
        def _(dve):
            dve.wait_ge(s_ss, N)
            dve.tensor_scalar(rs[:], k.PS[0][:, 0:4 * N], 1.0 / P, eps, ALU.mult, ALU.add).then_inc(s_rs, 1)
            dve.wait_ge(s_rt, 1)
            dve.reciprocal(rs[:], rs[:]).then_inc(s_rs, 1)
            dve.wait_ge(s_rs, 2)
            for n in range(N):
                if items[n][2] is not None:
                    dve.tensor_copy(items[n][2], rs[:, 4 * n:4 * n + 4])
            for j, n in enumerate(full + [None]):
                if n is not None:
                    if j >= 2:
                        dve.wait_ge(s_bk, j - 1)
                    for t in range(ST):
                        ins = dve.tensor_scalar(bc[:, j % 2, t, :], k.ones[:], rs[:, 4 * n + t:4 * n + t + 1], None, ALU.mult)
                    ins.then_inc(s_bc, 1)
                if j:
                    view, gain, _ = items[full[j - 1]]
                    dve.wait_ge(s_bk, j)
                    dve.scalar_tensor_tensor(view, view, gain, k.PS[1 + (j - 1) % 3][:, 0:S], ALU.mult, ALU.mult).then_inc(s_out, 1)
            dve.wait_ge(s_out, len(full))


def dilated_attention(k, dil):
    nc, a = k.nc, k.a
    w = a["w_in_2"][0]
    with ExitStack() as st:
        sb = lambda n, shape: st.enter_context(nc.sbuf_tensor(n, shape, F32))
        RQ = sb("rq", [P, GROUPS, GH, ST])
        jobs, used, items = [], [], []
        for g in range(GROUPS):
            for dst in (dil["q"], dil["k"]):
                for m in range(4):
                    if m % 2 == 0:
                        wt = shared(k)
                    jobs.append(Job(feature_product(k, k.H, [(0, S)], wt, cols=(m % 2) * P),
                                    act=lambda act, bank, s, m=m, g=g, dst=dst: act.activation(dst[:, g, m, :], bank[:, 0:S], ACT.Copy)))
                    name, where = ("dil_q_norm_g_2", RQ[:, g, m, :]) if dst is dil["q"] else ("dil_k_norm_g_2", None)
                    items.append((dst[:, g, m, :], norm_columns(k, name)(g), where))
            halves = [shared(k, lambda w: wide(w, 512, 4)) for _ in range(2)]
            for t in range(ST):
                jobs.append(Job(token_product(k, k.H, t, halves),
                                dve=lambda dve, bank, s, t=t, g=g: dve.tensor_copy(dil["v"][:, g, t, :], bank[:, 0:S])))
            used += [[12 * g + 2, 12 * g + 4, 12 * g + 6, 12 * g + 8], [12 * g + 12] * 2]
        product_stage(k, "d_in", jobs, used=used, pe_needs_loads=False, dve_last=lambda dve, s: dve.wait_ge(s.load, 16 * s.n_loads),
                      loads=[(dil["bias"][:, g, :, :], a["k_alibi"][g].rearrange("h p c -> p h c")) for g in range(GROUPS)])
        row_norm_stage(k, "d_norm", items, 1e-6)
        dilated_scores(k, dil, RQ)


def dilated_scores(k, dil, RQ):
    nc = k.nc
    N = GH * ST
    keys = [[list(range(max(0, t - 1), t + 1)), list(range(t + 1)), list(range(t + 1))] for t in range(ST)]
    tiles = [[(g, kt) for g in range(GROUPS) for kt in keys[t][g]] for t in range(ST)]
    lumps = [-(-len(x) // 4) for x in tiles]
    first_lump = [sum(lumps[m % ST] for m in range(n)) for n in range(N + 1)]
    with ExitStack() as st:
        sb = lambda n, shape: st.enter_context(nc.sbuf_tensor(n, shape, F32))
        SC, PT = sb("dil_scores", [P, 2, 10 * P]), sb("dil_turned", [P, 2, 10 * P])
        mx, neg, rs, ri, rqs = sb("dmx", [P, 2]), sb("dneg", [P, 2]), sb("drs", [P, 2]), sb("dri", [P, 2]), sb("drq", [P, GROUPS * GH * ST])
        sem = lambda n: k.sem(f"ds_{n}")
        s_rq, s_sc, s_bias, s_mx, s_nm, s_exp, s_ri, s_p, s_t, s_c, s_o, s_oc = (
            sem("rq"), sem("scores"), sem("biased"), sem("max"), sem("negmax"), sem("exp"), sem("rinv"), sem("probs"),
            sem("turned"), sem("copied"), sem("out"), sem("out_copied"))
        block = st.enter_context(nc.Block())
        B = lambda j: k.PS[j % 4 // 2][:, 512 * (j % 2):512 * (j % 2) + 512]
        T = lambda j: k.PS[2][:, 512 * (j % 2):512 * (j % 2) + 512]
        O = lambda n: k.PS[3][:, 512 * (n % 2):512 * (n % 2) + P]

        @block.tensor
        def _(pe):
            def scores(n):
                h, t = divmod(n, ST)
                for g in range(GROUPS):
                    j = GROUPS * n + g
                    if j >= 4:
                        pe.wait_ge(s_bias, j - 3)
                    k0, kn = keys[t][g][0], len(keys[t][g])
                    pe.matmul(B(j)[:, 0:kn * P], dil["q"][:, g, h, t * P:(t + 1) * P], dil["k"][:, g, h, k0 * P:(k0 + kn) * P],
                              start=True, stop=True).then_inc(s_sc, 1)

            def output(n):
                h, t = divmod(n, ST)
                pe.wait_ge(s_p, n + 1)
                for c in range(lumps[t]):
                    j = first_lump[n] + c
                    if j >= 2:
                        pe.wait_ge(s_c, j - 1)
                    part = tiles[t][4 * c:4 * c + 4]
                    for i in range(len(part)):
                        ins = pe.transpose(T(j)[:, i * P:(i + 1) * P], SC[:, n % 2, (4 * c + i) * P:(4 * c + i + 1) * P], k.ident[:])
                    ins.then_inc(s_t, 1)
                if n >= 2:
                    pe.wait_ge(s_oc, n - 1)
                for c in range(lumps[t]):
                    pe.wait_ge(s_c, first_lump[n] + c + 1)
                    for i, (g, kt) in enumerate(tiles[t][4 * c:4 * c + 4]):
                        x = 4 * c + i
                        ins = pe.matmul(O(n), dil["v"][:, g, kt, h * P:(h + 1) * P], PT[:, n % 2, x * P:(x + 1) * P],
                                        start=x == 0, stop=x == len(tiles[t]) - 1)
                ins.then_inc(s_o, 1)
            scores(0)
            for n in range(N):
                if n + 1 < N:
                    scores(n + 1)
                output(n)

        @block.vector
        def _(dve):
            dve.tensor_scalar(rqs[:], RQ[:].rearrange("p g h t -> p (g h t)"), P ** -0.5, None, ALU.mult).then_inc(s_rq, 1)
            dve.wait_ge(s_rq, 1)

            def score(n):
                h, t = divmod(n, ST)
                at = 0
                if n >= 2:
                    dve.wait_ge(s_t, first_lump[n - 1])
                for g in range(GROUPS):
                    w = len(keys[t][g]) * P
                    dve.wait_ge(s_sc, GROUPS * n + g + 1)
                    r = (g * GH + h) * ST + t
                    dve.scalar_tensor_tensor(SC[:, n % 2, at:at + w], B(GROUPS * n + g)[:, 0:w], rqs[:, r:r + 1],
                                             dil["bias"][:, g, h, S - w:S], ALU.mult, ALU.add).then_inc(s_bias, 1)
                    at += w
                dve.wait_ge(s_bias, GROUPS * (n + 1))
                dve.reduce_max(mx[:, n % 2:n % 2 + 1], SC[:, n % 2, 0:at], AXX).then_inc(s_mx, 1)
                dve.wait_ge(s_mx, n + 1)
                if n >= 2:
                    dve.wait_ge(s_exp, n - 1)
                dve.tensor_scalar(neg[:, n % 2:n % 2 + 1], mx[:, n % 2:n % 2 + 1], -1.0, None, ALU.mult).then_inc(s_nm, 1)

            def normalise(n):
                w = len(tiles[n % ST]) * P
                dve.wait_ge(s_exp, n + 1)
                dve.reciprocal(ri[:, n % 2:n % 2 + 1], rs[:, n % 2:n % 2 + 1]).then_inc(s_ri, 1)
                dve.wait_ge(s_ri, n + 1)
                dve.tensor_scalar(SC[:, n % 2, 0:w], SC[:, n % 2, 0:w], ri[:, n % 2:n % 2 + 1], None, ALU.mult).then_inc(s_p, 1)
            score(0)
            normalise(0)
            for n in range(N):
                if n + 1 < N:
                    score(n + 1)
                    normalise(n + 1)

        @block.scalar
        def _(act):
            def expo(n):
                w = len(tiles[n % ST]) * P
                act.wait_ge(s_nm, n + 1)
                if n >= 2:
                    act.wait_ge(s_ri, n - 1)
                act.activation(SC[:, n % 2, 0:w], SC[:, n % 2, 0:w], ACT.Exp, bias=neg[:, n % 2:n % 2 + 1],
                               accum_out=rs[:, n % 2:n % 2 + 1]).then_inc(s_exp, 1)

            def copies(n):
                h, t = divmod(n, ST)
                if n >= 2:
                    act.wait_ge(s_o, n - 1)
                for c in range(lumps[t]):
                    w = min(4, len(tiles[t]) - 4 * c) * P
                    act.wait_ge(s_t, first_lump[n] + c + 1)
                    act.activation(PT[:, n % 2, 4 * c * P:4 * c * P + w], T(first_lump[n] + c)[:, 0:w], ACT.Copy).then_inc(s_c, 1)
            expo(0)
            for n in range(N):
                if n + 1 < N:
                    expo(n + 1)
                copies(n)
                h, t = divmod(n, ST)
                act.wait_ge(s_o, n + 1)
                act.activation(dil["q"][:, 0, h, t * P:(t + 1) * P], O(n), ACT.Copy).then_inc(s_oc, 1)


def merge_branches(k, OG, OA):
    nc, a = k.nc, k.a
    b = norm_columns(k, "b_branch_gate_2")
    with ExitStack() as st:
        G = st.enter_context(nc.sbuf_tensor("branch_gates", [P, 2, 2, S], F32))
        t1 = st.enter_context(nc.sbuf_tensor("branch_tmp", [P, 2, S], F32))
        jobs = []
        for c in range(4):
            ws = [shared(k), shared(k), shared(k, lambda w: wide(w, 256, 4)), shared(k, lambda w: wide(w, 256, 4))]
            for half in range(2):
                m = 2 * c + half

                def gates(pe, bank, s, ws=ws, half=half):
                    feature_product(k, k.H, [(0, S)], ws[0], cols=half * P)(pe, bank, s)
                    return feature_product(k, k.H, [(0, S)], ws[1], cols=half * P)(pe, bank[:, 512:1024], s)

                def gate_act(act, bank, s, m=m):
                    if m >= 2:
                        act.wait_ge(s.dve, m - 1)
                    act.activation(G[:, m % 2, 0, :], bank[:, 0:S], ACT.Sigmoid, bias=b(m))
                    return act.activation(G[:, m % 2, 1, :], bank[:, 512:1024], ACT.Sigmoid, bias=b(KD + m))

                def projections(pe, bank, s, ws=ws, half=half):
                    feature_product(k, OG, [(0, S)], ws[2], cols=half * P, kt=4)(pe, bank, s)
                    return feature_product(k, OA, [(0, S)], ws[3], cols=half * P, kt=4)(pe, bank[:, 512:1024], s)

                def mix(dve, bank, s, m=m):
                    dve.wait_ge(s.act, m + 1)
                    s.link(dve, dve.tensor_tensor(t1[:, m % 2, :], bank[:, 512:1024], G[:, m % 2, 1, :], ALU.mult))
                    s.link(dve, dve.tensor_tensor(k.MX[:, m, :], bank[:, 0:S], G[:, m % 2, 0, :], ALU.mult))
                    return dve.tensor_tensor(k.MX[:, m, :], t1[:, m % 2, :], k.MX[:, m, :], ALU.add)
                jobs += [Job(gates, act=gate_act), Job(projections, dve=mix)]
        product_stage(k, "merge", jobs, used=[lambda i, r: i * 4 + (3 if r < 2 else 4)])


DUMMY = 2 * S


def mixture(k, out, stop):
    nc, a = k.nc, k.a
    k.rows_dram = nc.dram_tensor("normed_rows", (S, D), F32).ap()
    k.table = nc.dram_tensor("dispatch_table", (TABLE, 1), U32).ap()
    k.expert_out = nc.dram_tensor("expert_outputs", (DUMMY + TABLE, D), F32).ap()
    with ExitStack() as st:
        sb = lambda n, shape, dt=F32: st.enter_context(nc.sbuf_tensor(n, shape, dt))
        XR = sb("x_rows", [P, ST, D])
        gates = sb("gates", [P, 2, ST])
        pairs = sb("pairs", [P, 1], I32)
        ids, tokens = sb("slot_ids", [P, ST * EXPERTS + 2], U32), sb("slot_tokens", [P, ST * EXPERTS + 2], U32)
        route(k, XR, gates, pairs, ids, tokens)
        if stop == 8:
            return stop_here(k)
        experts(k, pairs, ids, tokens)
        combine(k, XR, gates, out)


def route(k, XR, gates, pairs, ids_by_turn, tokens_by_turn):
    nc, a = k.nc, k.a
    with ExitStack() as st:
        sb = lambda n, shape, dt=F32: st.enter_context(nc.sbuf_tensor(n, shape, dt))
        HR = sb("rt_h_rows", [P, ST, D])
        WR, BR = sb("rt_w_router", [P, KD, NG + EXPERTS]), sb("rt_b_router", [P, NG + EXPERTS])
        before, eid = sb("rt_before", [P, P]), sb("rt_expert_ids", [P, EXPERTS])
        GL, EL = sb("rt_group_logits", [P, ST, EG]), sb("rt_expert_logits", [P, ST, EXPERTS])
        top, topi, gi = sb("rt_top", [P, ST, 8]), sb("rt_topi", [P, ST, 8], U32), sb("rt_group", [P, ST, 8], U32)
        gtop, gif = sb("rt_gtop", [P, ST, 8]), sb("rt_gif", [P, ST])
        neg, eg, gs = sb("rt_neg", [P, ST]), sb("rt_eg", [P, ST, NG]), sb("rt_gs", [P, ST])
        gid, m1, ex, idf = sb("rt_gid", [P, EXPERTS]), sb("rt_m1", [P, ST, EXPERTS]), sb("rt_ex", [P, ST]), sb("rt_idf", [P, 2, ST])
        hot, both, rank, sel = sb("rt_hot", [P, 2, ST, EXPERTS]), sb("rt_both", [P, ST, EXPERTS]), sb("rt_rank", [P, ST, EXPERTS]), sb("rt_sel", [P, 2, ST, EXPERTS])
        loc, locu = sb("rt_loc", [P, 2, ST]), sb("rt_locu", [P, 2, ST], U32)
        cmax, pf = sb("rt_cmax", [P, 1]), sb("rt_pf", [P, 4])
        init, ids = sb("rt_table_init", [P, TABLE // P], U32), sb("rt_ids", [P, 2, ST], U32)
        sem = lambda n: k.sem(f"rt_{n}")
        s_ld, s_t, s_ca, s_cd, s_lg, s_ch, s_act, s_rk, s_rows, s_iota, s_tab, s_gn = (
            sem("load"), sem("turned"), sem("copied_act"), sem("copied_dve"), sem("logits"), sem("chain"), sem("act"),
            sem("ranks"), sem("rows"), sem("iota"), sem("table"), sem("gates"))
        block = st.enter_context(nc.Block())

        @block.sync
        def _(sp):
            sp.dma_start(WR[:, :, 0:NG], rows_of(a["w_router_group_2"][0])).then_inc(s_ld, 16)
            sp.dma_start(WR[:, :, NG:], rows_of(a["w_router_expert_2"][0])).then_inc(s_ld, 16)
            sp.dma_start(BR[:, 0:NG], a["b_router_group_2"].partition_broadcast(P)).then_inc(s_ld, 16)
            sp.dma_start(BR[:, NG:], a["b_router_expert_2"].partition_broadcast(P)).then_inc(s_ld, 16)
            sp.dma_start(before[:], a["k_before"]).then_inc(s_ld, 16)
            sp.dma_start(eid[:], a["k_expert"]).then_inc(s_ld, 16)
            sp.dma_start(gid[:], a["k_group"]).then_inc(s_ld, 16)
            sp.wait_ge(s_ca, 2 * ST)
            sp.dma_start(k.rows_dram.rearrange("(t p) d -> p t d", p=P), HR[:]).then_inc(s_rows, 16)
            sp.wait_ge(s_rows, 16)

        @block.tensor
        def _(pe):
            pe.wait_ge(s_ld, 16 * 7)
            for t in range(ST):
                for kk in range(KD):
                    ins = pe.matmul(k.PS[3][:, 64 * t:64 * t + NG + EXPERTS], k.H[:, kk, t * P:(t + 1) * P], WR[:, kk, :], start=kk == 0, stop=kk == KD - 1)
            ins.then_inc(s_lg, 1)
            def rows_of_tokens(bank, x, s_c):
                for j in range(2 * ST):
                    t, half = divmod(j, 2)
                    if j >= 2:
                        pe.wait_ge(s_c, j - 1)
                    for c in range(4):
                        ins = pe.transpose(bank[:, 512 * half + c * P:512 * half + (c + 1) * P], x[:, 4 * half + c, t * P:(t + 1) * P], k.ident[:])
                    ins.then_inc(s_t, 1)
            rows_of_tokens(k.PS[0], k.H, s_ca)
            pe.wait_ge(s_rk, 1)
            for t in range(ST):
                for u in range(t):
                    pe.matmul(k.PS[2][:, 32 * t:32 * t + 32], k.ones[:], both[:, u, :], start=u == 0, stop=False)
                pe.matmul(k.PS[2][:, 32 * t:32 * t + 32], before[:], both[:, t, :], start=t == 0, stop=True)
            for t in range(ST):
                ins = pe.matmul(k.PS[2][:, 512:544], k.ones[:], both[:, t, :], start=t == 0, stop=t == ST - 1)
            ins.then_inc(s_rk, 1)
            rows_of_tokens(k.PS[1], k.X, s_cd)

        @block.scalar
        def _(act):
            for t in range(ST):
                for half in range(2):
                    act.wait_ge(s_t, 2 * t + half + 1)
                    act.activation(HR[:, t, 512 * half:512 * half + 512], k.PS[0][:, 512 * half:512 * half + 512], ACT.Copy).then_inc(s_ca, 1)
            act.wait_ge(s_gn, 1)
            for t in range(ST):
                ins = act.activation(eg[:, t, :], GL[:, t, 0:NG], ACT.Exp, bias=neg[:, t:t + 1], accum_out=gs[:, t:t + 1])
            ins.then_inc(s_act, 1)
            act.wait_ge(s_gn, 2)
            act.activation(ex[:], ex[:], ACT.Exp).then_inc(s_act, 1)

        @block.vector
        def _(dve):
            n = [0]
            link = lambda ins: chained(dve, s_ch, n, ins)
            dve.memset(GL[:], -1e30).then_inc(s_ch, 1)
            n[0] += 1
            dve.wait_ge(s_ld, 16 * 7)
            dve.wait_ge(s_lg, 1)
            dve.wait_ge(s_ch, 1)
            lg = k.PS[3][:, 0:64 * ST].rearrange("p (t e) -> p t e", e=64)
            bc = lambda x, w: x.unsqueeze(1).broadcast_to([P, ST, w])
            link(dve.tensor_tensor(GL[:, :, 0:NG], lg[:, :, 0:NG], bc(BR[:, 0:NG], NG), ALU.add))
            link(dve.tensor_tensor(EL[:], lg[:, :, NG:NG + EXPERTS], bc(BR[:, NG:], EXPERTS), ALU.add))
            for t in range(ST):
                ins = dve.max(gtop[:, t, :], GL[:, t, :])
            link(ins)
            for t in range(ST):
                ins = dve.max_index(gi[:, t, :], gtop[:, t, :], GL[:, t, :])
            link(ins)
            dve.tensor_scalar(neg[:], gtop[:, :, 0], -1.0, None, ALU.mult).then_inc(s_gn, 1)
            link(dve.tensor_copy(gif[:], gi[:, :, 0]))
            for t in range(ST):
                ins = dve.tensor_scalar(m1[:, t, :], gid[:], gif[:, t:t + 1], None, ALU.is_equal)
            link(ins)
            link(dve.tensor_tensor(EL[:], EL[:], m1[:], ALU.mult))
            link(dve.tensor_scalar(m1[:], m1[:], 1.0, 1e30, ALU.subtract, ALU.mult))
            link(dve.tensor_tensor(EL[:], EL[:], m1[:], ALU.add))
            for t in range(ST):
                ins = dve.max(top[:, t, :], EL[:, t, :])
            link(ins)
            for t in range(ST):
                ins = dve.max_index(topi[:, t, :], top[:, t, :], EL[:, t, :])
            link(ins)
            dve.tensor_tensor(ex[:], top[:, :, 1], top[:, :, 0], ALU.subtract).then_inc(s_gn, 1)
            link(dve.tensor_copy(idf[:], topi[:, :, 0:2].rearrange("p t c -> p c t")))
            for c in range(2):
                for t in range(ST):
                    ins = dve.tensor_scalar(hot[:, c, t, :], eid[:], idf[:, c, t:t + 1], None, ALU.is_equal)
            link(ins)
            dve.tensor_tensor(both[:], hot[:, 0, :, :], hot[:, 1, :, :], ALU.add).then_inc(s_rk, 1)
            dve.wait_ge(s_act, 1)
            link(dve.reciprocal(gs[:], gs[:]))
            dve.wait_ge(s_act, 2)
            link(dve.tensor_scalar(gates[:, 0, :], ex[:], 1.0, None, ALU.add))
            link(dve.reciprocal(gates[:, 0, :], gates[:, 0, :]))
            link(dve.tensor_tensor(gates[:, 0, :], gates[:, 0, :], gs[:], ALU.mult))
            link(dve.tensor_tensor(gates[:, 1, :], gates[:, 0, :], ex[:], ALU.mult))
            dve.wait_ge(s_rk, 2)
            link(dve.tensor_copy(rank[:], k.PS[2][:, 0:32 * ST].rearrange("p (t e) -> p t e", e=32)))
            for c in range(2):
                ins = dve.tensor_tensor(sel[:, c, :, :], hot[:, c, :, :], rank[:], ALU.mult)
            link(ins)
            link(dve.tensor_reduce(loc[:], sel[:], AXX, ALU.add))
            link(dve.tensor_scalar(loc[:], loc[:], float(EXPERTS), None, ALU.mult))
            link(dve.tensor_tensor(loc[:], loc[:], idf[:], ALU.add))
            dve.tensor_copy(locu[:], loc[:]).then_inc(s_gn, 1)
            link(dve.reduce_max(cmax[:], k.PS[2][:, 512:544], AXX))
            for i in range(1, ST):
                ins = dve.tensor_scalar(pf[:, i:i + 1], cmax[:], float(P * i), None, ALU.is_gt)
            link(ins)
            link(dve.memset(pf[:, 0:1], 1.0))
            link(dve.tensor_reduce(cmax[:], pf[:], AXX, ALU.add))
            link(dve.tensor_scalar(cmax[:], cmax[:], float(EXPERTS // 2), None, ALU.mult))
            link(dve.tensor_copy(pairs[:], cmax[:]))
            link(dve.memset(ids_by_turn[:, ST * EXPERTS:], 0))
            for t in range(ST):
                for half in range(2):
                    dve.wait_ge(s_t, 2 * ST + 2 * t + half + 1)
                    dve.tensor_copy(XR[:, t, 512 * half:512 * half + 512], k.PS[1][:, 512 * half:512 * half + 512]).then_inc(s_cd, 1)
            dve.wait_ge(s_cd, 2 * ST)
            dve.wait_ge(s_tab, 16 * (2 + 2 * ST))
            link(dve.tensor_scalar(tokens_by_turn[:], ids_by_turn[:], S - 1, None, ALU.bitwise_and))

        @block.gpsimd
        def _(pool):
            pool.iota(init[:], pattern=[[1, TABLE // P]], base=DUMMY, channel_multiplier=TABLE // P).then_inc(s_iota, 1)
            pool.iota(ids[:], pattern=[[S, 2], [P, ST]], base=0, channel_multiplier=1).then_inc(s_iota, 1)
            pool.wait_ge(s_iota, 2)
            pool.dma_start(k.table.rearrange("(p j) o -> p (j o)", p=P), init[:]).then_inc(s_tab, 16)
            pool.wait_ge(s_tab, 16)
            pool.wait_ge(s_gn, 3)
            for c in range(2):
                for t in range(ST):
                    pool.indirect_dma_start(out=k.table, out_offset=bass.IndirectOffsetOnAxis(ap=locu[:, c, t:t + 1], axis=0),
                                            in_=ids[:, c, t:t + 1], in_offset=None).then_inc(s_tab, 16)
            pool.wait_ge(s_tab, 16 * (1 + 2 * ST))
            pool.dma_start(ids_by_turn[:, 0:ST * EXPERTS].rearrange("p (b e) -> p b e", b=ST),
                           k.table.rearrange("(b p e) o -> p b (e o)", b=ST, p=P)).then_inc(s_tab, 16)
            pool.wait_ge(s_tab, 16 * (2 + 2 * ST))


def experts(k, pairs, ids, tokens):
    nc, a = k.nc, k.a
    LOADS = 6
    ring, landed = k.weights.ring, k.weights.landed
    base = [16 * len(range(s, k.weights.total, SLOTS)) for s in range(SLOTS)]
    off = k.weights.total % SLOTS
    with ExitStack() as st:
        sb = lambda n, shape, dt=F32: st.enter_context(nc.sbuf_tensor(n, shape, dt))
        id_now = [sb(f"ids_now{i}", [P, 1], U32) for i in range(2)]
        token_now = [sb(f"tokens_now{i}", [P, 1], U32) for i in range(2)]
        XG, XT = sb("x_slots", [P, 2, D]), sb("x_turned", [P, 2, KD, P])
        SL, HE, YS = sb("ex_silu", [P, 2, DE]), sb("ex_hidden", [P, 2, DE]), sb("y_slots", [P, 2, D])
        sem = lambda n: k.sem(f"ex_{n}")
        s_ic, s_t, s_xa, s_xd, s_used, s_silu, s_he, s_ya, s_yd = (
            sem("ids_now"), sem("turned"), sem("xt_act"), sem("xt_dve"), sem("weights_used"), sem("silu"),
            sem("hidden"), sem("y_act"), sem("y_dve"))
        s_xg, s_ys = [sem(f"gathered{i}") for i in range(2)], [sem(f"scattered{i}") for i in range(2)]
        s_go = sem("go")
        s_free = [sem(f"rows_free{i}") for i in range(2)]
        block = st.enter_context(nc.Block())
        G, U = k.PS[1][:, 0:512], k.PS[1][:, 512:1024]
        steps = lambda eng: eng.value_load(pairs[0:1, 0:1], min_val=EXPERTS // 2, max_val=ST * EXPERTS // 2)

        @block.sync
        def _(sp):
            with sp.Fori(0, steps(sp)) as m:
                for c in range(2 * LOADS):
                    u, part = divmod(c, LOADS)
                    slot = (off + c) % SLOTS
                    sp.wait_ge(s_used, m * (2 * LOADS) + (c + 1))
                    e = (m % (EXPERTS // 2)) * 2 + u
                    if part < 4:
                        src = a["w_gate_2" if part < 2 else "w_up_2"][0]
                        view = wide(ring[:, slot, :])
                        src = src.rearrange("e (k p) n -> p e k n", p=P)[:, bass.ds(e, 1), :, 256 * (part % 2):256 * (part % 2) + 256]
                    else:
                        view = wide(ring[:, slot, :], 512, 4)
                        src = a["w_down_2"][0].rearrange("e (k p) n -> p e k n", p=P)[:, bass.ds(e, 1), :, 512 * (part % 2):512 * (part % 2) + 512]
                    sp.dma_start(view, src.rearrange("p e k n -> p (e k) n")).then_inc(landed[slot], 16)

        @block.gpsimd
        def _(pool):
            def gather(u, m):
                at = m * 2 + u
                col = slice(at, at + 1) if isinstance(at, int) else bass.ds(at, 1)
                if not isinstance(m, int) or m:
                    pool.wait_ge(s_ys[u], m * 16)
                pool.sem_inc(s_free[u], 1)
                pool.tensor_copy(id_now[u][:], ids[:, col]).then_inc(s_ic, 1)
                pool.tensor_copy(token_now[u][:], tokens[:, col]).then_inc(s_ic, 1)
                pool.wait_ge(s_t, m * 2 + (u + 1))
                pool.wait_ge(s_ic, m * 4 + (2 * u + 2))
                pool.sem_inc(s_go, 1)
                pool.indirect_dma_start(out=XG[:, u, :], out_offset=None, in_=k.rows_dram,
                                        in_offset=bass.IndirectOffsetOnAxis(ap=token_now[u][:, 0:1], axis=0)).then_inc(s_xg[u], 16)

            def scatter(u, m):
                pool.wait_ge(s_ya, m * 2 + (u + 3))
                pool.wait_ge(s_yd, m * 2 + (u + 3))
                pool.sem_inc(s_go, 1)
                pool.indirect_dma_start(out=k.expert_out, out_offset=bass.IndirectOffsetOnAxis(ap=id_now[u][:, 0:1], axis=0),
                                        in_=YS[:, u, :], in_offset=None).then_inc(s_ys[u], 16)
            gather(0, 0)
            gather(1, 0)
            scatter(0, 0)
            gather(0, 1)
            scatter(1, 0)
            n = steps(pool)
            with pool.Fori(1, n) as m:
                gather(1, m)
                scatter(0, m)
                gather(0, m + 1)
                scatter(1, m)
            pool.wait_ge(s_xg[0], n * 16 + 16)
            for u in range(2):
                pool.wait_ge(s_ys[u], n * 16)

        @block.tensor
        def _(pe):
            pe.sem_inc(s_used, SLOTS)
            pe.sem_inc(s_t, 2)

            def weights(u, part, m):
                c = LOADS * u + part
                slot = (off + c) % SLOTS
                uses = len([x for x in range(c + 1) if (off + x) % SLOTS == slot])
                pe.wait_ge(landed[slot], m * (16 * 2 * LOADS // SLOTS) + (base[slot] + 16 * uses))
                return ring[:, slot, :]

            def turn(u, m):
                pe.wait_ge(s_xg[u], m * 16 + 16)
                pe.wait_ge(s_xa, m * 2 + (u + 1))
                pe.wait_ge(s_xd, m * 2 + (u + 1))
                for kk in range(KD):
                    ins = pe.transpose(k.PS[0][:, kk * P:(kk + 1) * P], XG[:, u, kk * P:(kk + 1) * P], k.ident[:])
                ins.then_inc(s_t, 1)

            def up(u, m):
                pe.wait_ge(s_xa, m * 2 + (u + 2))
                pe.wait_ge(s_xd, m * 2 + (u + 2))
                for bank, first in ((G, 0), (U, 2)):
                    pe.wait_ge(s_silu if first == 0 else s_he, m * 2 + (u + (1 if first == 0 else 2)))
                    for half in range(2):
                        w = wide(weights(u, first + half, m))
                        for f in range(2):
                            for kk in range(KD):
                                at = (2 * half + f) * P
                                ins = pe.matmul(bank[:, at:at + P], w[:, kk, f * P:(f + 1) * P], XT[:, u, kk, :], start=kk == 0, stop=kk == KD - 1)
                        ins.then_inc(s_used, 1)

            def down(u, m):
                pe.wait_ge(s_he, m * 2 + (u + 3))
                pe.wait_ge(s_ya, m * 2 + (u + 1))
                pe.wait_ge(s_yd, m * 2 + (u + 1))
                for half in range(2):
                    w = wide(weights(u, 4 + half, m), 512, 4)
                    for f in range(4):
                        ins = pe.matmul(k.PS[2 + u][:, 512 * half:512 * half + 512], HE[:, u, f * P:(f + 1) * P], w[:, f, :],
                                        start=f == 0, stop=f == 3)
                    ins.then_inc(s_used, 1)

            turn(0, 0)
            with pe.Fori(0, steps(pe)) as m:
                up(0, m)
                turn(1, m)
                down(0, m)
                up(1, m)
                turn(0, m + 1)
                down(1, m)

        def copy_turned(eng, copy, half, done, u, m):
            eng.wait_ge(s_t, m * 2 + (u + 3))
            eng.wait_ge(s_he, m * 2 + (u + 1))
            copy(XT[:, u, 4 * half:4 * half + 4, :], k.PS[0][:, 512 * half:512 * half + 512].rearrange("p (a b) -> p a b", a=4)).then_inc(done, 1)

        def copy_out(eng, copy, half, done, u, m):
            eng.wait_ge(s_used, m * (2 * LOADS) + (LOADS * u + 5 + half + SLOTS))
            eng.wait_ge(s_free[u], m + 1)
            copy(YS[:, u, 512 * half:512 * half + 512], k.PS[2 + u][:, 512 * half:512 * half + 512]).then_inc(done, 1)

        @block.scalar
        def _(act):
            copy = lambda dst, src: act.activation(dst, src, ACT.Copy)
            act.sem_inc(s_xa, 1)
            act.sem_inc(s_silu, 1)
            act.sem_inc(s_ya, 2)

            def silu(u, m):
                act.wait_ge(s_used, m * (2 * LOADS) + (LOADS * u + 2 + SLOTS))
                act.wait_ge(s_he, m * 2 + (u + 1))
                act.activation(SL[:, u, :], G, ACT.Silu).then_inc(s_silu, 1)
            copy_turned(act, copy, 0, s_xa, 0, 0)
            with act.Fori(0, steps(act)) as m:
                silu(0, m)
                copy_turned(act, copy, 0, s_xa, 1, m)
                copy_out(act, copy, 0, s_ya, 0, m)
                silu(1, m)
                copy_turned(act, copy, 0, s_xa, 0, m + 1)
                copy_out(act, copy, 0, s_ya, 1, m)

        @block.vector
        def _(dve):
            copy = lambda dst, src: dve.tensor_copy(dst, src)
            dve.sem_inc(s_xd, 1)
            dve.sem_inc(s_he, 2)
            dve.sem_inc(s_yd, 2)

            def hidden(u, m):
                dve.wait_ge(s_silu, m * 2 + (u + 2))
                dve.wait_ge(s_used, m * (2 * LOADS) + (LOADS * u + 4 + SLOTS))
                dve.tensor_tensor(HE[:, u, :], SL[:, u, :], U, ALU.mult).then_inc(s_he, 1)
            copy_turned(dve, copy, 1, s_xd, 0, 0)
            with dve.Fori(0, steps(dve)) as m:
                hidden(0, m)
                copy_turned(dve, copy, 1, s_xd, 1, m)
                copy_out(dve, copy, 1, s_yd, 0, m)
                hidden(1, m)
                copy_turned(dve, copy, 1, s_xd, 0, m + 1)
                copy_out(dve, copy, 1, s_yd, 1, m)


def combine(k, XR, gates, out):
    nc = k.nc
    with ExitStack() as st:
        Y = st.enter_context(nc.sbuf_tensor("chosen_out", [P, 2, ST, D], F32))
        s_y = [k.sem(f"cb_loaded{t}") for t in range(ST)]
        s_1, s_2, s_out = k.sem("cb_first"), k.sem("cb_second"), k.sem("cb_out")
        block = st.enter_context(nc.Block())
        rows = out[0].rearrange("(t p) d -> p t d", p=P)
        chosen = k.expert_out[0:2 * S, :].rearrange("(c t p) d -> p c t d", c=2, p=P)

        @block.sync
        def _(sp):
            for t in range(ST):
                sp.dma_start(Y[:, :, t, :], chosen[:, :, t, :]).then_inc(s_y[t], 16)
            for t in range(ST):
                sp.wait_ge(s_2, t + 1)
                sp.dma_start(rows[:, t, :], XR[:, t, :]).then_inc(s_out, 16)
            sp.wait_ge(s_out, 16 * ST)

        @block.vector
        def _(dve):
            for t in range(ST):
                dve.wait_ge(s_y[t], 16)
                for c, done in ((0, s_1), (1, s_2)):
                    if c:
                        dve.wait_ge(s_1, t + 1)
                    dve.scalar_tensor_tensor(XR[:, t, :], Y[:, c, t, :], gates[:, c, t:t + 1], XR[:, t, :], ALU.mult, ALU.add).then_inc(done, 1)


def norm_columns(k, name, base=0):
    return lambda kk: k.col[:, COLUMN[name] + base + kk:COLUMN[name] + base + kk + 1]


def stop_here(k):
    with k.nc.Block() as block:
        @block.sync
        def _(sp):
            for s in range(SLOTS):
                sp.wait_ge(k.weights.landed[s], 16 * ((k.weights.issued - s + SLOTS - 1) // SLOTS))


def build(nc, a, out, stop=None):
    k = Core()
    k.nc, k.a, k.stage_sems = nc, a, []
    flat = lambda ap, pat: ap.rearrange(pat, p=P)
    k.flat = {
        "c": flat(a["c"], "o (k p) -> (o k) p"), "c_ctx": flat(a["c_ctx"], "(k p) -> k p"),
        "b_mod": flat(a["b_mod"], "l (k p) -> (l k) p"),
        "ln_g": flat(a["ln_g"], "l s (k p) -> (l s k) p"), "ln_b": flat(a["ln_b"], "l s (k p) -> (l s k) p"),
        "o_w_dw": flat(a["o_w_dw"], "o w (k p) -> (o w k) p"),
        "dil_q_norm_g_2": a["dil_q_norm_g_2"][0], "dil_k_norm_g_2": a["dil_k_norm_g_2"][0],
    }
    for name, _ in VECTORS:
        if name not in k.flat:
            k.flat[name] = flat(a[name], "o (k p) -> (o k) p")
    with ExitStack() as st:
        sb = lambda n, shape, dt=F32: st.enter_context(nc.sbuf_tensor(n, shape, dt))
        k.ident, k.ones = sb("ident", [P, P]), sb("ones", [P, P])
        k.col = sb("col", [P, COL_TILES * P])
        k.mod = [sb(f"mod{l}", [P, 2, 72]) for l in range(2)]
        k.cond = sb("cond", [P, 2, KD])
        k.cond2 = sb("conv_bias", [P, KD])
        k.X = sb("X", [P, KD, T0])
        ring = sb("weight_ring", [P, SLOTS, SLOT])
        k.PS = [st.enter_context(nc.psum_tensor(f"banks{i}", [P, 1024], F32)) for i in range(4)]
        landed = [st.enter_context(nc.semaphore(f"weights_landed{i}")) for i in range(SLOTS)]
        k.weights = WeightRing(ring, landed)
        plan_weights(k)
        LAT = [(0, 0, S)]
        BOTH = [(0, 0, S), (1, S, C)]
        ln = lambda l, s: (norm_columns(k, "ln_g", 24 * l + 8 * s), norm_columns(k, "ln_b", 24 * l + 8 * s))

        load_stage(k)
        adaln_stage(k, 0)
        ffn_stage(k, "f00", 0, 0, 0, BOTH)
        with ExitStack() as first:
            k.H = first.enter_context(nc.sbuf_tensor("H", [P, KD, T0], F32))
            norm_stage(k, "n00", k.X, T0, KD, D, LN_EPS, *ln(0, 0), then=(0, 1, BOTH))
            if stop == 1:
                return stop_here(k)
            even_mixer(k)
            if stop == 4:
                return stop_here(k)
        with ExitStack() as rest:
            k.H = rest.enter_context(nc.sbuf_tensor("H2", [P, KD, S], F32))
            norm_stage(k, "n01", k.X, S, KD, D, LN_EPS, *ln(0, 1))
            ffn_stage(k, "f01", 0, 1, 2, LAT)
            k.renew_semaphores()
            adaln_stage(k, 1)
            norm_stage(k, "n02", k.X, S, KD, D, LN_EPS, *ln(0, 2))
            if stop == 2:
                return stop_here(k)
            ffn_stage(k, "f10", 1, 0, 0, LAT)
            norm_stage(k, "n10", k.X, S, KD, D, LN_EPS, *ln(1, 0), then=(1, 1, LAT))
            conv_mixer(k)
            norm_stage(k, "n11", k.X, S, KD, D, LN_EPS, *ln(1, 1))
            ffn_stage(k, "f11", 1, 1, 2, LAT)
            norm_stage(k, "n12", k.X, S, KD, D, LN_EPS, *ln(1, 2))
            if stop == 3:
                return stop_here(k)
            k.renew_semaphores()
            second_block(k, out, stop)


def shape_constants():
    import numpy as np
    f = np.float32
    out = {"k_ident": np.eye(P, dtype=f)}
    p, q = np.arange(P)[:, None], np.arange(P)[None, :]
    out["k_causal"] = ((p // GC == q // GC) & (p <= q)).astype(f)
    out["k_before"] = (p < q).astype(f)
    out["k_chunk"] = (p // GC == np.arange(P // GC)[None, :]).astype(f)
    out["k_reset"] = np.broadcast_to((np.arange(S) % GC != 0).astype(f), (P, S)).copy()
    inv = (1.0 / (f(10000.0) ** (np.arange(0, ROPE // 2, 2, dtype=f) / f(ROPE // 2)))).astype(f)
    t = np.arange(S)
    ang = np.concatenate([(t // 64).astype(f)[:, None] * inv, (t % 64).astype(f)[:, None] * inv], axis=-1)
    rope = np.zeros((2, QK, S), f)
    rope[0, :NOPE] = 1.0
    rope[0, NOPE:] = np.repeat(np.cos(ang).T, 2, axis=0)
    rope[1, NOPE:] = np.repeat(np.sin(ang).T, 2, axis=0)
    out["k_rope"] = rope
    swap = np.zeros((QK, QK), f)
    for i in range(NOPE, QK, 2):
        swap[i + 1, i], swap[i, i + 1] = -1.0, 1.0
    out["k_swap"] = swap
    dist = (p + 384 - np.arange(S)[None, :])
    bias = np.zeros((GROUPS, GH, P, S), f)
    for g, (dil, span) in enumerate(((1, 128), (4, 128), (16, 128))):
        ok = (dist >= 0) & (dist % dil == 0) & (dist // dil <= span)
        for h in range(GH):
            slope = f(2.0 ** (-8.0 * (g * GH + h + 1) / (GROUPS * GH)))
            bias[g, h] = np.where(ok, -slope * dist.astype(f), f(-1e30))
    out["k_alibi"] = bias
    out["k_expert"] = np.broadcast_to(np.arange(EXPERTS, dtype=f), (P, EXPERTS)).copy()
    out["k_group"] = out["k_expert"] // EG
    return out


def kernel(**inputs):
    import numpy as np
    import concourse.bacc as bacc
    from concourse.bass_utils import run_bass_kernel_spmd

    nc = bacc.Bacc("TRN2", target_bir_lowering=False, num_devices=1)
    arrays = {n: np.ascontiguousarray(v) for n, v in inputs.items()}
    arrays.update(shape_constants())
    args = {n: nc.dram_tensor(n, v.shape, mybir.dt.from_np(v.dtype), kind="ExternalInput").ap()
            for n, v in arrays.items()}
    out = nc.dram_tensor("out", (1, S, D), F32, kind="ExternalOutput").ap()
    build(nc, args, out)
    r = run_bass_kernel_spmd(nc, [arrays], core_ids=[0])
    return r.results[0]["out"]
```

```python
import math
from contextlib import ExitStack

import concourse.bass as bass
from concourse import mybir

P = 128
ACT = mybir.ActivationFunctionType
ALU = mybir.AluOpType
AXX = mybir.AxisListType.X
F32 = mybir.dt.float32
F32R = mybir.dt.float32r
U32 = mybir.dt.uint32
I32 = mybir.dt.int32

D = 1024
KD = D // P
S = 512
C = 256
T0 = S + C
ST = S // P
FF = 2816
KF = FF // P
FG = 8
FGS, FREST = KF // FG, KF % FG
ALPHA = 4.0 ** 0.25
LN_EPS = 1e-5
RMS_EPS = 1e-6
HEADS = 8
NOPE, ROPE, VD = 64, 32, 64
QK = NOPE + ROPE
Q_RANK, KV_RANK = 384, 256
ATTN_SCALE = 1.0 / math.sqrt(QK)
BW = 512
TAPS = 31
PAD = TAPS // 2
GH = 4
GC = 16
NCH = S // GC
GLA_TAU = 16.0
GROUPS = 3
EXPERTS = 32
EG = 8
NG = 4
DE = 512
TABLE = S * EXPERTS

SLOTS = 4
SLOT = 2048

VECTORS = [("c", 8), ("c_ctx", 8), ("b_mod", 144), ("ln_g", 48), ("ln_b", 48), ("e_q_norm", 3), ("e_kv_norm", 2),
           ("o_b_pw1", 16), ("o_w_dw", 8 * TAPS), ("o_b_dw", 8), ("o_ln_g", 8), ("o_ln_b", 8), ("o_b_out", 8),
           ("norm1_g_2", 8), ("b_gla_a_2", 4), ("gla_out_norm_g_2", 1), ("dil_q_norm_g_2", 3),
           ("dil_k_norm_g_2", 3), ("b_branch_gate_2", 16), ("norm2_g_2", 8)]
COLUMN = {}
_at = 0
for _name, _rows in VECTORS:
    COLUMN[_name] = _at
    _at += _rows
NCOL = _at
COL_TILES = -(-NCOL // P)


class Core:

    def sem(self, name):
        s = self.nc.alloc_semaphore(name)
        self.stage_sems.append(s)
        return s

    def renew_semaphores(self):
        self.nc.clear_and_free_semaphores(self.stage_sems)
        self.nc.all_engine_barrier()
        self.stage_sems = []


class Extra:

    def __init__(self, layer, first, count, conds):
        self.layer, self.first, self.count, self.conds = layer, first, count, conds


FIRST_MOD = 12
MOD_IN_F00 = Extra(0, FIRST_MOD, 8, 2)
MOD_IN_F01 = Extra(1, 0, 12, 1)
CH = FG + 4


def extras_of(n, extra):
    if extra is None:
        return [0] * (n + 4)
    steps = n + 3
    each, more = divmod(extra.count, steps)
    return [each + (c < more) for c in range(steps)] + [0]


def group_loads(n, extra):
    order, q = [], 0
    for c, e in enumerate(extras_of(n, extra)):
        order += [("mod", q + x) for x in range(e)]
        q += e
        if n == FG or c + 2 < n + 4:
            order.append(("ffn", c + 2))
    return order


class WeightRing:

    def __init__(self, ring, landed):
        self.ring, self.landed = ring, landed
        self.sections, self.total, self.issued, self.taken, self.entered = [], 0, 0, 0, 0
        self.used = {}

    def plan(self, bodies, tail, source, per=SLOTS):
        self.sections.append((self.total, per, bodies, tail, source))
        self.total += per * bodies + tail

    def _load(self, sp, n, i, r):
        base, per, _, _, source = self.sections[n]
        slot = (base + r) % SLOTS
        if not isinstance(i, int):
            sem, value = self.used[n](i, r - SLOTS) if r >= SLOTS else self.used[n](i - 1, r - SLOTS + per)
            sp.wait_ge(sem, value)
        elif base + per * i + r >= SLOTS:
            before = base + per * i + r - SLOTS
            m = max(j for j, sec in enumerate(self.sections) if sec[0] <= before)
            at = before - self.sections[m][0]
            sem, value = self.used[m](at // self.sections[m][1], at % self.sections[m][1])
            sp.wait_ge(sem, value)
        view, src = source(self.ring[:, slot, :], i, r)
        sp.dma_start(view, src).then_inc(self.landed[slot], 16)

    def issue(self, sp, upto):
        upto = min(upto, self.total)
        for n, (base, per, bodies, tail, _) in enumerate(self.sections):
            size = per * bodies + tail
            at = self.issued - base
            end = min(upto - base, size)
            if at < 0 or end <= at:
                continue
            while at < end and (at % per or at >= per * bodies or at < per):
                self._load(sp, n, at // per, at % per)
                at += 1
            b0, b1 = at // per, min(end // per, bodies)
            if b1 - b0 >= 2:
                with sp.Fori(b0, b1) as i:
                    for r in range(per):
                        self._load(sp, n, i, r)
                at = per * b1
            while at < end:
                self._load(sp, n, at // per, at % per)
                at += 1
            self.issued = base + at

    def ahead(self, sp, *used):
        for fn in used:
            self.used[self.entered] = fn
            self.entered += 1
        base, per, bodies, tail, _ = self.sections[self.entered - 1]
        self.issue(sp, base + per * bodies + tail + SLOTS)

    def take(self, eng):
        g = self.taken
        self.taken += 1
        eng.wait_ge(self.landed[g % SLOTS], 16 * (g // SLOTS + 1))
        return self.ring[:, g % SLOTS, :]

    def take_in_loop(self, eng, i, r, per=SLOTS):
        g = self.taken + r
        eng.wait_ge(self.landed[g % SLOTS], (16 * per // SLOTS) * i + 16 * (g // SLOTS + 1))
        return self.ring[:, g % SLOTS, :]

    def slot(self, r):
        return self.ring[:, (self.taken + r) % SLOTS, :]

    def skip(self, n):
        self.taken += n


def wide(view, n=256, k=KD):
    return view[:, 0:k * n].rearrange("p (k n) -> p k n", k=k)


def rows_of(w, k=KD):
    return w.rearrange("(k p) n -> p k n", p=P)


def span(at, n):
    return slice(at, at + n) if isinstance(at, int) else bass.ds(at, n)


def sweep(w, cols=256):
    def source(view, i, r):
        n = w.shape[1]
        if isinstance(i, int):
            at = (SLOTS * i + r) * cols
            width = min(cols, n - at)
            return wide(view, width, w.shape[0] // P), rows_of(w)[:, :, at:at + width]
        return wide(view, cols, w.shape[0] // P), rows_of(w)[:, :, bass.ds(i * (SLOTS * cols) + r * cols, cols)]
    return source


def half_rows(w, at):
    def source(view, i, r):
        return wide(view, 512, 4), w.rearrange("(k p) n -> p k n", p=P)[:, 4 * r:4 * r + 4, at:at + 512]
    return source


def plan_weights(k):
    a, w = k.a, k.weights
    w.plan(FIRST_MOD // SLOTS, 0, sweep(a["w_mod"][0]))

    def ffn_plan(l, s, extra=None):
        w13, w2 = a["ffn_w13"][l, s], a["ffn_w2"][l, s]

        def chunk(view, i, c, n):
            f = i * FG
            if c < n or c >= CH:
                c, f = (c - CH, f + FG) if c >= CH else (c, f)
                return wide(view), rows_of(w13)[:, :, span(f * P + ((c // 2) * 256 + (c % 2) * FF), 256)]
            return wide(view, 256, n), rows_of(w2)[:, span(f, n), (c - n) * 256:(c - n) * 256 + 256]

        def group(first, n):
            order = group_loads(n, extra)

            def source(view, i, r):
                what, at = order[r]
                if what == "mod":
                    return wide(view), rows_of(a["w_mod"][extra.layer])[:, :, span((i + first) * (extra.count * 256) + (extra.first + at) * 256, 256)]
                return chunk(view, i + first, at, n)
            return source
        w.plan(0, 2, lambda view, i, r: chunk(view, 0, r, FG))
        w.plan(FGS, 0, group(0, FG), per=len(group_loads(FG, extra)))
        w.plan(0, len(group_loads(FREST, extra)), group(FGS, FREST), per=2 * len(group_loads(FG, extra)))

    ffn_plan(0, 0, MOD_IN_F00)
    w_in = a["e_w_in"][0]
    w.plan(0, 3, sweep(w_in[:, 0:672]))
    w.plan(0, 2, sweep(w_in[:, 672:1184]))
    w.plan(0, 2, half_rows(w_in, 1184))

    def q_up(view, i, r):
        return wide(view, 384, 3), a["e_w_q_up"][0].rearrange("(k p) n -> p k n", p=P)[:, :, 384 * r:384 * r + 384]

    def kv_up(view, i, r):
        return wide(view, 1024, 2), a["e_w_kv_up"][0].rearrange("(k p) n -> p k n", p=P)
    w.plan(0, 2, q_up)
    w.plan(0, 1, kv_up)
    w.plan(0, 4, sweep(a["e_w_out"][0]))
    ffn_plan(0, 1, MOD_IN_F01)
    ffn_plan(1, 0)
    pw1 = a["o_w_pw1"][0]

    def pw(view, i, r):
        at = (1 - r % 2) * D + (r // 2) * 256 + i * 512
        return wide(view), rows_of(pw1)[:, :, at:at + 256]
    w.plan(2, 0, pw)
    w.plan(0, 4, sweep(a["o_w_out"][0]))
    ffn_plan(1, 1)
    w2_in = a["w_in_2"][0]
    w.plan(0, 4, sweep(w2_in[:, 0:1024]))
    w.plan(0, 2, half_rows(w2_in, 1024))
    w.plan(0, 3, sweep(w2_in[:, 1536:2064]))
    for g in range(GROUPS):
        w.plan(0, 4, sweep(w2_in[:, 2064 + 1536 * g:2064 + 1536 * g + 1024]))
        w.plan(0, 2, half_rows(w2_in, 2064 + 1536 * g + 1024))

    def merge(view, i, r):
        if r < 2:
            return wide(view), rows_of(a["w_branch_gate_2"][0])[:, :, span(i * 256 + D * r, 256)]
        src = a["w_proj_gla_2"][0] if r == 2 else a["w_proj_attn_2"][0]
        return wide(view, 256, 4), rows_of(src)[:, :, span(i * 256, 256)]
    w.plan(4, 0, merge)
    w.plan(0, 4, sweep(a["w_out_2"][0]))


def load_stage(k):
    nc, a = k.nc, k.a
    with ExitStack() as st:
        rows = st.enter_context(nc.sbuf_tensor("token_rows", [P, T0 // P, D], F32))
        vec = st.enter_context(nc.sbuf_tensor("vector_rows", [P, COL_TILES, P], F32))
        sem = lambda n: k.sem(n)
        s_tok, s_vec, s_con, s_tp, s_cp = sem("ld_tokens"), sem("ld_vectors"), sem("ld_consts"), sem("ld_transposed"), sem("ld_copied")
        s_ms, s_z = sem("ld_memset"), sem("ld_zeroed")
        tiles = [(t, 0) for t in range(T0 // P)]
        block = st.enter_context(nc.Block())

        @block.sync
        def _(sp):
            sp.dma_start(k.ident[:], k.a["k_ident"]).then_inc(s_con, 16)
            sp.dma_start(rows[:, 0:ST, :], a["x"][0].rearrange("(t p) d -> p t d", p=P)).then_inc(s_tok, 16)
            sp.dma_start(rows[:, ST:, :], a["ctx"][0].rearrange("(t p) d -> p t d", p=P)).then_inc(s_tok, 16)
            k.weights.issue(sp, SLOTS)

        @block.scalar
        def _(act):
            act.wait_ge(s_z, 1)
            n = 0
            for name, count in VECTORS:
                src = k.flat[name]
                done = 0
                while done < count:
                    row = COLUMN[name] + done
                    m = min(P - row % P, count - done)
                    act.dma_start(vec[row % P:row % P + m, row // P, :], src[done:done + m, :]).then_inc(s_vec, 16)
                    done += m
                    n += 1
            k.n_vec = n
            for j in range(T0 // P * 2):
                act.wait_ge(s_tp, j + 1)
                t, h = divmod(j, 2)
                ins = act.activation(k.X[:, 4 * h:4 * h + 4, t * P:(t + 1) * P],
                                     k.PS[j % 4][:, 0:512].rearrange("p (a b) -> p a b", a=4), ACT.Copy)
                ins.then_inc(s_cp, 1)

        @block.gpsimd
        def _(pool):
            pool.memset(vec[:, COL_TILES - 1, :], 0.0).then_inc(s_z, 1)
            pool.memset(k.ones[:], 1.0).then_inc(s_ms, 1)
            pool.memset(k.rms_eps[:], RMS_EPS).then_inc(s_ms, 1)

        @block.tensor
        def _(pe):
            pe.wait_ge(s_con, 16)
            pe.wait_ge(s_tok, 32)
            for j in range(T0 // P * 2):
                if j >= 4:
                    pe.wait_ge(s_cp, j - 3)
                t, h = divmod(j, 2)
                for c in range(4):
                    ins = pe.transpose(k.PS[j % 4][:, c * P:(c + 1) * P], rows[:, t, (4 * h + c) * P:(4 * h + c + 1) * P], k.ident[:])
                ins.then_inc(s_tp, 1)
            pe.wait_ge(s_vec, 16 * k.n_vec)
            pe.wait_ge(s_cp, 2 * (T0 // P))
            for c in range(COL_TILES):
                ins = pe.transpose(k.PS[c // 4][:, (c % 4) * P:(c % 4 + 1) * P], vec[:, c, :], k.ident[:])
            ins.then_inc(s_tp, 1)

        @block.vector
        def _(dve):
            dve.wait_ge(s_tp, 2 * (T0 // P) + 1)
            dve.tensor_copy(k.col[:, 0:512], k.PS[0][:, 0:512]).then_inc(s_ms, 1)
            dve.tensor_copy(k.col[:, 512:COL_TILES * P], k.PS[1][:, 0:COL_TILES * P - 512]).then_inc(s_ms, 1)
            dve.wait_ge(s_ms, 4)


def chained(eng, s, n, ins):
    ins.then_inc(s, 1)
    n[0] += 1
    eng.wait_ge(s, n[0])


def finish_modulation(dve, link, mod, cols, b_mod, first, last, conds):
    for w in range(conds):
        link(dve.tensor_tensor(mod[:, w, 8 * first:8 * last], cols[:, 8 * first:8 * last, w], b_mod[:, 8 * first:8 * last], ALU.add))
    for idx in range(first, last):
        x = mod[:, 0:conds, 8 * idx:8 * idx + 8]
        if idx in (1, 4, 7):
            link(dve.tensor_scalar(x, x, 1.0, None, ALU.add))
        if idx in (2, 8):
            link(dve.tensor_scalar(x, x, 0.5, None, ALU.mult))


def first_modulation(k):
    nc = k.nc
    with ExitStack() as st:
        sem = lambda n: k.sem(f"ada_{n}")
        s_c, s_done, s_row, s_cols, s_ch = sem("silu"), sem("products"), sem("rows"), sem("columns"), sem("chain")
        rows = st.enter_context(nc.sbuf_tensor("ada_rows", [2, SLOTS, 256], F32))
        block = st.enter_context(nc.Block())
        cols = k.PS[2][:, 0:144].rearrange("p (m w) -> p m w", w=2)
        bank = lambda r: k.PS[r // 2][0:2, 512 * (r % 2):512 * (r % 2) + 256]

        @block.sync
        def _(sp):
            k.weights.ahead(sp, lambda i, r: (s_done, i * SLOTS + (r + 1)))

        @block.scalar
        def _(act):
            act.activation(k.cond[:], k.col[:, 0:16].rearrange("p (w k) -> p w k", w=2), ACT.Silu).then_inc(s_c, 1)
            act.sem_inc(s_cols, SLOTS)
            with act.Fori(0, FIRST_MOD // SLOTS) as i:
                for r in range(SLOTS):
                    act.wait_ge(s_done, i * SLOTS + (r + 1))
                    act.wait_ge(s_cols, i * SLOTS + (r + 1))
                    act.activation(rows[:, r, :], bank(r), ACT.Copy).then_inc(s_row, 1)

        @block.tensor
        def _(pe):
            def turn(i, r):
                pe.wait_ge(s_row, i * SLOTS + (r + 1))
                for m in range(2):
                    ins = pe.matmul(cols[:, bass.ds(i * 8 + (2 * r + m), 1), :], rows[:, r, m * P:(m + 1) * P],
                                    k.ident[0:2, 0:2], start=True, stop=True)
                ins.then_inc(s_cols, 1)
            pe.wait_ge(s_c, 1)
            with pe.Fori(0, FIRST_MOD // SLOTS) as i:
                for r in range(SLOTS):
                    w = wide(k.weights.take_in_loop(pe, i, r))
                    for kk in range(KD):
                        ins = pe.matmul(bank(r), k.cond[:, :, kk], w[:, kk, :], start=kk == 0, stop=kk == KD - 1)
                    ins.then_inc(s_done, 1)
                    if r:
                        turn(i, r - 1)
                turn(i, SLOTS - 1)
            k.weights.skip(FIRST_MOD)

        @block.vector
        def _(dve):
            n = [0]
            dve.wait_ge(s_cols, FIRST_MOD + SLOTS)
            finish_modulation(dve, lambda ins: chained(dve, s_ch, n, ins), k.mod[0], cols, k.b_mod(0), 0, FIRST_MOD // 4, 2)


def modulate_steps(eng, out, x, mod, idx, segments, wait, done):
    for kk in range(KD):
        wait(kk)
        for which, at, n in segments:
            j = 24 * idx + kk
            ins = eng.tensor_scalar(out[:, kk, at:at + n], x[:, kk, at:at + n], mod[:, which, j + 8:j + 9],
                                    mod[:, which, j:j + 1], ALU.mult, ALU.add)
        if done is not None:
            ins.then_inc(done, 1)


def split_product(pe, bank, w_hi, w_lo, x_hi, x_lo, halves, start, stop):
    passes = ((w_hi, x_hi), (w_hi, x_lo), (w_lo, x_hi))
    for n, (w, x) in enumerate(passes):
        for at, width in halves:
            ins = pe.matmul(bank[:, at:at + width], w, x[:, at:at + width],
                            start=start and n == 0, stop=stop and n == len(passes) - 1)
    return ins


def ffn_stage(k, name, l, s, idx, segments, extra=None):
    nc, W = k.nc, k.weights
    T = sum(n for _, _, n in segments)
    halves = [(0, 512)] + ([(512, T - 512)] if T > 512 else [])
    mod = k.mod[l]
    per = len(group_loads(FG, extra))
    assert per % SLOTS == 0 and FREST >= 4
    with ExitStack() as st:
        sb = lambda n, shape, dt: st.enter_context(nc.sbuf_tensor(f"{name}_{n}", shape, dt))
        h_hi, h_lo = sb("h_hi", [P, KD, T], F32R), sb("h_lo", [P, KD, T], F32R)
        f_hi, f_lo = sb("hidden_hi", [P, FG, T], F32R), sb("hidden_lo", [P, FG, T], F32R)
        w_hi, w_lo = sb("weights_hi", [P, 2, SLOT], F32R), sb("weights_lo", [P, 2, SLOT], F32R)
        tmp = sb("swiglu", [P, 2, T], F32)
        sem = lambda n: k.sem(f"{name}_{n}")
        s_hi, s_lo, s_mod, s_xhi, s_xlo, s_tile, s_silu, s_mul, s_fhi, s_flo, s_scaled, s_add = (
            sem("weights_hi"), sem("weights_lo"), sem("modulated"), sem("h_hi"), sem("h_lo"), sem("tiles"), sem("silu"), sem("product"),
            sem("hidden_hi"), sem("hidden_lo"), sem("scaled"), sem("added"))
        s_acc, s_col, s_ch = sem("modulation_sums"), sem("modulation_columns"), sem("chain")
        A, conds = (extra.count, extra.conds) if extra else (0, 0)
        if extra:
            slots = 4 // conds
            acc = sb("modulation_acc", [P, slots, conds, 256], F32)
        cols = k.PS[3][:, T0:T0 + 144].rearrange("p (m w) -> p m w", w=2)
        block = st.enter_context(nc.Block())
        G, U, Y = k.PS[0:2], k.PS[2:4], k.PS[0:2]
        CREDIT = 2

        @block.sync
        def _(sp):
            def used(first, n):
                def of_load(i, r):
                    what, at = group_loads(n, extra)[r]
                    if what == "mod":
                        return s_acc, (i + first) * (A * KD * conds) + (at + 1) * KD * conds
                    return s_lo, (i + first) * CH + (at + 1)
                return of_load
            W.ahead(sp, lambda i, r: (s_lo, r + 1), used(0, FG), used(FGS, FREST))

        @block.gpsimd
        def _(pool):
            pool.wait_ge(s_mod, KD)
            for kk in range(KD):
                ins = pool.tensor_scalar(k.X[:, kk, 0:T], k.X[:, kk, 0:T], ALPHA, 0.0, ALU.mult, ALU.add)
            ins.then_inc(s_scaled, 1)

        @block.tensor
        def _(pe):
            def group(i, n):
                for c in range(n + 4):
                    pe.wait_ge(s_lo, i * CH + (c + 1))
                    rows = KD if c < n else n
                    hi, lo = wide(w_hi[:, c % 2, :], 256, rows), wide(w_lo[:, c % 2, :], 256, rows)
                    x_hi, x_lo = (h_hi, h_lo) if c < n else (f_hi, f_lo)
                    bank = (Y if c >= n else U if c % 2 else G)

                    def free(b):
                        f = 2 * (c // 2) + b
                        m = 2 * (c - n) + b
                        if c >= n and m < 2:
                            pe.wait_ge(s_silu, i * FG + (n - 1 + b))
                        elif c >= n or (c % 2 == 0 and f < 2):
                            pe.wait_ge(s_add, i * KD + ((m if c >= n else f) - 1 + CREDIT))
                        elif c % 2 == 0:
                            pe.wait_ge(s_silu, i * FG + (f - 1))
                        elif f >= 2:
                            pe.wait_ge(s_mul, i * FG + (f - 1))

                    def step(b, kk):
                        return split_product(pe, bank[b], hi[:, kk, b * P:(b + 1) * P], lo[:, kk, b * P:(b + 1) * P],
                                             x_hi[:, kk, :], x_lo[:, kk, :], halves, kk == 0, kk == rows - 1)
                    if c in (0, n):
                        free(0)
                        free(1)
                        for kk in range(rows):
                            if c == 0:
                                pe.wait_ge(s_xlo, kk + 1)
                            else:
                                pe.wait_ge(s_flo, i * FG + (kk + 1))
                            for b in range(2):
                                ins = step(b, kk)
                                if kk == rows - 1:
                                    ins.then_inc(s_tile, 1)
                    else:
                        for b in range(2):
                            free(b)
                            for kk in range(rows):
                                ins = step(b, kk)
                            ins.then_inc(s_tile, 1)
                    if c >= n:
                        columns(i, n, range(c - 2 if c == n else c - 1, c))
                    elif c and c % 2 == 0:
                        pe.wait_ge(s_mul, i * FG + c)
                        columns(i, n, range(c - 2, c))

            def columns(i, n, steps):
                before = sum(extras_of(n, extra)[:steps[0]])
                for q in range(before, before + sum(extras_of(n, extra)[c] for c in steps)):
                    pe.wait_ge(s_acc, i * (A * KD * conds) + (q + 1) * KD * conds)
                    for half in range(2):
                        j = i * (2 * A) + (2 * (extra.first + q) + half)
                        for w in range(conds):
                            out = cols[:, j:j + 1, w] if isinstance(j, int) else cols[:, bass.ds(j, 1), w]
                            ins = pe.matmul(out, acc[:, q % slots, w, half * P:(half + 1) * P], k.ones[:, 0:1], start=True, stop=True)
                    ins.then_inc(s_col, 1)
            with pe.Fori(0, FGS) as i:
                group(i, FG)
            group(FGS, FREST)

        @block.scalar
        def _(act):
            def chunk_hi(i, c, n):
                rows = KD if c < n or c >= CH else n
                raw = W.take_in_loop(act, i, 2 + group_loads(n, extra).index(("ffn", c)) if c > 1 or i else c, per)
                act.activation(w_hi[:, c % 2, 0:rows * 256], raw[:, 0:rows * 256], ACT.Copy).then_inc(s_hi, 1)

            def group(i, n, last=False):
                for c in range(n + 4):
                    if c < n:
                        for b in range(2):
                            f = 2 * (c // 2) + b
                            if c % 2 == 0:
                                act.wait_ge(s_tile, i * (2 * CH) + (2 * c + b + 1))
                                if f >= 2:
                                    act.wait_ge(s_flo, i * FG + (f - 1))
                                act.activation(tmp[:, b, :], G[b][:, 0:T], ACT.Silu).then_inc(s_silu, 1)
                            else:
                                act.wait_ge(s_mul, i * FG + (f + 1))
                                act.activation(f_hi[:, f, :], tmp[:, b, :], ACT.Copy).then_inc(s_fhi, 1)
                    if not last or c + 2 < n + 4:
                        act.wait_ge(s_tile, i * (2 * CH) + (2 * c + 2))
                        chunk_hi(i, c + 2, n)
            chunk_hi(0, 0, FG)
            for kk in range(KD):
                act.wait_ge(s_mod, kk + 1)
                act.activation(h_hi[:, kk, :], tmp[:, kk % 2, :], ACT.Copy).then_inc(s_xhi, 1)
            chunk_hi(0, 1, FG)
            with act.Fori(0, FGS) as i:
                group(i, FG)
            group(FGS, FREST, last=True)

        @block.vector
        def _(dve):
            def chunk_lo(i, c, n):
                rows = KD if c < n or c >= CH else n
                dve.wait_ge(s_hi, i * CH + (c + 1))
                raw = W.slot(2 + group_loads(n, extra).index(("ffn", c)) if c > 1 else c)
                dve.tensor_tensor(w_lo[:, c % 2, 0:rows * 256], raw[:, 0:rows * 256],
                                  w_hi[:, c % 2, 0:rows * 256].bitcast(F32), ALU.subtract).then_inc(s_lo, 1)

            def group(i, n, last=False):
                for c in range(n + 4):
                    for b in range(2):
                        f, m = 2 * (c // 2) + b, 2 * (c - n) + b
                        if c >= n:
                            dve.wait_ge(s_tile, i * (2 * CH) + (2 * c + b + 1))
                            for which, at, width in segments:
                                j = 24 * idx + 16 + m
                                ins = dve.scalar_tensor_tensor(k.X[:, m, at:at + width], Y[b][:, at:at + width], mod[:, which, j:j + 1],
                                                               k.X[:, m, at:at + width], ALU.mult, ALU.add)
                            ins.then_inc(s_add, 1)
                        elif c % 2:
                            dve.wait_ge(s_silu, i * FG + (f + 1))
                            dve.wait_ge(s_tile, i * (2 * CH) + (2 * c + b + 1))
                            dve.tensor_tensor(tmp[:, b, :], tmp[:, b, :], U[b][:, 0:T], ALU.mult).then_inc(s_mul, 1)
                            dve.wait_ge(s_fhi, i * FG + (f + 1))
                            dve.tensor_tensor(f_lo[:, f, :], tmp[:, b, :], f_hi[:, f, :].bitcast(F32), ALU.subtract).then_inc(s_flo, 1)
                    before = sum(extras_of(n, extra)[:c])
                    for q in range(before, before + extras_of(n, extra)[c]):
                        modulation(i, n, q)
                    if not last or c + 2 < n + 4:
                        chunk_lo(i, c + 2, n)

            def modulation(i, n, q):
                w = wide(W.take_in_loop(dve, i, 2 + group_loads(n, extra).index(("mod", q)), per))
                done = i * (A * KD * conds) + q * KD * conds
                if q >= slots:
                    dve.wait_ge(s_col, i * A + (q - slots + 1))
                for kk in range(KD):
                    for x in range(conds):
                        out = acc[:, q % slots, x, :]
                        if kk == 0:
                            ins = dve.tensor_scalar(out, w[:, kk, :], k.cond[:, x, kk:kk + 1], None, ALU.mult)
                        else:
                            dve.wait_ge(s_acc, done + ((kk - 1) * conds + x + 1))
                            ins = dve.scalar_tensor_tensor(out, w[:, kk, :], k.cond[:, x, kk:kk + 1], out, ALU.mult, ALU.add)
                        ins.then_inc(s_acc, 1)
            dve.sem_inc(s_add, CREDIT)

            def modulated(kk):
                if kk >= 2:
                    dve.wait_ge(s_xlo, kk - 1)
                for which, at, width in segments:
                    j = 24 * idx + kk
                    ins = dve.tensor_scalar(tmp[:, kk % 2, at:at + width], k.X[:, kk, at:at + width], mod[:, which, j + 8:j + 9],
                                            mod[:, which, j:j + 1], ALU.mult, ALU.add)
                ins.then_inc(s_mod, 1)
            modulated(0)
            chunk_lo(0, 0, FG)
            for kk in range(KD):
                if kk + 1 < KD:
                    modulated(kk + 1)
                dve.wait_ge(s_xhi, kk + 1)
                dve.tensor_tensor(h_lo[:, kk, :], tmp[:, kk % 2, :], h_hi[:, kk, :].bitcast(F32), ALU.subtract).then_inc(s_xlo, 1)
            chunk_lo(0, 1, FG)
            dve.wait_ge(s_scaled, 1)
            with dve.Fori(0, FGS) as i:
                group(i, FG)
            group(FGS, FREST, last=True)
            if extra:
                dve.wait_ge(s_col, (FGS + 1) * A)
                n = [0]
                finish_modulation(dve, lambda ins: chained(dve, s_ch, n, ins), k.mod[extra.layer], cols, k.b_mod(extra.layer),
                                  extra.first // 4, 9, conds)
        W.skip(2 + FGS * per + len(group_loads(FREST, extra)))


def norm_stage(k, name, X, T, tiles, width, eps, gain, shift=None, center=True, out=None, func=None, then=None):
    nc = k.nc
    out = X if out is None else out
    halves = [(0, min(T, 512))] + ([(512, T - 512)] if T > 512 else [])
    with ExitStack() as st:
        sq = st.enter_context(nc.sbuf_tensor(f"{name}_sq", [P, 2, T], F32))
        rstd = st.enter_context(nc.sbuf_tensor(f"{name}_rstd", [P, T], F32))
        sem = lambda n: k.sem(f"{name}_{n}")
        s_mean, s_cen, s_sq, s_var, s_rs, s_root, s_nrm, s_out, s_h = (
            sem("mean"), sem("centred"), sem("squared"), sem("var"), sem("rs"), sem("root"), sem("scaled"), sem("out"), sem("h"))
        block = st.enter_context(nc.Block())
        MU, VAR = k.PS[0], k.PS[1]

        @block.tensor
        def _(pe):
            if center:
                for kk in range(tiles):
                    for at, n in halves:
                        ins = pe.matmul(MU[:, at:at + n], k.ones[:], X[:, kk, at:at + n], start=kk == 0, stop=kk == tiles - 1)
                ins.then_inc(s_mean, 1)
            for kk in range(tiles):
                pe.wait_ge(s_sq, kk + 1)
                for at, n in halves:
                    ins = pe.matmul(VAR[:, at:at + n], k.ones[:], sq[:, kk % 2, at:at + n], start=kk == 0, stop=kk == tiles - 1)
                ins.then_inc(s_var, 1)

        @block.scalar
        def _(act):
            for kk in range(tiles):
                if center:
                    act.wait_ge(s_cen, kk + 1)
                if kk >= 2:
                    act.wait_ge(s_var, kk - 1)
                act.activation(sq[:, kk % 2, :], X[:, kk, 0:T], ACT.Square).then_inc(s_sq, 1)
            act.wait_ge(s_rs, 1)
            act.activation(rstd[:], rstd[:], ACT.Ln).then_inc(s_root, 1)
            act.wait_ge(s_root, 1)
            act.activation(rstd[:], rstd[:], ACT.Exp, scale=-0.5).then_inc(s_root, 1)
            for kk in range(tiles):
                act.wait_ge(s_nrm, kk + 1)
                act.activation(out[:, kk, 0:T], out[:, kk, 0:T], func or ACT.Identity, scale=gain(kk),
                               bias=shift(kk) if shift else 0.0).then_inc(s_out, 1)

        @block.vector
        def _(dve):
            if center:
                dve.wait_ge(s_mean, 1)
                for kk in range(tiles):
                    dve.scalar_tensor_tensor(X[:, kk, 0:T], MU[:, 0:T], -1.0 / width, X[:, kk, 0:T],
                                             ALU.mult, ALU.add).then_inc(s_cen, 1)
            dve.wait_ge(s_var, tiles)
            dve.tensor_scalar(rstd[:], VAR[:, 0:T], 1.0 / width, eps, ALU.mult, ALU.add).then_inc(s_rs, 1)
            dve.wait_ge(s_root, 2)
            if center:
                dve.wait_ge(s_cen, tiles)
            for kk in range(tiles):
                dve.tensor_tensor(out[:, kk, 0:T], X[:, kk, 0:T], rstd[:], ALU.mult).then_inc(s_nrm, 1)

        if then is not None:
            @block.gpsimd
            def _(pool):
                l, idx, segments = then
                modulate_steps(pool, k.H, out, k.mod[l], idx, segments, lambda kk: pool.wait_ge(s_out, kk + 1), s_h)
                pool.wait_ge(s_h, KD)


class Job:

    def __init__(self, pe, act=None, dve=None, chunk=None):
        self.pe, self.act, self.dve, self.chunk = pe, act, dve, chunk


class Parts:

    def __init__(self, k, st, name, *sources):
        sb = lambda n, shape: st.enter_context(k.nc.sbuf_tensor(f"{name}_{n}", shape, F32R))
        self.w_hi, self.w_lo = sb("w_hi", [P, 2, SLOT]), sb("w_lo", [P, 2, SLOT])
        self.tiles, self.rhs, self.rows = [], [], []
        for n, (x, kt) in enumerate(sources):
            hi, lo = sb(f"x{n}_hi", [P, kt, S]), sb(f"x{n}_lo", [P, kt, S])
            self.rhs.append((hi, lo, len(self.tiles)))
            for kk in range(kt):
                if len(x.shape) == 4:
                    halves = lambda part: part[:, kk, :].rearrange("p (u t) -> p u t", u=2)
                    self.tiles.append((x[:, kk, :, :], halves(hi), halves(lo)))
                else:
                    self.tiles.append((x[:, kk, 0:S], hi[:, kk, :], lo[:, kk, :]))

    def chunk(self, kt=KD):
        self.rows.append(kt)
        return len(self.rows) - 1

    def product(self, chunk, m, source=0, first=False):
        x_hi, x_lo, at = self.rhs[source]
        kt = self.rows[chunk]
        hi, lo = (wide(w[:, chunk % 2, :], 256, kt) for w in (self.w_hi, self.w_lo))

        def pe_part(pe, bank, s):
            pe.wait_ge(s.w_lo, chunk + 1)
            for kk in range(kt):
                if first:
                    pe.wait_ge(s.x_lo, at + kk + 1)
                ins = split_product(pe, bank, hi[:, kk, m * P:(m + 1) * P], lo[:, kk, m * P:(m + 1) * P],
                                    x_hi[:, kk, :], x_lo[:, kk, :], [(0, S)], kk == 0, kk == kt - 1)
            return ins
        return pe_part


def product_stage(k, name, jobs, used=(), pool=None, dve_first=None, dve_last=None, loads=(), pe_needs_loads=True, parts=None):
    nc = k.nc
    banks = 4
    by_act = [j for j, job in enumerate(jobs) if job.act]
    by_dve = [j for j, job in enumerate(jobs) if job.dve]
    count = lambda js, j: sum(x <= j for x in js)
    chunks = len(parts.rows) if parts else 0
    last_of = [max(j for j, job in enumerate(jobs) if job.chunk == n) for n in range(chunks)]
    with ExitStack() as st:
        sem = lambda n: k.sem(f"{name}_{n}")
        s = Core()
        s.out, s.act, s.dve, s.chain, s.load, s.pool = (
            sem("products"), sem("act"), sem("dve"), sem("chain"), sem("load"), sem("pool"))
        if parts:
            s.x_hi, s.x_lo, s.w_hi, s.w_lo = sem("x_hi"), sem("x_lo"), sem("w_hi"), sem("w_lo")
            base = k.weights.taken
        s.n_chain, s.n_loads = [0], len(loads)
        s.link = lambda eng, ins: chained(eng, s.chain, s.n_chain, ins)
        s.acts_before = lambda j: count(by_act, j)
        s.dves_before = lambda j: count(by_dve, j)
        block = st.enter_context(nc.Block())

        def chunk_hi(act, n):
            raw = k.weights.take(act)
            if n >= 2:
                act.wait_ge(s.out, last_of[n - 2] + 1)
            size = 256 * parts.rows[n]
            act.activation(parts.w_hi[:, n % 2, 0:size], raw[:, 0:size], ACT.Copy).then_inc(s.w_hi, 1)

        def chunk_lo(dve, n):
            raw, size = k.weights.ring[:, (base + n) % SLOTS, :], 256 * parts.rows[n]
            dve.wait_ge(s.w_hi, n + 1)
            dve.tensor_tensor(parts.w_lo[:, n % 2, 0:size], raw[:, 0:size], parts.w_hi[:, n % 2, 0:size].bitcast(F32),
                              ALU.subtract).then_inc(s.w_lo, 1)

        def tiles_hi(act):
            for x, hi, _ in parts.tiles:
                act.activation(hi, x, ACT.Copy).then_inc(s.x_hi, 1)

        def tiles_lo(dve):
            for n, (x, hi, lo) in enumerate(parts.tiles):
                dve.wait_ge(s.x_hi, n + 1)
                dve.tensor_tensor(lo, x, hi.bitcast(F32), ALU.subtract).then_inc(s.x_lo, 1)

        def after(eng, part, j):
            for n in range(2, chunks):
                if last_of[n - 2] == j:
                    part(eng, n)

        @block.sync
        def _(sp):
            for dst, src in loads:
                sp.dma_start(dst, src).then_inc(s.load, 16)
            if parts:
                k.weights.ahead(sp, *[lambda i, r, at=at: (s.w_lo, at + SLOTS * i + r + 1) for at in used])
            elif used:
                k.weights.ahead(sp, *[(lambda i, r, u=u: (s.out, u[SLOTS * i + r])) for u in used])

        @block.tensor
        def _(pe):
            if loads and pe_needs_loads:
                pe.wait_ge(s.load, 16 * len(loads))
            for j, job in enumerate(jobs):
                if j >= banks:
                    if jobs[j - banks].dve:
                        pe.wait_ge(s.dve, count(by_dve, j - banks))
                    else:
                        pe.wait_ge(s.act, count(by_act, j - banks))
                job.pe(pe, k.PS[j % banks], s).then_inc(s.out, 1)

        @block.scalar
        def _(act):
            if parts:
                chunk_hi(act, 0)
                tiles_hi(act)
                chunk_hi(act, 1)
            for j, job in enumerate(jobs):
                if job.act:
                    act.wait_ge(s.out, j + 1)
                    job.act(act, k.PS[j % banks], s).then_inc(s.act, 1)
                after(act, chunk_hi, j)

        @block.vector
        def _(dve):
            if parts:
                chunk_lo(dve, 0)
                tiles_lo(dve)
                chunk_lo(dve, 1)
            if dve_first:
                dve_first(dve, s)
            for j, job in enumerate(jobs):
                if job.dve:
                    nth = count(by_dve, j) - 1
                    if nth >= 2:
                        dve.wait_ge(s.dve, nth - 1)
                    if job.act:
                        dve.wait_ge(s.act, count(by_act, j))
                    else:
                        dve.wait_ge(s.out, j + 1)
                    job.dve(dve, k.PS[j % banks], s).then_inc(s.dve, 1)
                after(dve, chunk_lo, j)
            if dve_last:
                dve.wait_ge(s.dve, len(by_dve))
                dve_last(dve, s)

        if pool:
            @block.gpsimd
            def _(gp):
                pool(gp, s)


def feature_product(k, rhs, segments, weights, rows=P, cols=0, kt=KD, at_row=0):
    def pe_part(pe, bank, s):
        w = weights(pe)
        for kk in range(kt):
            for at, n in segments:
                ins = pe.matmul(bank[at_row:at_row + rows, at:at + n], w[:, kk, cols:cols + rows], rhs[:, kk, at:at + n],
                                start=kk == 0, stop=kk == kt - 1)
        return ins
    return pe_part


def shared(k, shape=lambda w: wide(w)):
    got = []

    def weights(pe):
        if not got:
            got.append(shape(k.weights.take(pe)))
        return got[0]
    return weights


def token_product(k, lhs, t, halves, n=512):
    def pe_part(pe, bank, s):
        ws = [h(pe) for h in halves]
        for kk in range(KD):
            ins = pe.matmul(bank[:, 0:n], lhs[:, kk, t * P:(t + 1) * P], ws[kk // 4][:, kk % 4, 0:n],
                            start=kk == 0, stop=kk == KD - 1)
        return ins
    return pe_part


def residual_stage(k, name, rhs, gate, bias=None):
    with ExitStack() as st:
        parts = Parts(k, st, name, (rhs, KD))
        jobs = []
        for m in range(KD):
            if m % 2 == 0:
                w = parts.chunk()

            def add(dve, bank, s, m=m):
                if gate is None:
                    return dve.tensor_tensor(k.X[:, m, 0:S], bank[:, 0:S], k.X[:, m, 0:S], ALU.add)
                return dve.scalar_tensor_tensor(k.X[:, m, 0:S], bank[:, 0:S], gate(m), k.X[:, m, 0:S], ALU.mult, ALU.add)
            jobs.append(Job(parts.product(w, m % 2, first=m == 0), dve=add, chunk=w))

        def scale_x(pool, s):
            for kk in range(KD):
                ins = pool.tensor_scalar(k.X[:, kk, 0:S], k.X[:, kk, 0:S], ALPHA, 0.0 if bias is None else bias(kk), ALU.mult, ALU.add)
            ins.then_inc(s.pool, 1)
        needs_scaling = gate is not None
        product_stage(k, name, jobs, used=[0], parts=parts, pool=scale_x if needs_scaling else None,
                      dve_first=(lambda dve, s: dve.wait_ge(s.pool, 1)) if needs_scaling else None)


def even_mixer(k):
    nc, a = k.nc, k.a
    BOTH = [(0, S), (S, C)]
    with ExitStack() as st:
        sb = lambda n, shape: st.enter_context(nc.sbuf_tensor(n, shape, F32))
        AB = sb("AB", [P, KD, S])
        heads = ExitStack()
        sb = lambda n, shape: heads.enter_context(nc.sbuf_tensor(n, shape, F32))
        QT, KT = sb("QT", [P, HEADS, S]), sb("KT", [P, HEADS, T0])
        V = sb("V", [P, T0 // P, HEADS * VD])
        with ExitStack() as inner:
            sb = lambda n, shape: inner.enter_context(nc.sbuf_tensor(n, shape, F32))
            CQ, CKV, KR = sb("CQ", [P, 3, S]), sb("CKV", [P, 2, T0]), sb("KR", [P, 1, T0])
            UT, VT = sb("UT", [P, 4, S]), sb("VT", [P, ST, BW])
            copy_to = lambda dst, n, lo=0, hi=P: lambda act, bank, s: act.activation(dst[lo:hi], bank[lo:hi, 0:n], ACT.Copy)
            w0, w1, w2 = (shared(k), shared(k), shared(k, lambda w: wide(w, 160)))
            jobs = [Job(feature_product(k, k.H, BOTH[:1], w0), act=copy_to(CQ[:, 0, :], S)),
                    Job(feature_product(k, k.H, BOTH[:1], w0, cols=P), act=copy_to(CQ[:, 1, :], S)),
                    Job(feature_product(k, k.H, BOTH[:1], w1), act=copy_to(CQ[:, 2, :], S)),
                    Job(feature_product(k, k.H, BOTH, w1, cols=P), act=copy_to(CKV[:, 0, :], T0)),
                    Job(feature_product(k, k.H, BOTH, w2), act=copy_to(CKV[:, 1, :], T0)),
                    Job(feature_product(k, k.H, BOTH, w2, rows=QK, cols=64), act=copy_to(KR[:, 0, :], T0, NOPE, QK))]
            for m in range(4):
                if m % 2 == 0:
                    w = shared(k)
                jobs.append(Job(feature_product(k, k.H, BOTH[:1], w, cols=(m % 2) * P),
                                act=lambda act, bank, s, m=m: act.activation(UT[:, m, :], bank[:, 0:S], ACT.Gelu)))
            halves = [shared(k, lambda w: wide(w, 512, 4)) for _ in range(2)]
            for t in range(ST):
                jobs.append(Job(token_product(k, k.H, t, halves),
                                act=lambda act, bank, s, t=t: act.activation(VT[:, t, :], bank[:, 0:BW], ACT.Gelu)))
            product_stage(k, "e_in", jobs, used=[[2, 4, 6], [8, 10], [14, 14]])
            norm_stage(k, "e_qn", CQ, S, 3, Q_RANK, RMS_EPS, norm_columns(k, "e_q_norm"), center=False)
            norm_stage(k, "e_kvn", CKV, T0, 2, KV_RANK, RMS_EPS, norm_columns(k, "e_kv_norm"), center=False)
            spatial_norm(k, VT)
            even_heads(k, QT, KT, V, AB, CQ, CKV, KR, UT, VT)
        latent_attention(k, QT, KT, V, AB)
        heads.close()
        residual_stage(k, "e_out", AB, lambda m: k.mod[0][:, 0, 40 + m:41 + m])


def spatial_norm(k, VT):
    nc, a = k.nc, k.a
    with ExitStack() as st:
        sb = lambda n, shape: st.enter_context(nc.sbuf_tensor(n, shape, F32))
        g, b, stats, mv, rs = sb("sgu_g", [P, BW]), sb("sgu_b", [P, BW]), sb("sgu_st", [P, ST, 6]), sb("sgu_mv", [P, ST, 2]), sb("sgu_rs", [P, ST])
        sem = lambda n: k.sem(f"sgu_{n}")
        s_ld, s_ch, s_sq = sem("load"), sem("chain"), sem("sqrt")
        block = st.enter_context(nc.Block())

        @block.sync
        def _(sp):
            sp.dma_start(g[:], a["e_sgu_g"].partition_broadcast(P)).then_inc(s_ld, 16)
            sp.dma_start(b[:], a["e_sgu_b"].partition_broadcast(P)).then_inc(s_ld, 16)

        @block.vector
        def _(dve):
            n = [0]
            for t in range(ST):
                ins = dve.bn_stats(stats[:, t, :], VT[:, t, :])
            chained(dve, s_ch, n, ins)
            for t in range(ST):
                ins = dve.bn_aggr(mv[:, t, :], stats[:, t, :])
            chained(dve, s_ch, n, ins)
            chained(dve, s_ch, n, dve.tensor_scalar(rs[:], mv[:, :, 1], LN_EPS, None, ALU.add))
            dve.wait_ge(s_sq, 1)
            chained(dve, s_ch, n, dve.reciprocal(rs[:], rs[:]))
            for t in range(ST):
                ins = dve.tensor_scalar(VT[:, t, :], VT[:, t, :], mv[:, t, 0:1], rs[:, t:t + 1], ALU.subtract, ALU.mult)
            chained(dve, s_ch, n, ins)
            dve.wait_ge(s_ld, 32)
            for t in range(ST):
                ins = dve.tensor_tensor(VT[:, t, :], VT[:, t, :], g[:], ALU.mult)
            chained(dve, s_ch, n, ins)
            for t in range(ST):
                ins = dve.tensor_tensor(VT[:, t, :], VT[:, t, :], b[:], ALU.add)
            chained(dve, s_ch, n, ins)

        @block.scalar
        def _(act):
            act.wait_ge(s_ch, 3)
            act.activation(rs[:], rs[:], ACT.Sqrt).then_inc(s_sq, 1)


def even_heads(k, QT, KT, V, AB, CQ, CKV, KR, UT, VT):
    nc, a = k.nc, k.a
    with ExitStack() as st:
        sb = lambda n, shape: st.enter_context(nc.sbuf_tensor(n, shape, F32))
        WS, WST, BS = sb("WS", [P, 4, P]), sb("WST", [P, 4, P]), sb("BS", [P, 4, P])
        rope, swap, t1 = sb("rope", [P, 2, S]), sb("swap", [P, QK]), sb("rot", [P, 2, S])
        loads = [(swap[0:QK, :], a["k_swap"]), (rope[0:QK, :, :], a["k_rope"].rearrange("w p t -> p w t")),
                 (WS[:], a["e_w_s"][0].rearrange("g i j -> i g j")),
                 (BS[:].rearrange("p g i -> p (g i)"), a["e_b_s"].rearrange("o g i -> o (g i)").partition_broadcast(P))]
        jobs = []

        def rotate(x, lo, hi, slot):
            def dve_part(dve, bank, s):
                s.link(dve, dve.tensor_tensor(t1[lo:hi, slot, :], bank[lo:hi, 0:S], rope[lo:hi, 1, :], ALU.mult))
                s.link(dve, dve.tensor_tensor(x, x, rope[lo:hi, 0, :], ALU.mult))
                return dve.tensor_tensor(x, x, t1[lo:hi, slot, :], ALU.add)
            return dve_part
        jobs.append(Job(lambda pe, bank, s: pe.matmul(bank[NOPE:QK, 0:S], swap[NOPE:QK, NOPE:QK], KR[NOPE:QK, 0, 0:S], start=True, stop=True),
                        dve=rotate(KR[NOPE:QK, 0, 0:S], NOPE, QK, 0)))
        wq = [shared(k, lambda w: wide(w, 384, 3)) for _ in range(2)]

        def swap_job(h):
            def pe_part(pe, bank, s):
                pe.wait_ge(s.act, h + 1)
                return pe.matmul(bank[0:QK, 0:S], swap[0:QK, :], QT[0:QK, h, :], start=True, stop=True)
            return Job(pe_part, dve=rotate(QT[0:QK, h, :], 0, QK, (h + 1) % 2))
        for h in range(HEADS):
            jobs.append(Job(feature_product(k, CQ, [(0, S)], wq[h // 4], rows=QK, cols=(h % 4) * QK, kt=3),
                            act=lambda act, bank, s, h=h: act.activation(QT[0:QK, h, :], bank[0:QK, 0:S], ACT.Copy)))
            if h == 4:
                after_first = len(jobs) - 1
            if h:
                jobs.append(swap_job(h - 1))
        after_q = len(jobs)
        jobs.append(swap_job(HEADS - 1))
        wkv = shared(k, lambda w: wide(w, 1024, 2))
        for h in range(HEADS):
            jobs.append(Job(feature_product(k, CKV, [(0, S), (S, C)], wkv, rows=NOPE, cols=h * P, kt=2),
                            act=lambda act, bank, s, h=h: act.activation(KT[0:NOPE, h, :], bank[0:NOPE, 0:T0], ACT.Copy)))
        for t in range(T0 // P):
            def values(pe, bank, s, t=t):
                w = wkv(pe).rearrange("p k (h c) -> p k h c", c=P)
                for kk in range(2):
                    ins = pe.matmul(bank[:, 0:512].rearrange("p (h c) -> p h c", c=VD), CKV[:, kk, t * P:(t + 1) * P], w[:, kk, :, NOPE:P],
                                    start=kk == 0, stop=kk == 1)
                return ins
            jobs.append(Job(values, dve=lambda dve, bank, s, t=t: dve.tensor_copy(V[:, t, :], bank[:, 0:512])))
        after_kv = len(jobs)

        def turn(pe, bank, s):
            for g in range(4):
                ins = pe.transpose(bank[:, g * P:(g + 1) * P], WS[:, g, :], k.ident[:])
            return ins
        jobs.append(Job(turn, act=lambda act, bank, s: act.activation(WST[:].rearrange("p g i -> p (g i)"), bank[:, 0:512], ACT.Copy)))
        turned = len(jobs)
        for c in range(ST):
            def mix(pe, bank, s, c=c):
                if c == 0:
                    pe.wait_ge(s.act, s.acts_before(turned))
                for g in range(4):
                    ins = pe.matmul(bank[:, g * P:(g + 1) * P], VT[:, c, g * P:(g + 1) * P], WST[:, g, :], start=True, stop=True)
                return ins

            def gated(dve, bank, s, c=c):
                m = t1[:, c % 2, :].rearrange("p (g i) -> p g i", g=4)
                s.link(dve, dve.tensor_tensor(m, bank[:, 0:512].rearrange("p (g i) -> p g i", g=4), BS[:], ALU.add))
                return dve.tensor_tensor(AB[:, 4:8, c * P:(c + 1) * P], m, UT[:, :, c * P:(c + 1) * P], ALU.mult)
            jobs.append(Job(mix, dve=gated))

        def spread(pool, s):
            pool.wait_ge(s.dve, 1)
            for h in range(HEADS):
                pool.tensor_copy(KT[NOPE:QK, h, :], KR[NOPE:QK, 0, :])
        product_stage(k, "e_heads", jobs, used=[[after_first, after_q], [after_kv]], loads=loads, pool=spread,
                      dve_first=lambda dve, s: dve.wait_ge(s.load, 16 * s.n_loads))


def latent_attention(k, QT, KT, V, AB):
    nc = k.nc
    NK = T0 // P
    with ExitStack() as st:
        sb = lambda n, shape: st.enter_context(nc.sbuf_tensor(n, shape, F32))
        PT = sb("PT", [P, 2, NK, S])
        mx, neg, rs, ri = sb("mx", [P, 8]), sb("neg", [P, 8]), sb("rs", [P, 8]), sb("ri", [P, 8])
        sem = lambda n: k.sem(f"att_{n}")
        s_sc, s_mx, s_nm, s_exp, s_ri, s_p, s_t, s_cv, s_ca, s_pv, s_o = (
            sem("scores"), sem("max"), sem("negmax"), sem("exp"), sem("rinv"), sem("probs"), sem("turned"),
            sem("copied_dve"), sem("copied_act"), sem("pv"), sem("out"))
        Pr = lambda n: k.H[:, 4 * ((n // 4) % 2) + n % 4, :]
        block = st.enter_context(nc.Block())
        T = lambda kt: k.PS[2][:, 512 * (kt % 2):512 * (kt % 2) + 512]
        O = lambda h: k.PS[3][:, 512 * (h // 2 % 2):512 * (h // 2 % 2) + 512]

        @block.tensor
        def _(pe):
            def scores(n):
                h, q = divmod(n, 4)
                if n >= 2:
                    pe.wait_ge(s_exp, n - 1)
                for at, w in ((0, S), (S, C)):
                    ins = pe.matmul(k.PS[n % 2][:, at:at + w], QT[0:QK, h, q * P:(q + 1) * P], KT[0:QK, h, at:at + w], start=True, stop=True)
                ins.then_inc(s_sc, 1)

            def turn(h, kt):
                if kt == 0:
                    pe.wait_ge(s_p, 4 * h + 4)
                n = NK * h + kt
                if n >= 2:
                    pe.wait_ge((s_cv, s_ca)[kt % 2], (n - 2) // 2 + 1)
                for q in range(4):
                    ins = pe.transpose(T(kt)[:, q * P:(q + 1) * P], Pr(4 * h + q)[:, kt * P:(kt + 1) * P], k.ident[:])
                ins.then_inc(s_t, 1)

            def pv(h, kt):
                pe.wait_ge((s_cv, s_ca)[kt % 2], (NK * h + kt) // 2 + 1)
                if kt == 0 and h % 2 == 0 and h >= 4:
                    pe.wait_ge(s_o, h // 2 - 1)
                r = VD * (h % 2)
                ins = pe.matmul(O(h)[r:r + VD, :], V[:, kt, h * VD:(h + 1) * VD], PT[:, h % 2, kt, :], start=kt == 0, stop=kt == NK - 1)
                if kt == NK - 1:
                    ins.then_inc(s_pv, 1)
            for q in range(4):
                scores(q)
            for h in range(HEADS):
                for kt in range(NK):
                    if kt < 4 and h + 1 < HEADS:
                        scores(4 * h + 4 + kt)
                    turn(h, kt)
                    if kt:
                        pv(h, kt - 1)
                pv(h, NK - 1)

        @block.vector
        def _(dve):
            def top(n):
                dve.wait_ge(s_sc, n + 1)
                dve.reduce_max(mx[:, n % 8:n % 8 + 1], k.PS[n % 2][:, 0:T0], AXX).then_inc(s_mx, 1)
                dve.wait_ge(s_mx, n + 1)
                if n >= 8:
                    dve.wait_ge(s_exp, n - 7)
                dve.tensor_scalar(neg[:, n % 8:n % 8 + 1], mx[:, n % 8:n % 8 + 1], -ATTN_SCALE, None, ALU.mult).then_inc(s_nm, 1)

            def norm(n):
                dve.wait_ge(s_exp, n + 1)
                dve.reciprocal(ri[:, n % 8:n % 8 + 1], rs[:, n % 8:n % 8 + 1]).then_inc(s_ri, 1)
                dve.wait_ge(s_ri, n + 1)
                dve.tensor_scalar(Pr(n), Pr(n), ri[:, n % 8:n % 8 + 1], None, ALU.mult).then_inc(s_p, 1)

            def copy(h, kt):
                n = NK * h + kt
                dve.wait_ge(s_t, n + 1)
                if h >= 2:
                    dve.wait_ge(s_pv, h - 1)
                dve.tensor_copy(PT[:, h % 2, kt, :], T(kt)).then_inc(s_cv, 1)
            for q in range(4):
                top(q)
                if q:
                    norm(q - 1)
            norm(3)
            for h in range(HEADS):
                for kt in range(NK):
                    if kt < 4 and h + 1 < HEADS:
                        top(4 * h + 4 + kt)
                    if kt % 2 == 0:
                        copy(h, kt)
                    if 1 <= kt < 5 and h + 1 < HEADS:
                        norm(4 * h + 3 + kt)

        @block.scalar
        def _(act):
            def expo(n):
                act.wait_ge(s_nm, n + 1)
                if n >= 8:
                    act.wait_ge(s_t, NK * ((n - 4) // 4))
                    act.wait_ge(s_ri, n - 7)
                act.activation(Pr(n), k.PS[n % 2][:, 0:T0], ACT.Exp, bias=neg[:, n % 8:n % 8 + 1], scale=ATTN_SCALE,
                               accum_out=rs[:, n % 8:n % 8 + 1]).then_inc(s_exp, 1)

            for q in range(4):
                expo(q)
            for h in range(HEADS):
                for kt in range(NK):
                    if kt < 4 and h + 1 < HEADS:
                        expo(4 * h + 4 + kt)
                    if kt % 2:
                        act.wait_ge(s_t, NK * h + kt + 1)
                        if h >= 2:
                            act.wait_ge(s_pv, h - 1)
                        act.activation(PT[:, h % 2, kt, :], T(kt), ACT.Copy).then_inc(s_ca, 1)
                if h % 2:
                    act.wait_ge(s_pv, h + 1)
                    act.activation(AB[:, h // 2, :], O(h), ACT.Copy).then_inc(s_o, 1)


def conv_mixer(k):
    nc, a = k.nc, k.a
    c = lambda name: norm_columns(k, name)
    b1, bdw, wdw = c("o_b_pw1"), c("o_b_dw"), c("o_w_dw")
    with ExitStack() as st:
        sb = lambda n, shape: st.enter_context(nc.sbuf_tensor(n, shape, F32))
        Y = sb("conv_in", [P, KD, S + 2 * PAD])
        sig = sb("conv_sig", [P, 2, S])
        with ExitStack() as inner:
            parts = Parts(k, inner, "c_in", (k.H, KD))
            jobs, gate_job = [], {}
            for c2 in range(4):
                w = parts.chunk()
                for m in (2 * c2, 2 * c2 + 1):
                    def gate(act, bank, s, m=m):
                        if m >= 2:
                            act.wait_ge(s.dve, m - 1)
                        return act.activation(sig[:, m % 2, :], bank[:, 0:S], ACT.Sigmoid, bias=b1(KD + m))
                    gate_job[m] = len(jobs)
                    jobs.append(Job(parts.product(w, m % 2, first=m == 0), act=gate, chunk=w))
                w = parts.chunk()
                for m in (2 * c2, 2 * c2 + 1):
                    def value(dve, bank, s, m=m):
                        dve.wait_ge(s.act, s.acts_before(gate_job[m]))
                        return dve.scalar_tensor_tensor(Y[:, m, PAD:PAD + S], bank[:, 0:S], b1(m), sig[:, m % 2, :], ALU.add, ALU.mult)
                    jobs.append(Job(parts.product(w, m % 2), dve=value, chunk=w))

            def edges(pool, s):
                pool.memset(Y[:, :, 0:PAD], 0.0)
                pool.memset(Y[:, :, PAD + S:], 0.0)
                for kk in range(KD):
                    ins = pool.tensor_tensor(k.cond2[:, kk:kk + 1], c("o_b_out")(kk), k.mod[1][:, 0, 40 + kk:41 + kk], ALU.mult)
            product_stage(k, "c_in", jobs, used=[0], pool=edges, parts=parts)
        depthwise(k, Y, wdw, bdw)
        norm_stage(k, "c_n", k.H, S, KD, D, LN_EPS, c("o_ln_g"), c("o_ln_b"), func=ACT.Silu)
        residual_stage(k, "c_out", k.H, lambda m: k.mod[1][:, 0, 40 + m:41 + m], bias=lambda kk: k.cond2[:, kk:kk + 1])


ON_PE = 13


def depthwise(k, Y, wdw, bdw):
    nc = k.nc
    with ExitStack() as st:
        sb = lambda n, shape: st.enter_context(nc.sbuf_tensor(n, shape, F32))
        diag = sb("diag", [P, 4, P])
        sem = lambda n: k.sem(f"dw_{n}")
        s_diag, s_tap, s_pe, s_acc, s_left = sem("diagonals"), sem("taps"), sem("summed"), sem("acc"), sem("left")
        block = st.enter_context(nc.Block())

        @block.scalar
        def _(act):
            for n in range(KD * ON_PE):
                m, w = divmod(n, ON_PE)
                if n >= 4:
                    act.wait_ge(s_tap, n - 3)
                act.activation(diag[:, n % 4, :], k.ident[:], ACT.Copy, scale=wdw(w * KD + m)).then_inc(s_diag, 1)

        @block.tensor
        def _(pe):
            for n in range(KD * ON_PE):
                m, w = divmod(n, ON_PE)
                if w == 0 and m >= 4:
                    pe.wait_ge(s_left, m - 3)
                pe.wait_ge(s_diag, n + 1)
                pe.matmul(k.PS[m % 4][:, 0:S], diag[:, n % 4, :], Y[:, m, w:w + S], start=w == 0, stop=w == ON_PE - 1).then_inc(s_tap, 1)

        @block.vector
        def _(dve):
            n = 0

            def step(ins):
                nonlocal n
                ins.then_inc(s_acc, 1)
                n += 1
            for m0 in range(0, KD, 2):
                for m in (m0, m0 + 1):
                    step(dve.tensor_scalar(k.H[:, m, 0:S], Y[:, m, ON_PE:ON_PE + S], wdw(ON_PE * KD + m), bdw(m), ALU.mult, ALU.add))
                for w in range(ON_PE + 1, TAPS):
                    for m in (m0, m0 + 1):
                        dve.wait_ge(s_acc, n - 1)
                        step(dve.scalar_tensor_tensor(k.H[:, m, 0:S], Y[:, m, w:w + S], wdw(w * KD + m), k.H[:, m, 0:S], ALU.mult, ALU.add))
                for m in (m0, m0 + 1):
                    dve.wait_ge(s_acc, n - 1 + m - m0)
                    dve.wait_ge(s_tap, (m + 1) * ON_PE)
                    dve.tensor_tensor(k.H[:, m, 0:S], k.PS[m % 4][:, 0:S], k.H[:, m, 0:S], ALU.add).then_inc(s_left, 1)


def second_block(k, out, stop):
    nc, a = k.nc, k.a
    c = lambda name: norm_columns(k, name)
    norm_stage(k, "s_n1", k.X, S, KD, D, 1e-6, c("norm1_g_2"), center=False, out=k.H)
    with ExitStack() as st:
        OG = st.enter_context(nc.sbuf_tensor("gla_out", [P, GH, S], F32))
        linear_attention(k, OG)
        if stop == 5:
            return stop_here(k)
        OA = k.X[:, :, S:].rearrange("p (h u) t -> p h u t", u=2)
        with ExitStack() as inner:
            sb = lambda n, shape: inner.enter_context(nc.sbuf_tensor(n, shape, F32))
            dil = dict(q=sb("dil_q", [P, GROUPS, GH, S]), k=sb("dil_k", [P, GROUPS, GH, S]), v=sb("dil_v", [P, GROUPS, ST, S]),
                       bias=sb("alibi", [P, GROUPS, GH, S]))
            dilated_attention(k, dil, OA)
        merge_branches(k, OG, OA)
        residual_stage(k, "s_out", k.H, None)
    if stop == 7:
        return stop_here(k)
    norm_stage(k, "s_n2", k.X, S, KD, D, 1e-6, c("norm2_g_2"), center=False, out=k.H)
    k.renew_semaphores()
    mixture(k, out, stop)


def to_rows(x):
    return x.rearrange("p h t -> p (h t)")


def linear_attention(k, OG):
    nc, a = k.nc, k.a
    w = a["w_in_2"][0]
    with ExitStack() as st:
        sb = lambda n, shape: st.enter_context(nc.sbuf_tensor(n, shape, F32))
        Q, K, R, V = sb("gq", [P, GH, S]), sb("gk", [P, GH, S]), sb("gr", [P, GH, S]), sb("gv", [P, ST, S])
        Z, KE, KET = sb("gz", [P, GH, S]), sb("gke", [P, GH, S]), sb("gket", [P, ST, S])
        E = sb("ge", [P, GH, S])
        LR, WA, reset = sb("glr", [P, S]), sb("gwa", [P, S]), sb("reset", [P, S])
        causal, chunk = sb("causal", [P, P]), sb("chunk_mask", [P, P // GC])
        jobs = []
        one = [(0, S)]
        for name, dst, first in (("q", Q, 0), ("k", K, 4)):
            for m in range(4):
                if m % 2 == 0:
                    wt = shared(k)
                jobs.append(Job(feature_product(k, k.H, one, wt, cols=(m % 2) * P),
                                act=lambda act, bank, s, m=m, dst=dst: act.activation(
                                    dst[:, m, :], bank[:, 0:S], ACT.Copy, scale=P ** -0.5 if dst is Q else 1.0)))
        halves = [shared(k, lambda w: wide(w, 512, 4)) for _ in range(2)]
        for t in range(ST):
            jobs.append(Job(token_product(k, k.H, t, halves), dve=lambda dve, bank, s, t=t: dve.tensor_copy(V[:, t, :], bank[:, 0:S])))
        for m in range(4):
            if m % 2 == 0:
                wt = shared(k)
            jobs.append(Job(feature_product(k, k.H, one, wt, cols=(m % 2) * P),
                            act=lambda act, bank, s, m=m: act.activation(R[:, m, :], bank[:, 0:S], ACT.Silu)))
        wl = shared(k, lambda w: wide(w, GC))
        jobs.append(Job(feature_product(k, k.H, one, wl, rows=GC),
                        act=lambda act, bank, s: act.activation(LR[0:GC, :], bank[0:GC, 0:S], ACT.Copy)))
        lowrank = len(jobs)
        b = norm_columns(k, "b_gla_a_2")
        for m in range(4):
            def decay(pe, bank, s, m=m):
                if m == 0:
                    pe.wait_ge(s.act, s.acts_before(lowrank))
                return pe.matmul(bank[:, 0:S], WA[0:GC, m * P:(m + 1) * P], LR[0:GC, :], start=True, stop=True)
            jobs.append(Job(decay, dve=lambda dve, bank, s, m=m: dve.tensor_scalar(Z[:, m, :], bank[:, 0:S], b(m), None, ALU.add)))
        product_stage(k, "g_in", jobs, used=[[2, 4, 6, 8], [12, 12], [14, 16, 17]],
                      loads=[(WA[0:GC, :], a["w_gla_a2_2"][0]), (reset[:], a["k_reset"]), (causal[:], a["k_causal"]), (chunk[:], a["k_chunk"])])
        s_a, s_d, s_p = k.sem("gd_act"), k.sem("gd_dve"), k.sem("gd_pool")
        fl = to_rows
        with nc.Block() as block:
            @block.scalar
            def _(act):
                act.activation(fl(E[:]), fl(Z[:]), ACT.Abs).then_inc(s_a, 1)
                act.wait_ge(s_a, 1)
                act.activation(fl(E[:]), fl(E[:]), ACT.Exp, scale=-1.0).then_inc(s_a, 1)
                act.wait_ge(s_a, 2)
                act.activation(fl(E[:]), fl(E[:]), ACT.Ln, bias=1.0).then_inc(s_a, 1)
                act.wait_ge(s_d, 6)
                act.activation(fl(KE[:]), fl(KE[:]), ACT.Exp, scale=1.0 / GLA_TAU).then_inc(s_a, 1)
                act.activation(fl(E[:]), fl(Z[:]), ACT.Exp, scale=-1.0 / GLA_TAU).then_inc(s_a, 1)
                act.wait_ge(s_a, 5)
                act.activation(fl(Z[:]), fl(Z[:]), ACT.Exp, scale=1.0 / GLA_TAU).then_inc(s_a, 1)

            @block.vector
            def _(dve):
                dve.wait_ge(s_a, 3)
                dve.scalar_tensor_tensor(fl(E[:]), fl(Z[:]), 0.0, fl(E[:]), ALU.min, ALU.subtract).then_inc(s_d, 1)
                dve.wait_ge(s_d, 1)
                for h in range(GH):
                    dve.tensor_tensor_scan(Z[:, h, :], reset[:], E[:, h, :], 0.0, ALU.mult, ALU.add).then_inc(s_d, 1)
                dve.wait_ge(s_d, 5)
                z = fl(Z[:]).rearrange("p (c i) -> p c i", i=GC)
                dve.tensor_tensor(fl(KE[:]).rearrange("p (c i) -> p c i", i=GC), z[:, :, GC - 1:GC].broadcast_to([P, GH * NCH, GC]), z,
                                  ALU.subtract).then_inc(s_d, 1)
                dve.wait_ge(s_a, 4)
                dve.tensor_tensor(fl(KE[:]), fl(KE[:]), fl(K[:]), ALU.mult).then_inc(s_d, 1)
                dve.wait_ge(s_a, 5)
                dve.wait_ge(s_d, 7)
                dve.tensor_tensor(fl(K[:]), fl(E[:]), fl(K[:]), ALU.mult).then_inc(s_d, 1)
                dve.wait_ge(s_a, 6)
                dve.tensor_tensor(fl(Q[:]), fl(Z[:]), fl(Q[:]), ALU.mult).then_inc(s_d, 1)
                dve.wait_ge(s_d, 9)
        jobs = []
        for t in range(ST):
            def turn(pe, bank, s, t=t):
                for h in range(GH):
                    ins = pe.transpose(bank[:, h * P:(h + 1) * P], KE[:, h, t * P:(t + 1) * P], k.ident[:])
                return ins
            jobs.append(Job(turn, act=lambda act, bank, s, t=t: act.activation(KET[:, t, :], bank[:, 0:S], ACT.Copy)))
        product_stage(k, "g_turn", jobs)
        gla_scan(k, Q, K, V, KET, Z, causal, chunk, OG)
        row_norm_stage(k, "g_norm", [(OG[:, h, :], norm_columns(k, "gla_out_norm_g_2")(0), None) for h in range(GH)], 1e-6)
        s_g = k.sem("gate_done")
        with nc.Block() as block:
            @block.vector
            def _(dve):
                dve.tensor_tensor(fl(OG[:]), fl(OG[:]), fl(R[:]), ALU.mult).then_inc(s_g, 1)
                dve.wait_ge(s_g, 1)


def gla_scan(k, Q, K, V, KET, DEC, causal, chunk, OG):
    nc = k.nc
    NC = P // GC
    N = ST * GH
    with ExitStack() as st:
        sb = lambda n, shape: st.enter_context(nc.sbuf_tensor(n, shape, F32))
        VX, AT, SS = sb("v_spread", [P, 2, NC, P]), sb("att", [P, 2, P]), sb("states", [P, GH, NC + 1, P])
        sem = lambda n: k.sem(f"gs_{n}")
        s_vx, s_att, s_kv, s_mask, s_st, s_scan, s_o, s_oc = (sem("v_spread"), sem("att"), sem("kv"), sem("masked"),
                                                              sem("state"), sem("scanned"), sem("out"), sem("copied"))
        block = st.enter_context(nc.Block())
        A = lambda n: k.PS[2][:, 512 * (n % 2):512 * (n % 2) + P]
        O = lambda n: k.PS[3][:, 512 * (n % 2):512 * (n % 2) + P]
        tok = lambda n: slice((n // GH) * P, (n // GH + 1) * P)

        @block.gpsimd
        def _(pool):
            for n in range(N):
                t, h = divmod(n, GH)
                if n >= 2:
                    pool.wait_ge(s_kv, n - 1)
                pool.tensor_tensor(VX[:, n % 2, :, :], V[:, t:t + 1, h * P:(h + 1) * P].broadcast_to([P, NC, P]),
                                   chunk[:].unsqueeze(2).broadcast_to([P, NC, P]), ALU.mult).then_inc(s_vx, 1)

        @block.tensor
        def _(pe):
            def first(n):
                t, h = divmod(n, GH)
                if n >= 2:
                    pe.wait_ge(s_mask, n - 1)
                pe.matmul(A(n), K[:, h, tok(n)], Q[:, h, tok(n)], start=True, stop=True).then_inc(s_att, 1)
                pe.wait_ge(s_vx, n + 1)
                if n >= 2:
                    pe.wait_ge(s_scan, n - 1)
                for c in range(2):
                    ins = pe.matmul(k.PS[n % 2][:, 512 * c:512 * c + 512], KET[:, t, h * P:(h + 1) * P],
                                    VX[:, n % 2, 4 * c:4 * c + 4, :].rearrange("p a b -> p (a b)"), start=True, stop=True)
                ins.then_inc(s_kv, 1)

            def second(n):
                t, h = divmod(n, GH)
                pe.wait_ge(s_mask, n + 1)
                pe.wait_ge(s_scan, n + 1)
                if n >= 2:
                    pe.wait_ge(s_oc, n - 1)
                pe.matmul(O(n), V[:, t, h * P:(h + 1) * P], AT[:, n % 2, :], start=True, stop=True)
                for c in range(NC):
                    at = t * P + c * GC
                    ins = pe.matmul(O(n)[:, c * GC:(c + 1) * GC], SS[:, h, c, :], Q[:, h, at:at + GC], start=False, stop=True,
                                    skip_group_check=True)
                ins.then_inc(s_o, 1)
            first(0)
            for n in range(N):
                if n + 1 < N:
                    first(n + 1)
                second(n)

        @block.vector
        def _(dve):
            c_st = [0]
            chained(dve, s_st, c_st, dve.memset(SS[:, :, 0, :], 0.0))
            for n in range(N):
                t, h = divmod(n, GH)
                dve.wait_ge(s_att, n + 1)
                if n >= 2:
                    dve.wait_ge(s_o, n - 1)
                dve.tensor_tensor(AT[:, n % 2, :], A(n), causal[:], ALU.mult).then_inc(s_mask, 1)
                if t:
                    dve.wait_ge(s_o, n - GH + 1)
                    chained(dve, s_st, c_st, dve.tensor_copy(SS[:, h, 0, :], SS[:, h, NC, :]))
                dve.wait_ge(s_kv, n + 1)
                for c in range(NC):
                    at = t * P + c * GC + GC - 1
                    ins = dve.scalar_tensor_tensor(SS[:, h, c + 1, :], SS[:, h, c, :], DEC[:, h, at:at + 1],
                                                   k.PS[n % 2][:, c * P:(c + 1) * P], ALU.mult, ALU.add)
                    if c < NC - 1:
                        chained(dve, s_st, c_st, ins)
                ins.then_inc(s_scan, 1)
                dve.wait_ge(s_scan, n + 1)

        @block.scalar
        def _(act):
            for n in range(N):
                act.wait_ge(s_o, n + 1)
                act.activation(OG[:, n % GH, tok(n)], O(n), ACT.Copy).then_inc(s_oc, 1)


def row_norm_stage(k, name, items, eps):
    nc = k.nc
    N = len(items)
    full = [n for n in range(N) if items[n][2] is None]
    with ExitStack() as st:
        sb = lambda n, shape: st.enter_context(nc.sbuf_tensor(f"{name}_{n}", shape, F32))
        sq, rs, bc = sb("sq", [P, 2, S]), sb("rs", [P, 4 * N]), sb("bc", [P, 2, ST, P])
        sem = lambda n: k.sem(f"{name}_{n}")
        s_sq, s_ss, s_rs, s_rt, s_bc, s_bk, s_out, s_gain = (sem("squared"), sem("sums"), sem("rs"), sem("root"),
                                                             sem("spread"), sem("bank"), sem("out"), sem("gain"))
        block = st.enter_context(nc.Block())

        @block.scalar
        def _(act):
            for n in range(N):
                if n >= 2:
                    act.wait_ge(s_ss, n - 1)
                act.activation(sq[:, n % 2, :], items[n][0], ACT.Square).then_inc(s_sq, 1)
            act.wait_ge(s_rs, 1)
            act.activation(rs[:], rs[:], ACT.Sqrt).then_inc(s_rt, 1)
            act.wait_ge(s_sq, N)
            for n in range(N):
                if items[n][2] is not None:
                    act.activation(items[n][0], items[n][0], ACT.Copy, scale=items[n][1])

        @block.tensor
        def _(pe):
            for n in range(N):
                pe.wait_ge(s_sq, n + 1)
                for t in range(ST):
                    ins = pe.matmul(k.PS[0][:, 4 * n + t:4 * n + t + 1], sq[:, n % 2, t * P:(t + 1) * P], k.ones[:, 0:1], start=True, stop=True)
                ins.then_inc(s_ss, 1)
            for j, n in enumerate(full):
                pe.wait_ge(s_bc, j + 1)
                if j >= 3:
                    pe.wait_ge(s_out, j - 2)
                for t in range(ST):
                    ins = pe.matmul(k.PS[1 + j % 3][:, t * P:(t + 1) * P], bc[:, j % 2, t, :], k.ident[:], start=True, stop=True)
                ins.then_inc(s_bk, 1)

        @block.vector
        def _(dve):
            dve.wait_ge(s_ss, N)
            dve.tensor_scalar(rs[:], k.PS[0][:, 0:4 * N], 1.0 / P, eps, ALU.mult, ALU.add).then_inc(s_rs, 1)
            dve.wait_ge(s_rt, 1)
            dve.reciprocal(rs[:], rs[:]).then_inc(s_rs, 1)
            dve.wait_ge(s_rs, 2)
            for n in range(N):
                if items[n][2] is not None:
                    dve.tensor_copy(items[n][2], rs[:, 4 * n:4 * n + 4])
            for j, n in enumerate(full + [None]):
                if n is not None:
                    if j >= 2:
                        dve.wait_ge(s_bk, j - 1)
                    for t in range(ST):
                        ins = dve.tensor_scalar(bc[:, j % 2, t, :], k.ones[:], rs[:, 4 * n + t:4 * n + t + 1], None, ALU.mult)
                    ins.then_inc(s_bc, 1)
                if j:
                    view, gain, _ = items[full[j - 1]]
                    dve.wait_ge(s_bk, j)
                    dve.scalar_tensor_tensor(view, view, gain, k.PS[1 + (j - 1) % 3][:, 0:S], ALU.mult, ALU.mult).then_inc(s_out, 1)
            dve.wait_ge(s_out, len(full))


def dilated_attention(k, dil, OA):
    nc, a = k.nc, k.a
    w = a["w_in_2"][0]
    with ExitStack() as st:
        sb = lambda n, shape: st.enter_context(nc.sbuf_tensor(n, shape, F32))
        sq, rms = sb("dil_squares", [P, 3, S]), sb("dil_rms", [P, 2, S])
        used, jobs, summed, scaled = [], [], [], []

        def project(i, g, m, dst, gain, wt):
            def split_off(act, bank, s):
                if i >= 3:
                    act.wait_ge(s.out, summed[i - 3] + 1)
                act.activation(sq[:, i % 3, :], bank[:, 0:S], ACT.Square)
                if dst is dil["q"]:
                    return act.activation(dst[:, g, m, :], bank[:, 0:S], ACT.Copy, scale=gain)
                return act.activation(dst[:, g, m, :], bank[:, 0:S], ACT.Copy)
            jobs.append(Job(feature_product(k, k.H, [(0, S)], wt, cols=(m % 2) * P), act=split_off))
            return len(jobs)

        def norm(i, g, m, dst, gain, projected):
            summed.append(len(jobs))
            if dst is dil["q"]:
                def pe_part(pe, bank, s):
                    pe.wait_ge(s.act, s.acts_before(projected - 1))
                    for t in range(ST):
                        at = 512 + (g * GH + m) * ST + t
                        ins = pe.matmul(k.PS[3][:, at:at + 1], sq[:, i % 3, t * P:(t + 1) * P], k.ones[:, 0:1], start=True, stop=True)
                    return ins
                jobs.append(Job(pe_part))
                return
            nth = len(scaled)
            scaled.append(len(jobs))

            def pe_part(pe, bank, s):
                pe.wait_ge(s.act, s.acts_before(projected - 1))
                return pe.matmul(bank[:, 0:S], k.ones[:], sq[:, i % 3, :], start=True, stop=True)

            def root(act, bank, s):
                if nth >= 2:
                    act.wait_ge(s.dve, s.dves_before(scaled[nth - 2]))
                s.link(act, act.activation(rms[:, nth % 2, :], bank[:, 0:S], ACT.Ln, scale=1.0 / P, bias=k.rms_eps[:]))
                return act.activation(rms[:, nth % 2, :], rms[:, nth % 2, :], ACT.Exp, scale=-0.5)

            def scale(dve, bank, s):
                return dve.scalar_tensor_tensor(dst[:, g, m, :], dst[:, g, m, :], gain, rms[:, nth % 2, :], ALU.mult, ALU.mult)
            jobs.append(Job(pe_part, act=root, dve=scale))
        i, pending = 0, None
        for g in range(GROUPS):
            at = []
            for dst, name in ((dil["q"], "dil_q_norm_g_2"), (dil["k"], "dil_k_norm_g_2")):
                for m in range(4):
                    if m % 2 == 0:
                        wt = shared(k)
                    gain = norm_columns(k, name)(g)
                    now = (i, g, m, dst, gain, project(i, g, m, dst, gain, wt))
                    at.append(len(jobs))
                    if pending:
                        norm(*pending)
                    pending = now
                    i += 1
            halves = [shared(k, lambda w: wide(w, 512, 4)) for _ in range(2)]
            for t in range(ST):
                jobs.append(Job(token_product(k, k.H, t, halves),
                                dve=lambda dve, bank, s, t=t, g=g: dve.tensor_copy(dil["v"][:, g, t, :], bank[:, 0:S])))
            used += [[at[1], at[3], at[5], at[7]], [len(jobs)] * 2]
        norm(*pending)
        product_stage(k, "d_in", jobs, used=used, pe_needs_loads=False, dve_last=lambda dve, s: dve.wait_ge(s.load, 16 * s.n_loads),
                      loads=[(dil["bias"][:, g, :, :], a["k_alibi"][g].rearrange("h p c -> p h c")) for g in range(GROUPS)])
    dilated_scores(k, dil, OA)


def dilated_scores(k, dil, OA):
    nc = k.nc
    N = GH * ST
    keys = [[list(range(max(0, t - 1), t + 1)), list(range(t + 1)), list(range(t + 1))] for t in range(ST)]
    tiles = [[(g, kt) for g in range(GROUPS) for kt in keys[t][g]] for t in range(ST)]
    lumps = [-(-len(x) // 4) for x in tiles]
    first_lump = [sum(lumps[m % ST] for m in range(n)) for n in range(N + 1)]
    with ExitStack() as st:
        sb = lambda n, shape: st.enter_context(nc.sbuf_tensor(n, shape, F32))
        SC, PT = sb("dil_scores", [P, 3, 10 * P]), sb("dil_turned", [P, 2, 10 * P])
        mx, neg, rs, ri, rqs = sb("dmx", [P, 3]), sb("dneg", [P, 3]), sb("drs", [P, 3]), sb("dri", [P, 3]), sb("drq", [P, GROUPS * GH * ST])
        sem = lambda n: k.sem(f"ds_{n}")
        s_root, s_rq, s_sc, s_bias, s_mx, s_nm, s_exp, s_ri, s_p, s_t, s_c, s_o, s_oc = (
            sem("root"), sem("rq"), sem("scores"), sem("biased"), sem("max"), sem("negmax"), sem("exp"), sem("rinv"), sem("probs"),
            sem("turned"), sem("copied"), sem("out"), sem("out_copied"))
        block = st.enter_context(nc.Block())
        B = lambda j: k.PS[j % 4 // 2][:, 512 * (j % 2):512 * (j % 2) + 512]
        T = lambda j: k.PS[2][:, 512 * (j % 2):512 * (j % 2) + 512]
        O = lambda n: k.PS[3][:, 512 * (n % 2):512 * (n % 2) + P]

        @block.tensor
        def _(pe):
            def scores(n):
                h, t = divmod(n, ST)
                for g in range(GROUPS):
                    j = GROUPS * n + g
                    if j >= 4:
                        pe.wait_ge(s_bias, j - 3)
                    k0, kn = keys[t][g][0], len(keys[t][g])
                    pe.matmul(B(j)[:, 0:kn * P], dil["q"][:, g, h, t * P:(t + 1) * P], dil["k"][:, g, h, k0 * P:(k0 + kn) * P],
                              start=True, stop=True).then_inc(s_sc, 1)

            def turn(n, c):
                if c == 0:
                    pe.wait_ge(s_p, n + 1)
                j = first_lump[n] + c
                if j >= 2:
                    pe.wait_ge(s_c, j - 1)
                part = tiles[n % ST][4 * c:4 * c + 4]
                for i in range(len(part)):
                    ins = pe.transpose(T(j)[:, i * P:(i + 1) * P], SC[:, n % 3, (4 * c + i) * P:(4 * c + i + 1) * P], k.ident[:])
                ins.then_inc(s_t, 1)

            def output(n, c):
                h, t = divmod(n, ST)
                if n >= 2 and c == 0:
                    pe.wait_ge(s_oc, n - 1)
                pe.wait_ge(s_c, first_lump[n] + c + 1)
                for i, (g, kt) in enumerate(tiles[t][4 * c:4 * c + 4]):
                    x = 4 * c + i
                    ins = pe.matmul(O(n), dil["v"][:, g, kt, h * P:(h + 1) * P], PT[:, n % 2, x * P:(x + 1) * P],
                                    start=x == 0, stop=x == len(tiles[t]) - 1)
                if c == lumps[t] - 1:
                    ins.then_inc(s_o, 1)
            scores(0)
            scores(1)
            for n in range(N + 1):
                if n + 2 < N:
                    scores(n + 2)
                turns = lumps[n % ST] if n < N else 0
                outputs = lumps[(n - 1) % ST] if n else 0
                for c in range(max(turns, outputs)):
                    if c < turns:
                        turn(n, c)
                    if c < outputs:
                        output(n - 1, c)

        @block.vector
        def _(dve):
            dve.wait_ge(s_root, 2)
            dve.tensor_scalar(rqs[:], rqs[:], P ** -0.5, None, ALU.mult).then_inc(s_rq, 1)
            dve.wait_ge(s_rq, 1)

            def score(n):
                h, t = divmod(n, ST)
                at = 0
                if n >= 3:
                    dve.wait_ge(s_t, first_lump[n - 2])
                for g in range(GROUPS):
                    w = len(keys[t][g]) * P
                    dve.wait_ge(s_sc, GROUPS * n + g + 1)
                    r = (g * GH + h) * ST + t
                    dve.scalar_tensor_tensor(SC[:, n % 3, at:at + w], B(GROUPS * n + g)[:, 0:w], rqs[:, r:r + 1],
                                             dil["bias"][:, g, h, S - w:S], ALU.mult, ALU.add).then_inc(s_bias, 1)
                    at += w
                dve.wait_ge(s_bias, GROUPS * (n + 1))
                dve.reduce_max(mx[:, n % 3:n % 3 + 1], SC[:, n % 3, 0:at], AXX).then_inc(s_mx, 1)
                dve.wait_ge(s_mx, n + 1)
                if n >= 3:
                    dve.wait_ge(s_exp, n - 2)
                dve.tensor_scalar(neg[:, n % 3:n % 3 + 1], mx[:, n % 3:n % 3 + 1], -1.0, None, ALU.mult).then_inc(s_nm, 1)

            def normalise(n):
                w = len(tiles[n % ST]) * P
                dve.wait_ge(s_exp, n + 1)
                dve.reciprocal(ri[:, n % 3:n % 3 + 1], rs[:, n % 3:n % 3 + 1]).then_inc(s_ri, 1)
                dve.wait_ge(s_ri, n + 1)
                dve.tensor_scalar(SC[:, n % 3, 0:w], SC[:, n % 3, 0:w], ri[:, n % 3:n % 3 + 1], None, ALU.mult).then_inc(s_p, 1)
            score(0)
            score(1)
            normalise(0)
            for n in range(N - 1):
                if n + 2 < N:
                    score(n + 2)
                normalise(n + 1)

        @block.scalar
        def _(act):
            def expo(n):
                w = len(tiles[n % ST]) * P
                act.wait_ge(s_nm, n + 1)
                if n >= 3:
                    act.wait_ge(s_ri, n - 2)
                act.activation(SC[:, n % 3, 0:w], SC[:, n % 3, 0:w], ACT.Exp, bias=neg[:, n % 3:n % 3 + 1],
                               accum_out=rs[:, n % 3:n % 3 + 1]).then_inc(s_exp, 1)

            def copies(n):
                h, t = divmod(n, ST)
                if n >= 2:
                    act.wait_ge(s_o, n - 1)
                for c in range(lumps[t]):
                    w = min(4, len(tiles[t]) - 4 * c) * P
                    act.wait_ge(s_t, first_lump[n] + c + 1)
                    act.activation(PT[:, n % 2, 4 * c * P:4 * c * P + w], T(first_lump[n] + c)[:, 0:w], ACT.Copy).then_inc(s_c, 1)
            def copy_out(n):
                h, t = divmod(n, ST)
                act.wait_ge(s_o, n + 1)
                act.activation(OA[:, h, t // 2, (t % 2) * P:(t % 2 + 1) * P], O(n), ACT.Copy).then_inc(s_oc, 1)
            act.activation(rqs[:], k.PS[3][:, 512:512 + GROUPS * GH * ST], ACT.Ln, scale=1.0 / P, bias=k.rms_eps[:]).then_inc(s_root, 1)
            act.wait_ge(s_root, 1)
            act.activation(rqs[:], rqs[:], ACT.Exp, scale=-0.5).then_inc(s_root, 1)
            expo(0)
            expo(1)
            for n in range(N):
                copies(n)
                if n + 2 < N:
                    expo(n + 2)
                if n:
                    copy_out(n - 1)
            copy_out(N - 1)


def merge_branches(k, OG, OA):
    nc = k.nc
    b = norm_columns(k, "b_branch_gate_2")
    with ExitStack() as st:
        sb = lambda n, shape: st.enter_context(nc.sbuf_tensor(n, shape, F32))
        G, t1 = sb("branch_gates", [P, 2, 2, S]), sb("branch_tmp", [P, 2, S])
        parts = Parts(k, st, "merge", (k.H, KD), (OG, GH), (OA, GH))
        jobs, gate_job = [], {}
        for c in range(4):
            pair = (2 * c, 2 * c + 1)
            for x in range(2):
                w = parts.chunk()
                for m in pair:
                    def gate(act, bank, s, m=m, x=x):
                        if m >= 2:
                            act.wait_ge(s.dve, 4 * (m // 2 - 1) + m % 2 + 2 * x + 1)
                        return act.activation(G[:, m % 2, x, :], bank[:, 0:S], ACT.Sigmoid, bias=b(KD * x + m))
                    gate_job[m, x] = len(jobs)
                    jobs.append(Job(parts.product(w, m % 2, first=m == 0 and x == 0), act=gate, chunk=w))
            for x in range(2):
                w = parts.chunk(GH)
                for m in pair:
                    def mix(dve, bank, s, m=m, x=x):
                        dve.wait_ge(s.act, s.acts_before(gate_job[m, x]))
                        if x == 0:
                            return dve.tensor_tensor(k.H[:, m, :], bank[:, 0:S], G[:, m % 2, 0, :], ALU.mult)
                        s.link(dve, dve.tensor_tensor(t1[:, m % 2, :], bank[:, 0:S], G[:, m % 2, 1, :], ALU.mult))
                        return dve.tensor_tensor(k.H[:, m, :], t1[:, m % 2, :], k.H[:, m, :], ALU.add)
                    jobs.append(Job(parts.product(w, m % 2, 1 + x, first=m == 0), dve=mix, chunk=w))
        product_stage(k, "merge", jobs, used=[0], parts=parts)


DUMMY = 2 * S


def mixture(k, out, stop):
    nc, a = k.nc, k.a
    k.rows_dram = nc.dram_tensor("normed_rows", (S, D), F32).ap()
    k.table = nc.dram_tensor("dispatch_table", (TABLE, 1), U32).ap()
    k.expert_out = nc.dram_tensor("expert_outputs", (DUMMY + TABLE, D), F32).ap()
    with ExitStack() as st:
        sb = lambda n, shape, dt=F32: st.enter_context(nc.sbuf_tensor(n, shape, dt))
        XR = sb("x_rows", [P, ST, D])
        gates = sb("gates", [P, 2, ST])
        pairs = sb("pairs", [P, 1], I32)
        ids, tokens = sb("slot_ids", [P, ST * EXPERTS + 2], U32), sb("slot_tokens", [P, ST * EXPERTS + 2], U32)
        route(k, XR, gates, pairs, ids, tokens)
        if stop == 8:
            return stop_here(k)
        experts(k, pairs, ids, tokens)
        combine(k, XR, gates, out)


def route(k, XR, gates, pairs, ids_by_turn, tokens_by_turn):
    nc, a = k.nc, k.a
    with ExitStack() as st:
        sb = lambda n, shape, dt=F32: st.enter_context(nc.sbuf_tensor(n, shape, dt))
        HR = sb("rt_h_rows", [P, ST, D])
        WR, BR = sb("rt_w_router", [P, KD, NG + EXPERTS]), sb("rt_b_router", [P, NG + EXPERTS])
        before, eid = sb("rt_before", [P, P]), sb("rt_expert_ids", [P, EXPERTS])
        GL, EL = sb("rt_group_logits", [P, ST, EG]), sb("rt_expert_logits", [P, ST, EXPERTS])
        top, topi, gi = sb("rt_top", [P, ST, 8]), sb("rt_topi", [P, ST, 8], U32), sb("rt_group", [P, ST, 8], U32)
        gtop, gif = sb("rt_gtop", [P, ST, 8]), sb("rt_gif", [P, ST])
        neg, eg, gs = sb("rt_neg", [P, ST]), sb("rt_eg", [P, ST, NG]), sb("rt_gs", [P, ST])
        gid, m1, ex, idf = sb("rt_gid", [P, EXPERTS]), sb("rt_m1", [P, ST, EXPERTS]), sb("rt_ex", [P, ST]), sb("rt_idf", [P, 2, ST])
        hot, both, rank, sel = sb("rt_hot", [P, 2, ST, EXPERTS]), sb("rt_both", [P, ST, EXPERTS]), sb("rt_rank", [P, ST, EXPERTS]), sb("rt_sel", [P, 2, ST, EXPERTS])
        loc, locu = sb("rt_loc", [P, 2, ST]), sb("rt_locu", [P, 2, ST], U32)
        cmax, pf = sb("rt_cmax", [P, 1]), sb("rt_pf", [P, 4])
        init, ids = sb("rt_table_init", [P, TABLE // P], U32), sb("rt_ids", [P, 2, ST], U32)
        sem = lambda n: k.sem(f"rt_{n}")
        s_ld, s_t, s_ca, s_cd, s_lg, s_ch, s_act, s_rk, s_rows, s_iota, s_tab, s_gn = (
            sem("load"), sem("turned"), sem("copied_act"), sem("copied_dve"), sem("logits"), sem("chain"), sem("act"),
            sem("ranks"), sem("rows"), sem("iota"), sem("table"), sem("gates"))
        block = st.enter_context(nc.Block())

        @block.sync
        def _(sp):
            sp.dma_start(WR[:, :, 0:NG], rows_of(a["w_router_group_2"][0])).then_inc(s_ld, 16)
            sp.dma_start(WR[:, :, NG:], rows_of(a["w_router_expert_2"][0])).then_inc(s_ld, 16)
            sp.dma_start(BR[:, 0:NG], a["b_router_group_2"].partition_broadcast(P)).then_inc(s_ld, 16)
            sp.dma_start(BR[:, NG:], a["b_router_expert_2"].partition_broadcast(P)).then_inc(s_ld, 16)
            sp.dma_start(before[:], a["k_before"]).then_inc(s_ld, 16)
            sp.dma_start(eid[:], a["k_expert"]).then_inc(s_ld, 16)
            sp.dma_start(gid[:], a["k_group"]).then_inc(s_ld, 16)
            sp.wait_ge(s_ca, 2 * ST)
            sp.dma_start(k.rows_dram.rearrange("(t p) d -> p t d", p=P), HR[:]).then_inc(s_rows, 16)
            sp.wait_ge(s_rows, 16)

        @block.tensor
        def _(pe):
            pe.wait_ge(s_ld, 16 * 7)
            for t in range(ST):
                for kk in range(KD):
                    ins = pe.matmul(k.PS[3][:, 64 * t:64 * t + NG + EXPERTS], k.H[:, kk, t * P:(t + 1) * P], WR[:, kk, :], start=kk == 0, stop=kk == KD - 1)
            ins.then_inc(s_lg, 1)
            def rows_of_tokens(bank, x, s_c):
                for j in range(2 * ST):
                    t, half = divmod(j, 2)
                    if j >= 2:
                        pe.wait_ge(s_c, j - 1)
                    for c in range(4):
                        ins = pe.transpose(bank[:, 512 * half + c * P:512 * half + (c + 1) * P], x[:, 4 * half + c, t * P:(t + 1) * P], k.ident[:])
                    ins.then_inc(s_t, 1)
            rows_of_tokens(k.PS[0], k.H, s_ca)
            pe.wait_ge(s_rk, 1)
            for t in range(ST):
                for u in range(t):
                    pe.matmul(k.PS[2][:, 32 * t:32 * t + 32], k.ones[:], both[:, u, :], start=u == 0, stop=False)
                pe.matmul(k.PS[2][:, 32 * t:32 * t + 32], before[:], both[:, t, :], start=t == 0, stop=True)
            for t in range(ST):
                ins = pe.matmul(k.PS[2][:, 512:544], k.ones[:], both[:, t, :], start=t == 0, stop=t == ST - 1)
            ins.then_inc(s_rk, 1)
            rows_of_tokens(k.PS[1], k.X, s_cd)

        @block.scalar
        def _(act):
            for t in range(ST):
                for half in range(2):
                    act.wait_ge(s_t, 2 * t + half + 1)
                    act.activation(HR[:, t, 512 * half:512 * half + 512], k.PS[0][:, 512 * half:512 * half + 512], ACT.Copy).then_inc(s_ca, 1)
            act.wait_ge(s_gn, 1)
            for t in range(ST):
                ins = act.activation(eg[:, t, :], GL[:, t, 0:NG], ACT.Exp, bias=neg[:, t:t + 1], accum_out=gs[:, t:t + 1])
            ins.then_inc(s_act, 1)
            act.wait_ge(s_gn, 2)
            act.activation(ex[:], ex[:], ACT.Exp).then_inc(s_act, 1)

        @block.vector
        def _(dve):
            n = [0]
            link = lambda ins: chained(dve, s_ch, n, ins)
            dve.memset(GL[:], -1e30).then_inc(s_ch, 1)
            n[0] += 1
            dve.wait_ge(s_ld, 16 * 7)
            dve.wait_ge(s_lg, 1)
            dve.wait_ge(s_ch, 1)
            lg = k.PS[3][:, 0:64 * ST].rearrange("p (t e) -> p t e", e=64)
            bc = lambda x, w: x.unsqueeze(1).broadcast_to([P, ST, w])
            link(dve.tensor_tensor(GL[:, :, 0:NG], lg[:, :, 0:NG], bc(BR[:, 0:NG], NG), ALU.add))
            link(dve.tensor_tensor(EL[:], lg[:, :, NG:NG + EXPERTS], bc(BR[:, NG:], EXPERTS), ALU.add))
            for t in range(ST):
                ins = dve.max(gtop[:, t, :], GL[:, t, :])
            link(ins)
            for t in range(ST):
                ins = dve.max_index(gi[:, t, :], gtop[:, t, :], GL[:, t, :])
            link(ins)
            dve.tensor_scalar(neg[:], gtop[:, :, 0], -1.0, None, ALU.mult).then_inc(s_gn, 1)
            link(dve.tensor_copy(gif[:], gi[:, :, 0]))
            for t in range(ST):
                ins = dve.tensor_scalar(m1[:, t, :], gid[:], gif[:, t:t + 1], None, ALU.is_equal)
            link(ins)
            link(dve.tensor_tensor(EL[:], EL[:], m1[:], ALU.mult))
            link(dve.tensor_scalar(m1[:], m1[:], 1.0, 1e30, ALU.subtract, ALU.mult))
            link(dve.tensor_tensor(EL[:], EL[:], m1[:], ALU.add))
            for t in range(ST):
                ins = dve.max(top[:, t, :], EL[:, t, :])
            link(ins)
            for t in range(ST):
                ins = dve.max_index(topi[:, t, :], top[:, t, :], EL[:, t, :])
            link(ins)
            dve.tensor_tensor(ex[:], top[:, :, 1], top[:, :, 0], ALU.subtract).then_inc(s_gn, 1)
            link(dve.tensor_copy(idf[:], topi[:, :, 0:2].rearrange("p t c -> p c t")))
            for c in range(2):
                for t in range(ST):
                    ins = dve.tensor_scalar(hot[:, c, t, :], eid[:], idf[:, c, t:t + 1], None, ALU.is_equal)
            link(ins)
            dve.tensor_tensor(both[:], hot[:, 0, :, :], hot[:, 1, :, :], ALU.add).then_inc(s_rk, 1)
            dve.wait_ge(s_act, 1)
            link(dve.reciprocal(gs[:], gs[:]))
            dve.wait_ge(s_act, 2)
            link(dve.tensor_scalar(gates[:, 0, :], ex[:], 1.0, None, ALU.add))
            link(dve.reciprocal(gates[:, 0, :], gates[:, 0, :]))
            link(dve.tensor_tensor(gates[:, 0, :], gates[:, 0, :], gs[:], ALU.mult))
            link(dve.tensor_tensor(gates[:, 1, :], gates[:, 0, :], ex[:], ALU.mult))
            dve.wait_ge(s_rk, 2)
            link(dve.tensor_copy(rank[:], k.PS[2][:, 0:32 * ST].rearrange("p (t e) -> p t e", e=32)))
            for c in range(2):
                ins = dve.tensor_tensor(sel[:, c, :, :], hot[:, c, :, :], rank[:], ALU.mult)
            link(ins)
            link(dve.tensor_reduce(loc[:], sel[:], AXX, ALU.add))
            link(dve.tensor_scalar(loc[:], loc[:], float(EXPERTS), None, ALU.mult))
            link(dve.tensor_tensor(loc[:], loc[:], idf[:], ALU.add))
            dve.tensor_copy(locu[:], loc[:]).then_inc(s_gn, 1)
            link(dve.reduce_max(cmax[:], k.PS[2][:, 512:544], AXX))
            for i in range(1, ST):
                ins = dve.tensor_scalar(pf[:, i:i + 1], cmax[:], float(P * i), None, ALU.is_gt)
            link(ins)
            link(dve.memset(pf[:, 0:1], 1.0))
            link(dve.tensor_reduce(cmax[:], pf[:], AXX, ALU.add))
            link(dve.tensor_scalar(cmax[:], cmax[:], float(EXPERTS // 2), None, ALU.mult))
            link(dve.tensor_copy(pairs[:], cmax[:]))
            link(dve.memset(ids_by_turn[:, ST * EXPERTS:], 0))
            for t in range(ST):
                for half in range(2):
                    dve.wait_ge(s_t, 2 * ST + 2 * t + half + 1)
                    dve.tensor_copy(XR[:, t, 512 * half:512 * half + 512], k.PS[1][:, 512 * half:512 * half + 512]).then_inc(s_cd, 1)
            dve.wait_ge(s_cd, 2 * ST)
            dve.wait_ge(s_tab, 16 * (2 + 2 * ST))
            link(dve.tensor_scalar(tokens_by_turn[:], ids_by_turn[:], S - 1, None, ALU.bitwise_and))

        @block.gpsimd
        def _(pool):
            pool.iota(init[:], pattern=[[1, TABLE // P]], base=DUMMY, channel_multiplier=TABLE // P).then_inc(s_iota, 1)
            pool.iota(ids[:], pattern=[[S, 2], [P, ST]], base=0, channel_multiplier=1).then_inc(s_iota, 1)
            pool.wait_ge(s_iota, 2)
            pool.dma_start(k.table.rearrange("(p j) o -> p (j o)", p=P), init[:]).then_inc(s_tab, 16)
            pool.wait_ge(s_tab, 16)
            pool.wait_ge(s_gn, 3)
            for c in range(2):
                for t in range(ST):
                    pool.indirect_dma_start(out=k.table, out_offset=bass.IndirectOffsetOnAxis(ap=locu[:, c, t:t + 1], axis=0),
                                            in_=ids[:, c, t:t + 1], in_offset=None).then_inc(s_tab, 16)
            pool.wait_ge(s_tab, 16 * (1 + 2 * ST))
            pool.dma_start(ids_by_turn[:, 0:ST * EXPERTS].rearrange("p (b e) -> p b e", b=ST),
                           k.table.rearrange("(b p e) o -> p b (e o)", b=ST, p=P)).then_inc(s_tab, 16)
            pool.wait_ge(s_tab, 16 * (2 + 2 * ST))


def experts(k, pairs, ids, tokens):
    nc, a = k.nc, k.a
    LOADS = 6
    ring, landed = k.weights.ring, k.weights.landed
    base = [16 * len(range(s, k.weights.total, SLOTS)) for s in range(SLOTS)]
    off = k.weights.total % SLOTS
    with ExitStack() as st:
        sb = lambda n, shape, dt=F32: st.enter_context(nc.sbuf_tensor(n, shape, dt))
        id_now = [sb(f"ids_now{i}", [P, 1], U32) for i in range(2)]
        token_now = [sb(f"tokens_now{i}", [P, 1], U32) for i in range(2)]
        XG, XT = sb("x_slots", [P, 2, D]), sb("x_turned", [P, 2, KD, P])
        SL, HE, YS = sb("ex_silu", [P, 2, DE]), sb("ex_hidden", [P, 2, DE]), sb("y_slots", [P, 2, D])
        sem = lambda n: k.sem(f"ex_{n}")
        s_ic, s_t, s_xa, s_xd, s_used, s_silu, s_he, s_ya, s_yd = (
            sem("ids_now"), sem("turned"), sem("xt_act"), sem("xt_dve"), sem("weights_used"), sem("silu"),
            sem("hidden"), sem("y_act"), sem("y_dve"))
        s_xg, s_ys = [sem(f"gathered{i}") for i in range(2)], [sem(f"scattered{i}") for i in range(2)]
        s_go = sem("go")
        s_free = [sem(f"rows_free{i}") for i in range(2)]
        block = st.enter_context(nc.Block())
        G, U = k.PS[1][:, 0:512], k.PS[1][:, 512:1024]
        steps = lambda eng: eng.value_load(pairs[0:1, 0:1], min_val=EXPERTS // 2, max_val=ST * EXPERTS // 2)

        @block.sync
        def _(sp):
            with sp.Fori(0, steps(sp)) as m:
                for c in range(2 * LOADS):
                    u, part = divmod(c, LOADS)
                    slot = (off + c) % SLOTS
                    sp.wait_ge(s_used, m * (2 * LOADS) + (c + 1))
                    e = (m % (EXPERTS // 2)) * 2 + u
                    if part < 4:
                        src = a["w_gate_2" if part < 2 else "w_up_2"][0]
                        view = wide(ring[:, slot, :])
                        src = src.rearrange("e (k p) n -> p e k n", p=P)[:, bass.ds(e, 1), :, 256 * (part % 2):256 * (part % 2) + 256]
                    else:
                        view = wide(ring[:, slot, :], 512, 4)
                        src = a["w_down_2"][0].rearrange("e (k p) n -> p e k n", p=P)[:, bass.ds(e, 1), :, 512 * (part % 2):512 * (part % 2) + 512]
                    sp.dma_start(view, src.rearrange("p e k n -> p (e k) n")).then_inc(landed[slot], 16)

        @block.gpsimd
        def _(pool):
            def gather(u, m):
                at = m * 2 + u
                col = slice(at, at + 1) if isinstance(at, int) else bass.ds(at, 1)
                if not isinstance(m, int) or m:
                    pool.wait_ge(s_ys[u], m * 16)
                pool.sem_inc(s_free[u], 1)
                pool.tensor_copy(id_now[u][:], ids[:, col]).then_inc(s_ic, 1)
                pool.tensor_copy(token_now[u][:], tokens[:, col]).then_inc(s_ic, 1)
                pool.wait_ge(s_t, m * 2 + (u + 1))
                pool.wait_ge(s_ic, m * 4 + (2 * u + 2))
                pool.sem_inc(s_go, 1)
                pool.indirect_dma_start(out=XG[:, u, :], out_offset=None, in_=k.rows_dram,
                                        in_offset=bass.IndirectOffsetOnAxis(ap=token_now[u][:, 0:1], axis=0)).then_inc(s_xg[u], 16)

            def scatter(u, m):
                pool.wait_ge(s_ya, m * 2 + (u + 3))
                pool.wait_ge(s_yd, m * 2 + (u + 3))
                pool.sem_inc(s_go, 1)
                pool.indirect_dma_start(out=k.expert_out, out_offset=bass.IndirectOffsetOnAxis(ap=id_now[u][:, 0:1], axis=0),
                                        in_=YS[:, u, :], in_offset=None).then_inc(s_ys[u], 16)
            gather(0, 0)
            gather(1, 0)
            scatter(0, 0)
            gather(0, 1)
            scatter(1, 0)
            n = steps(pool)
            with pool.Fori(1, n) as m:
                gather(1, m)
                scatter(0, m)
                gather(0, m + 1)
                scatter(1, m)
            pool.wait_ge(s_xg[0], n * 16 + 16)
            for u in range(2):
                pool.wait_ge(s_ys[u], n * 16)

        @block.tensor
        def _(pe):
            pe.sem_inc(s_used, SLOTS)
            pe.sem_inc(s_t, 2)

            def weights(u, part, m):
                c = LOADS * u + part
                slot = (off + c) % SLOTS
                uses = len([x for x in range(c + 1) if (off + x) % SLOTS == slot])
                pe.wait_ge(landed[slot], m * (16 * 2 * LOADS // SLOTS) + (base[slot] + 16 * uses))
                return ring[:, slot, :]

            def turn(u, m):
                pe.wait_ge(s_xg[u], m * 16 + 16)
                pe.wait_ge(s_xa, m * 2 + (u + 1))
                pe.wait_ge(s_xd, m * 2 + (u + 1))
                for kk in range(KD):
                    ins = pe.transpose(k.PS[0][:, kk * P:(kk + 1) * P], XG[:, u, kk * P:(kk + 1) * P], k.ident[:])
                ins.then_inc(s_t, 1)

            def up(u, m):
                pe.wait_ge(s_xa, m * 2 + (u + 2))
                pe.wait_ge(s_xd, m * 2 + (u + 2))
                for bank, first in ((G, 0), (U, 2)):
                    pe.wait_ge(s_silu if first == 0 else s_he, m * 2 + (u + (1 if first == 0 else 2)))
                    for half in range(2):
                        w = wide(weights(u, first + half, m))
                        for f in range(2):
                            for kk in range(KD):
                                at = (2 * half + f) * P
                                ins = pe.matmul(bank[:, at:at + P], w[:, kk, f * P:(f + 1) * P], XT[:, u, kk, :], start=kk == 0, stop=kk == KD - 1)
                        ins.then_inc(s_used, 1)

            def down(u, m):
                pe.wait_ge(s_he, m * 2 + (u + 3))
                pe.wait_ge(s_ya, m * 2 + (u + 1))
                pe.wait_ge(s_yd, m * 2 + (u + 1))
                for half in range(2):
                    w = wide(weights(u, 4 + half, m), 512, 4)
                    for f in range(4):
                        ins = pe.matmul(k.PS[2 + u][:, 512 * half:512 * half + 512], HE[:, u, f * P:(f + 1) * P], w[:, f, :],
                                        start=f == 0, stop=f == 3)
                    ins.then_inc(s_used, 1)

            turn(0, 0)
            with pe.Fori(0, steps(pe)) as m:
                up(0, m)
                turn(1, m)
                down(0, m)
                up(1, m)
                turn(0, m + 1)
                down(1, m)

        def copy_turned(eng, copy, half, done, u, m):
            eng.wait_ge(s_t, m * 2 + (u + 3))
            eng.wait_ge(s_he, m * 2 + (u + 1))
            copy(XT[:, u, 4 * half:4 * half + 4, :], k.PS[0][:, 512 * half:512 * half + 512].rearrange("p (a b) -> p a b", a=4)).then_inc(done, 1)

        def copy_out(eng, copy, half, done, u, m):
            eng.wait_ge(s_used, m * (2 * LOADS) + (LOADS * u + 5 + half + SLOTS))
            eng.wait_ge(s_free[u], m + 1)
            copy(YS[:, u, 512 * half:512 * half + 512], k.PS[2 + u][:, 512 * half:512 * half + 512]).then_inc(done, 1)

        @block.scalar
        def _(act):
            copy = lambda dst, src: act.activation(dst, src, ACT.Copy)
            act.sem_inc(s_xa, 1)
            act.sem_inc(s_silu, 1)
            act.sem_inc(s_ya, 2)

            def silu(u, m):
                act.wait_ge(s_used, m * (2 * LOADS) + (LOADS * u + 2 + SLOTS))
                act.wait_ge(s_he, m * 2 + (u + 1))
                act.activation(SL[:, u, :], G, ACT.Silu).then_inc(s_silu, 1)
            copy_turned(act, copy, 0, s_xa, 0, 0)
            with act.Fori(0, steps(act)) as m:
                silu(0, m)
                copy_turned(act, copy, 0, s_xa, 1, m)
                copy_out(act, copy, 0, s_ya, 0, m)
                silu(1, m)
                copy_turned(act, copy, 0, s_xa, 0, m + 1)
                copy_out(act, copy, 0, s_ya, 1, m)

        @block.vector
        def _(dve):
            copy = lambda dst, src: dve.tensor_copy(dst, src)
            dve.sem_inc(s_xd, 1)
            dve.sem_inc(s_he, 2)
            dve.sem_inc(s_yd, 2)

            def hidden(u, m):
                dve.wait_ge(s_silu, m * 2 + (u + 2))
                dve.wait_ge(s_used, m * (2 * LOADS) + (LOADS * u + 4 + SLOTS))
                dve.tensor_tensor(HE[:, u, :], SL[:, u, :], U, ALU.mult).then_inc(s_he, 1)
            copy_turned(dve, copy, 1, s_xd, 0, 0)
            with dve.Fori(0, steps(dve)) as m:
                hidden(0, m)
                copy_turned(dve, copy, 1, s_xd, 1, m)
                copy_out(dve, copy, 1, s_yd, 0, m)
                hidden(1, m)
                copy_turned(dve, copy, 1, s_xd, 0, m + 1)
                copy_out(dve, copy, 1, s_yd, 1, m)


def combine(k, XR, gates, out):
    nc = k.nc
    with ExitStack() as st:
        Y = st.enter_context(nc.sbuf_tensor("chosen_out", [P, 2, ST, D], F32))
        s_y = [k.sem(f"cb_loaded{t}") for t in range(ST)]
        s_1, s_2, s_out = k.sem("cb_first"), k.sem("cb_second"), k.sem("cb_out")
        block = st.enter_context(nc.Block())
        rows = out[0].rearrange("(t p) d -> p t d", p=P)
        chosen = k.expert_out[0:2 * S, :].rearrange("(c t p) d -> p c t d", c=2, p=P)

        @block.sync
        def _(sp):
            for t in range(ST):
                sp.dma_start(Y[:, :, t, :], chosen[:, :, t, :]).then_inc(s_y[t], 16)
            for t in range(ST):
                sp.wait_ge(s_2, t + 1)
                sp.dma_start(rows[:, t, :], XR[:, t, :]).then_inc(s_out, 16)
            sp.wait_ge(s_out, 16 * ST)

        @block.vector
        def _(dve):
            for t in range(ST):
                dve.wait_ge(s_y[t], 16)
                for c, done in ((0, s_1), (1, s_2)):
                    if c:
                        dve.wait_ge(s_1, t + 1)
                    dve.scalar_tensor_tensor(XR[:, t, :], Y[:, c, t, :], gates[:, c, t:t + 1], XR[:, t, :], ALU.mult, ALU.add).then_inc(done, 1)


def norm_columns(k, name, base=0):
    return lambda kk: k.col[:, COLUMN[name] + base + kk:COLUMN[name] + base + kk + 1]


def stop_here(k):
    with k.nc.Block() as block:
        @block.sync
        def _(sp):
            for s in range(SLOTS):
                sp.wait_ge(k.weights.landed[s], 16 * ((k.weights.issued - s + SLOTS - 1) // SLOTS))


def build(nc, a, out, stop=None):
    k = Core()
    k.nc, k.a, k.stage_sems = nc, a, []
    flat = lambda ap, pat: ap.rearrange(pat, p=P)
    k.flat = {
        "c": flat(a["c"], "o (k p) -> (o k) p"), "c_ctx": flat(a["c_ctx"], "(k p) -> k p"),
        "b_mod": flat(a["b_mod"], "l (k p) -> (l k) p"),
        "ln_g": flat(a["ln_g"], "l s (k p) -> (l s k) p"), "ln_b": flat(a["ln_b"], "l s (k p) -> (l s k) p"),
        "o_w_dw": flat(a["o_w_dw"], "o w (k p) -> (o w k) p"),
        "dil_q_norm_g_2": a["dil_q_norm_g_2"][0], "dil_k_norm_g_2": a["dil_k_norm_g_2"][0],
    }
    for name, _ in VECTORS:
        if name not in k.flat:
            k.flat[name] = flat(a[name], "o (k p) -> (o k) p")
    with ExitStack() as st:
        sb = lambda n, shape, dt=F32: st.enter_context(nc.sbuf_tensor(n, shape, dt))
        k.ident, k.ones = sb("ident", [P, P]), sb("ones", [P, P])
        k.rms_eps = sb("rms_eps", [P, 1])
        k.col = sb("col", [P, COL_TILES * P])
        k.mod = [sb(f"mod{l}", [P, 2, 72]) for l in range(2)]
        k.b_mod = lambda l: k.col[:, COLUMN["b_mod"] + 72 * l:COLUMN["b_mod"] + 72 * l + 72]
        k.cond = sb("cond", [P, 2, KD])
        k.cond2 = sb("conv_bias", [P, KD])
        k.X = sb("X", [P, KD, T0])
        ring = sb("weight_ring", [P, SLOTS, SLOT])
        k.PS = [st.enter_context(nc.psum_tensor(f"banks{i}", [P, 1024], F32)) for i in range(4)]
        landed = [st.enter_context(nc.semaphore(f"weights_landed{i}")) for i in range(SLOTS)]
        k.weights = WeightRing(ring, landed)
        plan_weights(k)
        LAT = [(0, 0, S)]
        BOTH = [(0, 0, S), (1, S, C)]
        ln = lambda l, s: (norm_columns(k, "ln_g", 24 * l + 8 * s), norm_columns(k, "ln_b", 24 * l + 8 * s))

        load_stage(k)
        first_modulation(k)
        ffn_stage(k, "f00", 0, 0, 0, BOTH, MOD_IN_F00)
        with ExitStack() as first:
            k.H = first.enter_context(nc.sbuf_tensor("H", [P, KD, T0], F32))
            norm_stage(k, "n00", k.X, T0, KD, D, LN_EPS, *ln(0, 0), then=(0, 1, BOTH))
            if stop == 1:
                return stop_here(k)
            even_mixer(k)
            if stop == 4:
                return stop_here(k)
        with ExitStack() as rest:
            k.H = rest.enter_context(nc.sbuf_tensor("H2", [P, KD, S], F32))
            norm_stage(k, "n01", k.X, S, KD, D, LN_EPS, *ln(0, 1))
            ffn_stage(k, "f01", 0, 1, 2, LAT, MOD_IN_F01)
            k.renew_semaphores()
            norm_stage(k, "n02", k.X, S, KD, D, LN_EPS, *ln(0, 2))
            if stop == 2:
                return stop_here(k)
            ffn_stage(k, "f10", 1, 0, 0, LAT)
            norm_stage(k, "n10", k.X, S, KD, D, LN_EPS, *ln(1, 0), then=(1, 1, LAT))
            conv_mixer(k)
            norm_stage(k, "n11", k.X, S, KD, D, LN_EPS, *ln(1, 1))
            ffn_stage(k, "f11", 1, 1, 2, LAT)
            norm_stage(k, "n12", k.X, S, KD, D, LN_EPS, *ln(1, 2))
            if stop == 3:
                return stop_here(k)
            k.renew_semaphores()
            second_block(k, out, stop)


def shape_constants():
    import numpy as np
    f = np.float32
    out = {"k_ident": np.eye(P, dtype=f)}
    p, q = np.arange(P)[:, None], np.arange(P)[None, :]
    out["k_causal"] = ((p // GC == q // GC) & (p <= q)).astype(f)
    out["k_before"] = (p < q).astype(f)
    out["k_chunk"] = (p // GC == np.arange(P // GC)[None, :]).astype(f)
    out["k_reset"] = np.broadcast_to((np.arange(S) % GC != 0).astype(f), (P, S)).copy()
    inv = (1.0 / (f(10000.0) ** (np.arange(0, ROPE // 2, 2, dtype=f) / f(ROPE // 2)))).astype(f)
    t = np.arange(S)
    ang = np.concatenate([(t // 64).astype(f)[:, None] * inv, (t % 64).astype(f)[:, None] * inv], axis=-1)
    rope = np.zeros((2, QK, S), f)
    rope[0, :NOPE] = 1.0
    rope[0, NOPE:] = np.repeat(np.cos(ang).T, 2, axis=0)
    rope[1, NOPE:] = np.repeat(np.sin(ang).T, 2, axis=0)
    out["k_rope"] = rope
    swap = np.zeros((QK, QK), f)
    for i in range(NOPE, QK, 2):
        swap[i + 1, i], swap[i, i + 1] = -1.0, 1.0
    out["k_swap"] = swap
    dist = (p + 384 - np.arange(S)[None, :])
    bias = np.zeros((GROUPS, GH, P, S), f)
    for g, (dil, span) in enumerate(((1, 128), (4, 128), (16, 128))):
        ok = (dist >= 0) & (dist % dil == 0) & (dist // dil <= span)
        for h in range(GH):
            slope = f(2.0 ** (-8.0 * (g * GH + h + 1) / (GROUPS * GH)))
            bias[g, h] = np.where(ok, -slope * dist.astype(f), f(-1e30))
    out["k_alibi"] = bias
    out["k_expert"] = np.broadcast_to(np.arange(EXPERTS, dtype=f), (P, EXPERTS)).copy()
    out["k_group"] = out["k_expert"] // EG
    return out


def kernel(**inputs):
    import numpy as np
    import concourse.bacc as bacc
    from concourse.bass_utils import run_bass_kernel_spmd

    nc = bacc.Bacc("TRN2", target_bir_lowering=False, num_devices=1)
    arrays = {n: np.ascontiguousarray(v) for n, v in inputs.items()}
    arrays.update(shape_constants())
    args = {n: nc.dram_tensor(n, v.shape, mybir.dt.from_np(v.dtype), kind="ExternalInput").ap()
            for n, v in arrays.items()}
    out = nc.dram_tensor("out", (1, S, D), F32, kind="ExternalOutput").ap()
    build(nc, args, out)
    r = run_bass_kernel_spmd(nc, [arrays], core_ids=[0])
    return r.results[0]["out"]
```
